# Optimizing a Trainium2 kernel written in Bass

```python
import math
import jax, jax.numpy as jnp
from jax import lax
import numpy as np

D_MODEL = 1024
BATCH = 1
SEQ = 256
DEPTH = 2

GRID_W = 64
CTX_LEN = 256

N_EVEN = (DEPTH + 1) // 2
N_ODD = DEPTH // 2
DN_ALPHA = (2 * DEPTH) ** 0.25
DN_BETA = (8 * DEPTH) ** -0.25
LN_EPS = 1e-6
D_FF = 2816

HY_W = D_MODEL // 2
HY_ORDER = 2
HY_IN = (HY_ORDER + 1) * HY_W
HY_EMB = 33
HY_FO = 64
HY_TARGET = 1e-2
HY_FAST = 0.3
HY_SLOW = 1.5

RW_W = D_MODEL - HY_W
RW_N = 64
RW_H = RW_W // RW_N
RW_DECAY_LORA = 64
RW_A_LORA = 64
RW_GATE_LORA = 128
RW_GN_EPS = 64e-5
RW_IN = 3 * RW_W + 2 * RW_DECAY_LORA + 2 * RW_A_LORA + RW_GATE_LORA
EV_IN = HY_IN + RW_IN

GLA_H = 4
GLA_DK = D_MODEL // 2
GLA_DV = D_MODEL
GLA_HK = GLA_DK // GLA_H
GLA_HV = GLA_DV // GLA_H
GLA_GATE_LORA = 16
GLA_NORMALIZER = 16.0
GLA_CHUNK = 64
GLA_EPS = 1e-5
OD_IN = 2 * GLA_DK + 2 * GLA_DV + 2 * GLA_GATE_LORA

kernel_name = "hyena_rwkv7_gla_prefix_trunk"

def split_sizes(z, sizes):
    idx = [sum(sizes[:i + 1]) for i in range(len(sizes) - 1)]
    return jnp.split(z, idx, axis=-1)

def layer_norm(h, g, b):
    hf = h.astype(jnp.float32)
    mu = jnp.mean(hf, -1, keepdims=True)
    var = jnp.mean(jnp.square(hf - mu), -1, keepdims=True)
    return ((hf - mu) * lax.rsqrt(var + LN_EPS)).astype(h.dtype) * g + b

def modulate(h, shift, scale):
    return h * (1 + scale) + shift

def post_norm_residual(h, y, gate, weight, g, b):
    return layer_norm(DN_ALPHA * h + weight * gate * y, g, b)

def swiglu(h, wg, wu, wd):
    return (jax.nn.silu(h @ wg) * (h @ wu)) @ wd

def neighbours(z):
    zp = jnp.pad(z, ((0, 0), (1, 1), (0, 0)))
    return zp[:, :-2], zp[:, 2:]

def conv3_centered(z, w, b):
    prev, nxt = neighbours(z)
    return prev * w[0] + z * w[1] + nxt * w[2] + b

def raster_to_columns(z):
    B, T = z.shape[:2]
    rows = T // GRID_W
    return z.reshape(B, rows, GRID_W, *z.shape[2:]).swapaxes(1, 2).reshape(z.shape)

def columns_to_raster(z):
    B, T = z.shape[:2]
    rows = T // GRID_W
    return z.reshape(B, GRID_W, rows, *z.shape[2:]).swapaxes(1, 2).reshape(z.shape)

def hyena_filters(L, w1, b1, f1, w2, b2, f2, w3):
    f32 = jnp.float32
    t = jnp.linspace(0.0, 1.0, L, dtype=f32)[:, None]
    bands = (HY_EMB - 1) // 2
    w = 2.0 * math.pi * jnp.arange(L, dtype=f32)[:, None] / L
    f = jnp.linspace(1e-4, bands - 1, bands, dtype=f32)[None, :]
    z = jnp.concatenate([t, jnp.cos(f * w), -jnp.sin(f * w)], axis=-1)
    h = jnp.sin(f1 * (z @ w1 + b1))
    h = jnp.sin(f2 * (h @ w2 + b2))
    h = (h @ w3).astype(f32).reshape(L, HY_ORDER, 2, HY_W)
    deltas = jnp.linspace(math.log(HY_TARGET) / HY_SLOW, math.log(HY_TARGET) / HY_FAST, HY_W, dtype=f32)
    window = jnp.exp(-t * jnp.abs(deltas))
    return h * window[:, None, None, :]

def bidir_long_conv(u, h_fwd, h_bwd, skip):
    L = u.shape[1]
    k = jnp.concatenate([h_fwd, jnp.zeros_like(h_fwd[:1]), h_bwd[:0:-1]], axis=0)
    uf = u.astype(jnp.float32)
    y = jnp.fft.irfft(jnp.fft.rfft(uf, n=2 * L, axis=1) * jnp.fft.rfft(k, n=2 * L, axis=0)[None],
                      n=2 * L, axis=1)[:, :L]
    return y + uf * skip

def hyena_segment(zh, conv_w, conv_b, filt, skip):
    zh = conv3_centered(zh, conv_w, conv_b)
    v, x1, x2 = jnp.split(zh, 3, axis=-1)
    y = x1.astype(jnp.float32) * bidir_long_conv(v, filt[:, 0, 0], filt[:, 0, 1], skip[0])
    y = x2.astype(jnp.float32) * bidir_long_conv(y, filt[:, 1, 0], filt[:, 1, 1], skip[1])
    return y.astype(zh.dtype)

def rwkv_prepare(zr, mu, w0, w_up, a0, a_up, g_up, k_k, k_a):
    f32 = jnp.float32
    B, T, _ = zr.shape
    prev, nxt = neighbours(zr)
    zr = zr + mu * (0.5 * (prev + nxt) - zr)
    r, k, v, wdf, wdb, adf, adb, gd = split_sizes(
        zr, [RW_W, RW_W, RW_W, RW_DECAY_LORA, RW_DECAY_LORA, RW_A_LORA, RW_A_LORA, RW_GATE_LORA])
    heads = lambda t: t.astype(f32).reshape(B, T, RW_H, RW_N)
    g = jax.nn.sigmoid(gd) @ g_up
    kk = heads(k * k_k)
    kk = kk / jnp.maximum(jnp.sqrt(jnp.sum(kk * kk, -1, keepdims=True)), 1e-12)
    dirs = []
    for d, (wd, ad) in enumerate(((wdf, adf), (wdb, adb))):
        w_log = -jax.nn.softplus(-(w0[d] + jnp.tanh(wd) @ w_up[d]).astype(f32)) - 0.5
        decay = jnp.exp(-jnp.exp(w_log))
        a = jax.nn.sigmoid((a0[d] + ad @ a_up[d]).astype(f32))
        kd = k.astype(f32) * (1 + (a - 1) * k_a)
        dirs.append((heads(decay), heads(kd), heads(a)))
    return heads(r), heads(v), kk, g, dirs

def rwkv7_scan(r, decay, k, v, kk, a, s0, reverse):
    def step(S, inp):
        r_t, w_t, k_t, v_t, kk_t, a_t = inp
        sa = jnp.einsum('bhvk,bhk->bhv', S, -kk_t)
        S = (S * w_t[:, :, None, :] + sa[..., None] * (kk_t * a_t)[:, :, None, :]
             + v_t[..., None] * k_t[:, :, None, :])
        return S, jnp.einsum('bhvk,bhk->bhv', S, r_t)
    xs = tuple(jnp.moveaxis(t, 1, 0) for t in (r, decay, k, v, kk, a))
    S, out = lax.scan(step, s0, xs, reverse=reverse)
    return jnp.moveaxis(out, 0, 1), S

def rwkv_bidir(prep, inits):
    r, v, kk, _, dirs = prep
    o_sum, k_sum, finals = 0.0, 0.0, []
    for d, ((decay, kd, a), s0) in enumerate(zip(dirs, inits)):
        o, S = rwkv7_scan(r, decay, kd, v, kk, a, s0, reverse=(d == 1))
        o_sum = o_sum + o
        k_sum = k_sum + kd
        finals.append(S)
    return o_sum, k_sum, tuple(finals)

def rwkv_readout(o, prep, k_sum, r_k, gn_g, gn_b):
    r, v, _, g, _ = prep
    B, T = o.shape[:2]
    mu = jnp.mean(o, -1, keepdims=True)
    var = jnp.mean(jnp.square(o - mu), -1, keepdims=True)
    y = ((o - mu) * lax.rsqrt(var + RW_GN_EPS)).reshape(B, T, RW_W) * gn_g + gn_b
    bonus = jnp.sum(r * k_sum * r_k, -1, keepdims=True) * v
    return (y + bonus.reshape(B, T, RW_W)) * g

def even_mixer(u_ctx, u_lat, w_in, w_out, conv_w, conv_b, f_w1, f_b1, f_freq1, f_w2, f_b2, f_freq2, f_w3,
               skip, mu, w0, w_up, a0, a_up, g_up, k_k, k_a, r_k, gn_g, gn_b, ctx_out):
    z_ctx, z_lat = u_ctx @ w_in, u_lat @ w_in

    def hyena(z):
        filt = hyena_filters(z.shape[1], f_w1, f_b1, f_freq1, f_w2, f_b2, f_freq2, f_w3)
        return hyena_segment(z[..., :HY_IN], conv_w, conv_b, filt, skip)

    p_ctx = rwkv_prepare(z_ctx[..., HY_IN:], mu, w0, w_up, a0, a_up, g_up, k_k, k_a)
    p_lat = rwkv_prepare(z_lat[..., HY_IN:], mu, w0, w_up, a0, a_up, g_up, k_k, k_a)
    s0 = jnp.zeros((z_ctx.shape[0], RW_H, RW_N, RW_N), jnp.float32)
    o_ctx, ks_ctx, fin_ctx = rwkv_bidir(p_ctx, (s0, s0))
    o_lat, ks_lat, _ = rwkv_bidir(p_lat, fin_ctx)
    y_lat = jnp.concatenate([hyena(z_lat).astype(u_lat.dtype),
                             rwkv_readout(o_lat, p_lat, ks_lat, r_k, gn_g, gn_b).astype(u_lat.dtype)], -1) @ w_out
    y_ctx = None
    if ctx_out:
        y_ctx = jnp.concatenate([hyena(z_ctx).astype(u_ctx.dtype),
                                 rwkv_readout(o_ctx, p_ctx, ks_ctx, r_k, gn_g, gn_b).astype(u_ctx.dtype)], -1) @ w_out
    return y_ctx, y_lat

def gla_prepare(z, g_up, g_b):
    f32 = jnp.float32
    B, T, _ = z.shape
    q, k, v, gdf, gdb, og = split_sizes(z, [GLA_DK, GLA_DK, GLA_DV, GLA_GATE_LORA, GLA_GATE_LORA, GLA_DV])
    logs = [(jax.nn.log_sigmoid((gd @ g_up[d] + g_b[d]).astype(f32)) / GLA_NORMALIZER).reshape(B, T, GLA_H, GLA_HK)
            for d, gd in enumerate((gdf, gdb))]
    q = q.astype(f32).reshape(B, T, GLA_H, GLA_HK) * GLA_HK ** -0.5
    k = k.astype(f32).reshape(B, T, GLA_H, GLA_HK)
    v = v.astype(f32).reshape(B, T, GLA_H, GLA_HV)
    return q, k, v, logs, og

def gla_chunked(q, k, v, g, s0):
    B, T, H, K = q.shape
    V = v.shape[-1]
    C = GLA_CHUNK
    n = T // C
    ch = lambda t: t.reshape(B, n, C, H, t.shape[-1]).transpose(0, 1, 3, 2, 4)
    q, k, v, g = ch(q), ch(k), ch(v), ch(g)
    b = jnp.cumsum(g, axis=3)
    b_ref = b[:, :, :, C // 2:C // 2 + 1]
    b_last = b[:, :, :, -1:]
    scores = jnp.einsum('bnhck,bnhsk->bnhcs', q * jnp.exp(b - b_ref), k * jnp.exp(b_ref - b))
    lower = jnp.tril(jnp.ones((C, C), bool))
    o_intra = jnp.einsum('bnhcs,bnhsv->bnhcv', jnp.where(lower, scores, 0.0), v)
    q_in = q * jnp.exp(b)
    k_out = k * jnp.exp(b_last - b)
    d_last = jnp.exp(b_last[:, :, :, 0])

    def step(S, inp):
        qc, kc, vc, dc = inp
        o = jnp.einsum('bhck,bhkv->bhcv', qc, S)
        S = S * dc[..., None] + jnp.einsum('bhck,bhcv->bhkv', kc, vc)
        return S, o
    S, o_inter = lax.scan(step, s0, tuple(jnp.moveaxis(t, 1, 0) for t in (q_in, k_out, v, d_last)))
    o = o_intra + jnp.moveaxis(o_inter, 0, 1)
    return o.transpose(0, 1, 3, 2, 4).reshape(B, T, H, V), S

def gla_bidir(q, k, v, logs, inits):
    flip = lambda t: jnp.flip(t, axis=1)
    o_f, S_f = gla_chunked(q, k, v, logs[0], inits[0])
    o_b, S_b = gla_chunked(flip(q), flip(k), flip(v), flip(logs[1]), inits[1])
    return o_f + flip(o_b), (S_f, S_b)

def gla_readout(o, og, norm_g):
    B, T = o.shape[:2]
    y = o * lax.rsqrt(jnp.mean(jnp.square(o), -1, keepdims=True) + GLA_EPS) * norm_g
    return y.reshape(B, T, GLA_DV) * jax.nn.silu(og.astype(jnp.float32))

def odd_mixer(u_ctx, u_lat, w_in, w_out, g_up, g_b, norm_g, ctx_out):
    qc, kc, vc, lc, ogc = gla_prepare(u_ctx @ w_in, g_up, g_b)
    ql, kl, vl, ll, ogl = gla_prepare(u_lat @ w_in, g_up, g_b)
    s0 = jnp.zeros((u_ctx.shape[0], GLA_H, GLA_HK, GLA_HV), jnp.float32)
    o_ctx, fin_ctx = gla_bidir(qc, kc, vc, lc, (s0, s0))
    o_lat, _ = gla_bidir(raster_to_columns(ql), raster_to_columns(kl), raster_to_columns(vl),
                         [raster_to_columns(t) for t in ll], fin_ctx)
    o_lat = columns_to_raster(o_lat)
    y_lat = gla_readout(o_lat, ogl, norm_g).astype(u_lat.dtype) @ w_out
    y_ctx = None
    if ctx_out:
        y_ctx = gla_readout(o_ctx, ogc, norm_g).astype(u_ctx.dtype) @ w_out
    return y_ctx, y_lat

def setup_inputs(seed: int = 0) -> dict:
    key = jax.random.key(seed)
    ks = iter(jax.random.split(key, 48))
    f32 = jnp.float32
    D, F, NE, NO = D_MODEL, D_FF, N_EVEN, N_ODD

    def nrm(shape, scale):
        return scale * jax.random.normal(next(ks), shape, f32)

    def near(shape, center, spread):
        return center + spread * jax.random.normal(next(ks), shape, f32)

    return {
        "x": nrm((BATCH, SEQ, D), 1.0),
        "c": nrm((BATCH, D), 1.0),
        "ctx": nrm((BATCH, CTX_LEN, D), 1.0),
        "c_ctx": nrm((D,), 1.0),
        "ada_w": nrm((DEPTH, D, 9 * D), 0.5 * D ** -0.5),
        "ada_b": nrm((DEPTH, 9 * D), 0.02),
        "ln_g": near((DEPTH, 3, D), 1.0, 0.02),
        "ln_b": nrm((DEPTH, 3, D), 0.02),
        "ffn_wg": nrm((DEPTH, 2, D, F), D ** -0.5),
        "ffn_wu": nrm((DEPTH, 2, D, F), D ** -0.5),
        "ffn_wd": nrm((DEPTH, 2, F, D), DN_BETA * F ** -0.5),
        "ev_w_in": nrm((NE, D, EV_IN), D ** -0.5),
        "ev_w_out": nrm((NE, D, D), DN_BETA * D ** -0.5),
        "hy_conv_w": nrm((NE, 3, HY_IN), 3 ** -0.5),
        "hy_conv_b": nrm((NE, HY_IN), 0.02),
        "hy_f_w1": nrm((NE, HY_EMB, HY_FO), HY_EMB ** -0.5),
        "hy_f_b1": nrm((NE, HY_FO), 0.1),
        "hy_f_freq1": near((NE, HY_FO), 1.0, 0.02),
        "hy_f_w2": nrm((NE, HY_FO, HY_FO), HY_FO ** -0.5),
        "hy_f_b2": nrm((NE, HY_FO), 0.1),
        "hy_f_freq2": near((NE, HY_FO), 1.0, 0.02),
        "hy_f_w3": nrm((NE, HY_FO, 2 * HY_ORDER * HY_W), 0.1 * HY_FO ** -0.5),
        "hy_skip": nrm((NE, HY_ORDER, HY_W), 0.5),
        "rw_mu": jax.random.uniform(next(ks), (NE, RW_IN), f32),
        "rw_w0": jax.random.uniform(next(ks), (NE, 2, RW_W), f32, -2.0, 1.0),
        "rw_w_up": nrm((NE, 2, RW_DECAY_LORA, RW_W), 0.5 * RW_DECAY_LORA ** -0.5),
        "rw_a0": nrm((NE, 2, RW_W), 0.5),
        "rw_a_up": nrm((NE, 2, RW_A_LORA, RW_W), 0.5 * RW_A_LORA ** -0.5),
        "rw_g_up": nrm((NE, RW_GATE_LORA, RW_W), RW_GATE_LORA ** -0.5),
        "rw_k_k": near((NE, RW_W), 0.85, 0.02),
        "rw_k_a": near((NE, RW_W), 1.0, 0.02),
        "rw_r_k": nrm((NE, RW_H, RW_N), 0.1),
        "rw_gn_g": near((NE, RW_W), 1.0, 0.02),
        "rw_gn_b": nrm((NE, RW_W), 0.02),
        "od_w_in": nrm((NO, D, OD_IN), D ** -0.5),
        "od_w_out": nrm((NO, GLA_DV, D), DN_BETA * GLA_DV ** -0.5),
        "gla_g_up": nrm((NO, 2, GLA_GATE_LORA, GLA_DK), GLA_GATE_LORA ** -0.5),
        "gla_g_b": nrm((NO, 2, GLA_DK), 0.5),
        "gla_norm_g": near((NO, GLA_HV), 1.0, 0.02),
    }

def reference(x, c, ctx, c_ctx, ada_w, ada_b, ln_g, ln_b, ffn_wg, ffn_wu, ffn_wd, ev_w_in, ev_w_out,
              hy_conv_w, hy_conv_b, hy_f_w1, hy_f_b1, hy_f_freq1, hy_f_w2, hy_f_b2, hy_f_freq2, hy_f_w3, hy_skip,
              rw_mu, rw_w0, rw_w_up, rw_a0, rw_a_up, rw_g_up, rw_k_k, rw_k_a, rw_r_k, rw_gn_g, rw_gn_b,
              od_w_in, od_w_out, gla_g_up, gla_g_b, gla_norm_g):
    h_lat, h_ctx = x, ctx
    s_lat = jax.nn.silu(c)[:, None, :]
    s_ctx = jax.nn.silu(c_ctx)[None, None, :]
    for l in range(DEPTH):
        last = l == DEPTH - 1
        m_lat = jnp.split(s_lat @ ada_w[l] + ada_b[l], 9, axis=-1)
        m_ctx = jnp.split(s_ctx @ ada_w[l] + ada_b[l], 9, axis=-1)

        h_lat = post_norm_residual(
            h_lat, swiglu(modulate(h_lat, m_lat[0], m_lat[1]), ffn_wg[l, 0], ffn_wu[l, 0], ffn_wd[l, 0]),
            m_lat[2], 0.5, ln_g[l, 0], ln_b[l, 0])
        h_ctx = post_norm_residual(
            h_ctx, swiglu(modulate(h_ctx, m_ctx[0], m_ctx[1]), ffn_wg[l, 0], ffn_wu[l, 0], ffn_wd[l, 0]),
            m_ctx[2], 0.5, ln_g[l, 0], ln_b[l, 0])

        u_lat = modulate(h_lat, m_lat[3], m_lat[4])
        u_ctx = modulate(h_ctx, m_ctx[3], m_ctx[4])
        if l % 2 == 0:
            e = l // 2
            y_ctx, y_lat = even_mixer(
                u_ctx, u_lat, ev_w_in[e], ev_w_out[e], hy_conv_w[e], hy_conv_b[e], hy_f_w1[e], hy_f_b1[e],
                hy_f_freq1[e], hy_f_w2[e], hy_f_b2[e], hy_f_freq2[e], hy_f_w3[e], hy_skip[e], rw_mu[e], rw_w0[e],
                rw_w_up[e], rw_a0[e], rw_a_up[e], rw_g_up[e], rw_k_k[e], rw_k_a[e], rw_r_k[e], rw_gn_g[e], rw_gn_b[e],
                ctx_out=not last)
        else:
            o = l // 2
            y_ctx, y_lat = odd_mixer(u_ctx, u_lat, od_w_in[o], od_w_out[o], gla_g_up[o], gla_g_b[o],
                                     gla_norm_g[o], ctx_out=not last)
        h_lat = post_norm_residual(h_lat, y_lat, m_lat[5], 1.0, ln_g[l, 1], ln_b[l, 1])

        h_lat = post_norm_residual(
            h_lat, swiglu(modulate(h_lat, m_lat[6], m_lat[7]), ffn_wg[l, 1], ffn_wu[l, 1], ffn_wd[l, 1]),
            m_lat[8], 0.5, ln_g[l, 2], ln_b[l, 2])
        if not last:
            h_ctx = post_norm_residual(h_ctx, y_ctx, m_ctx[5], 1.0, ln_g[l, 1], ln_b[l, 1])
            h_ctx = post_norm_residual(
                h_ctx, swiglu(modulate(h_ctx, m_ctx[6], m_ctx[7]), ffn_wg[l, 1], ffn_wu[l, 1], ffn_wd[l, 1]),
                m_ctx[8], 0.5, ln_g[l, 2], ln_b[l, 2])
    return h_lat


_drawn_inputs = setup_inputs


def setup_inputs(seed=0):
    import zlib

    import numpy as np

    out = dict(_drawn_inputs(seed))
    spreads = {}
    factors = {'ctx': 3.973,
     'c_ctx': 5.332,
     'ada_b': 5.362,
     'hy_conv_b': 36.884,
     'hy_f_b1': 6.895,
     'hy_f_freq1': 8.0,
     'hy_f_b2': 7.623,
     'hy_f_freq2': 49.105,
     'rw_w0': 3.888,
     'rw_w_up': 8.0,
     'rw_a0': 6.002,
     'rw_a_up': 7.528,
     'rw_k_k': 8.0,
     'rw_k_a': 8.0,
     'rw_r_k': 3.135,
     'rw_gn_g': 50.191,
     'rw_gn_b': 40.788,
     'gla_g_up': 4.473,
     'gla_g_b': 3.257,
     'gla_norm_g': 41.405}
    for name, (base, spread) in spreads.items():
        noise = np.random.default_rng([zlib.crc32(name.encode()), seed]).standard_normal(out[name].shape)
        drawn = base * np.exp(spread * noise) if base else spread * noise
        out[name] = __import__('jax').numpy.asarray(drawn.astype(out[name].dtype))
    for name, factor in factors.items():
        out[name] = (out[name] * factor).astype(out[name].dtype)
    return out
```

```python
import math
from contextlib import ExitStack

import numpy as np
import concourse.bass as bass
from concourse import mybir

F32 = mybir.dt.float32
U8 = mybir.dt.uint8
ALU = mybir.AluOpType
ACT = mybir.ActivationFunctionType

P = 128
D = 1024
KT = D // P
SEG = 256
NT = 2 * SEG
DEPTH = 2
F = 2816
FT = F // P
GRID_W = 64
ROWS = SEG // GRID_W
ALPHA = (2 * DEPTH) ** 0.25
LN_EPS = 1e-6
HW = 512
CT = HW // P
ZT = 27
HY_EMB, HY_FO = 33, 64
GN_EPS = 64e-5
GLA_EPS = 1e-5
GLA_N = 16.0
HK, HV = 128, 256
DECAY = math.exp(-0.5)

R = 4
SLOT = 4096
SUBS = 3 * DEPTH
LEVELS = 7

PAR = {}


def _columns():
    at = 0
    for name, n in (("ada_b0", 72), ("ln_g", 48)):
        PAR[name] = at
        at += n
    at = P
    for name, n in (("ada_b1", 72), ("ln_b", 48)):
        PAR[name] = at
        at += n
    at = 2 * P
    for name, n in (("conv_w", 36), ("conv_b", 12), ("mu", 15), ("w0", 8), ("a0", 8), ("k_k", 4), ("k_a", 4),
                    ("r_k", 4), ("gn_g", 4), ("gn_b", 4), ("gla_b", 8), ("norm_g", 2), ("c", 8), ("c_ctx", 8)):
        PAR[name] = at
        at += n


_columns()

M_UP, M_LO, M_STRICT, M_GLA = 0, LEVELS, 2 * LEVELS, 2 * LEVELS + 4


def constants():
    i = np.arange(P)
    row, col = i[:, None], i[None, :]
    masks = []
    for lv in range(LEVELS):
        m = 1 << lv
        masks.append((row // (2 * m) == col // (2 * m)) & (row // m % 2 == 0) & (col // m % 2 == 1))
    masks += [m.T for m in masks]
    masks += [row < col, row <= col, row > col, row >= col]
    same = row // 64 == col // 64
    masks += [same & (row <= col), same & (row >= col)]
    t = np.arange(SEG)
    f = np.arange(SEG)
    w = 2 * np.pi * np.outer(t, f) / (2 * SEG)
    fwd = np.concatenate([np.cos(w), -np.sin(w)], 1)
    fwd[:, SEG] = np.cos(np.pi * t)
    s0 = -np.sin(w[:, :P])
    inv = np.concatenate([2 * np.cos(w.T), -2 * np.sin(w.T)], 0) / (2 * SEG)
    inv[0] = 1 / (2 * SEG)
    inv[SEG] = np.cos(np.pi * t) / (2 * SEG)
    tt = np.linspace(0.0, 1.0, SEG)[:, None]
    bands = (HY_EMB - 1) // 2
    fr = np.linspace(1e-4, bands - 1, bands)[None, :]
    ww = 2 * np.pi * t[:, None] / SEG
    z = np.concatenate([tt, np.cos(fr * ww), -np.sin(fr * ww)], 1)
    deltas = np.linspace(math.log(1e-2) / 1.5, math.log(1e-2) / 0.3, HW)
    win = np.exp(-tt * np.abs(deltas))
    reset = np.ones((P, NT))
    reset[:, [0, 256, 320, 384, 448]] = 0
    tile = lambda a, n: a.reshape(n, P, -1).transpose(1, 0, 2).reshape(P, -1)
    blk = np.kron(np.eye(2), np.ones((64, 64)))
    f32 = lambda a: np.ascontiguousarray(a, dtype=np.float32)
    return {
        "k_ident": f32(np.eye(P)), "k_mean": f32(np.full((P, P), 1 / D)), "k_blk": f32(blk),
        "k_ones": f32(np.ones((P, P))),
        "k_masks": f32(np.stack(masks, 1).reshape(P, -1)),
        "k_dft": f32(tile(fwd, 2)), "k_sin0": f32(tile(s0, 2)), "k_idft": f32(tile(inv, 4)),
        "k_zT": f32(z.T), "k_win": f32(tile(win, 2)), "k_reset": f32(reset),
    }


NMASK = 2 * LEVELS + 6


def _round_bits(x, bits):
    e = math.floor(math.log2(abs(x)))
    s = 2.0 ** (bits - 1 - e)
    return math.floor(x * s) / s


TWO_PI = 2 * math.pi
PI_A = _round_bits(TWO_PI, 10)
PI_B = _round_bits(TWO_PI - PI_A, 11)
PI_C = TWO_PI - PI_A - PI_B
MAGIC = 1.5 * 2.0 ** 23


def plan():
    items = []

    def add(phase, n, each=16):
        items.extend((phase, c, each) for c in range(n))

    add(("ada", 0), 6)
    for g in range(SUBS):
        if g % 3 != 1:
            add(("up", g), FT // 2, 32)
            add(("down", g), 6)
        elif g == 1:
            add(("even_in", g), 7)
            add(("even_out", g), 2)
        else:
            add(("odd_in", g), 7)
            add(("odd_out", g), 2)
        if g + 1 < SUBS:
            add(("ada", g + 1), 6)
    first, arrival, slot_total = {}, [], [0] * R
    for n, (phase, c, each) in enumerate(items):
        first.setdefault(phase, n)
        slot_total[n % R] += each
        arrival.append(slot_total[n % R])
    return first, arrival


def program(nc, A, K, out):
    first, arrival = plan()
    with ExitStack() as ctx:
        def sb(name, n, dt=F32, parts=P):
            return ctx.enter_context(nc.sbuf_tensor(name, [parts, n], dt))

        h = sb("h", KT * NT)
        u = sb("u", KT * NT)
        ring = sb("ring", R * SLOT)
        big = sb("big", ZT * NT)
        extra = sb("extra", 9472)
        tmp = sb("tmp", 2 * NT)
        rs = sb("rs", NT)
        par = sb("par", 3 * P)
        masks = sb("masks", NMASK * P, U8)
        ident = sb("ident", P)
        mean_w = sb("mean_w", P)
        blk = sb("blk", P)
        ones = sb("ones", P)
        sc = sb("sc", 2 * KT)
        sgc = sb("sgc", 2 * KT)
        mods = sb("mods", 2 * 48)
        cf = sb("cf", ZT * 4)
        hyp = sb("hyp", 4)
        eps = sb("eps", 4)
        small = sb("small", 64)
        psum = ctx.enter_context(nc.psum_tensor("psum", [P, 8, 512], F32))

        hv = h[:, :].rearrange("p (k t) -> p k t", k=KT)
        uv = u[:, :].rearrange("p (k t) -> p k t", k=KT)
        hs = h[:, :].rearrange("p (k s t) -> p k s t", k=KT, s=2)
        us = u[:, :].rearrange("p (k s t) -> p k s t", k=KT, s=2)
        modv = mods[:, :].rearrange("p (b s) -> p b s", s=2)
        bank = [psum[:, b, :] for b in range(8)]
        bigt = big[:, :].rearrange("p (i t) -> p i t", t=NT)
        maskv = masks[:, :].rearrange("p (m t) -> p m t", t=P)
        cfv = cf[:, :].rearrange("p (i j) -> p i j", j=4)

        sems = {}

        def S(name):
            if name not in sems:
                sems[name] = ctx.enter_context(nc.semaphore(name))
            return sems[name]

        def col(name, i=0):
            return par[:, PAR[name] + i:PAR[name] + i + 1]

        def slot(n):
            return ring[:, (n % R) * SLOT:(n % R + 1) * SLOT]

        class Count:
            n = 0

            def step(self):
                self.n += 1
                return 1

        tok_in = big[:, 0:4096].rearrange("p (b d) -> p b d", b=4)
        stage = [big[:, 4096 + i * P:4096 + (i + 1) * P] for i in range(3)]
        w3 = big[0:HY_FO, 4608:6656]
        win = big[:, 6656:7680].rearrange("p (a c) -> p a c", a=2)
        taps = big[:, 7680:9728].rearrange("p (d a c) -> p d a c", d=2, a=2)
        tap_m = big[:, 9728:10752].rearrange("p (a c) -> p a c", a=2)
        zT = big[0:HY_EMB, 10752:11008]
        fw1 = big[0:HY_EMB, 11008:11072]
        fw2 = big[0:HY_FO, 11072:11136]
        pre = big[0:HY_FO, 11136:11392]
        turns = big[0:HY_FO, 11392:11648]
        h1 = big[0:HY_FO, 11648:11904]
        h2 = big[0:HY_FO, 11904:12160]
        skip_row = big[0:1, 12160:13184].rearrange("p (o c) -> p o c", o=2)
        yhy = extra[:, 0:2048].rearrange("p (c t) -> p c t", t=NT)
        kf = extra[:, 2048:7168].rearrange("p (o i c) -> p o i c", o=2, i=5)
        dft = extra[:, 7168:8192].rearrange("p (a f) -> p a f", a=2)
        sin0 = extra[:, 8192:8448].rearrange("p (a f) -> p a f", a=2)
        idft = extra[:, 8448:9472].rearrange("p (f t) -> p f t", f=4)
        vtok = ring[:, 0:2048].rearrange("p (b c) -> p b c", b=4)
        x1tok = ring[:, 2048:4096].rearrange("p (b c) -> p b c", b=4)
        yf = ring[:, 4096:8192].rearrange("p (s i c) -> p s i c", s=2, i=4)
        ft = [ring[:, 8192 + i * 512:8704 + i * 512] for i in range(2)]
        w_up = ring[:, 9216:9728]
        a_up = ring[:, 9728:10240]
        g_up = ring[:, 10240:10752]
        prep = ring[:, 0:2048]
        prep2 = ring[:, 2048:4096]
        three = lambda ap: ap.rearrange("p (c t) -> p c t", t=NT)
        zr, zk, zv = big[:, 12 * NT:16 * NT], big[:, 16 * NT:20 * NT], big[:, 20 * NT:24 * NT]
        sgw = [big[:, 0:2048], big[:, 2048:4096]]
        aa = [big[:, 4096:6144], extra[:, 2048:4096]]
        kd = [extra[:, 4096:6144], zk]
        oacc = extra[:, 6144:8192]
        state = extra[:, 8448:8960].rearrange("p (d c v) -> p d c v", d=2, c=CT)
        gate, kk = u[:, 0:2048], u[:, 2048:4096]
        ar = ring[:, 0:2048].rearrange("p (d c a t) -> p d c a t", d=2, c=CT, a=2)
        bk = ring[:, 2048:4096].rearrange("p (d c a t) -> p d c a t", d=2, c=CT, a=2)
        bkt = ring[:, 4096:6144].rearrange("p (d a c) -> p d a c", d=2, a=2)
        nm = ring[:, 6144:10240].rearrange("p (d h a t) -> p d h a t", d=2, h=4, a=4)
        tu = ring[:, 10240:12288].rearrange("p (d a h t) -> p d a h t", d=2, a=2, h=4)
        zs = ring[:, 12288:13312].rearrange("p (d h t) -> p d h t", d=2, h=4)
        xs = ring[:, 13312:14336].rearrange("p (d a h v) -> p d a h v", d=2, a=2, h=4)
        vt = ring[:, 14336:16384].rearrange("p (b c) -> p b c", b=4)
        cs = tmp[:, 0:512].rearrange("p (c t) -> p c t", c=CT)
        ce = tmp[:, 512:1024].rearrange("p (c t) -> p c t", c=CT)
        half = small[:, 0:8].rearrange("p (d c) -> p d c", d=2)
        edec = small[:, 8:16].rearrange("p (d c) -> p d c", d=2)
        gq = big[:, 0:1024].rearrange("p (c t) -> p c t", c=4)
        gk = big[:, 1024:3072].rearrange("p (c t) -> p c t", c=4)
        gvt = big[:, 3072:7168].rearrange("p (b c) -> p b c", b=4)
        gog = big[:, 7168:9216].rearrange("p (c t) -> p c t", c=8)
        ggd = big[0:32, 9216:9728]
        kout = big[:, 9728:11776].rearrange("p (d c t) -> p d c t", d=2, c=4)
        go = big[:, 9728:11776].rearrange("p (c t) -> p c t", c=8)
        pm = big[:, 11776:13824].rearrange("p (d b h t) -> p d b h t", d=2, b=2, h=4)
        gcs = extra[:, 0:4096].rearrange("p (d c t) -> p d c t", d=2, c=4)
        gup = extra[0:32, 4096:5120].rearrange("p (d c) -> p d c", d=2)
        greset = extra[:, 5120:5632]
        grs = extra[:, 5632:6656].rearrange("p (c t) -> p c t", c=4)
        sq2 = extra[:, 6656:8704].rearrange("p (c t) -> p c t", c=8)
        gg = ring[:, 8192:12288].rearrange("p (d c t) -> p d c t", d=2, c=4)
        gst = ring[:, 0:8192].rearrange("p (d n c v) -> p d n c v", d=2, n=4, c=4)
        qh = ring[:, 8192:10240].rearrange("p (d c t) -> p d c t", d=2, c=4)
        kh = ring[:, 10240:12288].rearrange("p (d c t) -> p d c t", d=2, c=4)
        kht = ring[:, 12288:14336].rearrange("p (d b c) -> p d b c", d=2, b=2)
        kot = ring[:, 14336:16384].rearrange("p (d b c) -> p d b c", d=2, b=2)
        ghalf = small[:, 0:32].rearrange("p (d c n) -> p d c n", d=2, c=4)
        gexp = small[:, 32:64].rearrange("p (d c n) -> p d c n", d=2, c=4)

        def chunk_of(d, j):
            return j if d == 0 else j ^ 1

        XCHUNK = lambda d, n: n if d == 0 else 3 - n

        def segments(g):
            return (0, 1) if g < 4 else (1,)

        resid_base = [0]
        for g in range(SUBS):
            resid_base.append(resid_base[-1] + KT * len(segments(g)))

        block = ctx.enter_context(nc.Block())

        @block.sync
        def _(sp):
            def free(n):
                if not isinstance(n, int) or n >= R:
                    sp.wait_ge(S("slot_used"), n - (R - 1))

            def load_ada(g):
                w = A["ada_w"][g // 3].rearrange("(k p) n -> p k n", p=P)
                for c in range(6):
                    n = first["ada", g] + c
                    free(n)
                    at = 3 * D * (g % 3) + 512 * c
                    sp.dma_start(slot(n).rearrange("p (k n) -> p k n", k=KT),
                                 w[:, :, at:at + 512]).then_inc(S(f"slot{n % R}"), 16)

            def load_ffn(g):
                l, i = g // 3, (g % 3) // 2
                wg = A["ffn_wg"][l, i].rearrange("(k p) f -> p k f", p=P)
                wu = A["ffn_wu"][l, i].rearrange("(k p) f -> p k f", p=P)
                n0 = first["up", g]

                def pair(n, c, wait):
                    dst = slot(n).rearrange("p (a k f) -> p a k f", a=2, k=KT)
                    sp.wait_ge(S("slot_used"), wait)
                    sp.dma_start(dst[:, 0], wg[:, :, bass.ds(c * 256, 256)]).then_inc(S(f"slot{n % R}"), 16)
                    sp.dma_start(dst[:, 1], wu[:, :, bass.ds(c * 256, 256)]).then_inc(S(f"slot{n % R}"), 16)

                full = FT // 2 // R
                with sp.Fori(0, full) as i4:
                    for r in range(R):
                        pair(n0 + r, i4 * R + r, i4 * R + (n0 + r - R + 1))
                for c in range(full * R, FT // 2):
                    pair(n0 + c, c, n0 + c - R + 1)
                wd = A["ffn_wd"][l, i].rearrange("(k p) d -> p k d", p=P)
                for c in range(6):
                    n = first["down", g] + c
                    m = min(4, FT - 4 * c)
                    free(n)
                    sp.dma_start(slot(n)[:, 0:m * D].rearrange("p (k d) -> p k d", k=m),
                                 wd[:, 4 * c:4 * c + m, :]).then_inc(S(f"slot{n % R}"), 16)

            def load_cols(phase, g, w, blocks):
                v = w.rearrange("(k p) n -> p k n", p=P)
                for c, (at, m) in enumerate(blocks):
                    n = first[phase, g] + c
                    free(n)
                    sp.dma_start(slot(n)[:, 0:KT * m].rearrange("p (k n) -> p k n", k=KT),
                                 v[:, :, at:at + m]).then_inc(S(f"slot{n % R}"), 16)

            load_ada(0)
            for g in range(SUBS):
                if g == 1:
                    load_cols("even_in", g, A["ev_w_in"][0], [(512 * c, min(512, ZT * P - 512 * c)) for c in range(7)])
                    sp.wait_ge(S("scratch_free"), 1)
                    load_cols("even_out", g, A["ev_w_out"][0], [(0, 512), (512, 512)])
                elif g == 4:
                    load_cols("odd_in", g, A["od_w_in"][0],
                              [(512, 512), (2048, 32), (0, 512), (1024, 512), (1536, 512), (2080, 512), (2592, 512)])
                    sp.wait_ge(S("scratch_free"), 2)
                    load_cols("odd_out", g, A["od_w_out"][0], [(0, 512), (512, 512)])
                else:
                    load_ffn(g)
                if g + 1 < SUBS:
                    load_ada(g + 1)
            sp.wait_ge(S("rows_out"), 4)
            rows = out[0].rearrange("(r c) d -> r c d", r=ROWS)
            o_sb = big[:, 0:2048].rearrange("p (b d) -> p b d", b=2)
            for b in range(2):
                for r in range(ROWS):
                    sp.dma_start(rows[r, 32 * b:32 * b + 32, :], o_sb[r:P:ROWS, b, :]).then_inc(S("stored"), 16)
            sp.wait_ge(S("stored"), 16 * 8)

        @block.scalar
        def _(act):
            def load(name, dst, src):
                act.dma_start(dst, src).then_inc(S(name), 16)

            load("ld_ident", ident[:, :], K["k_ident"])
            l0 = [("ada_b", 0, 72, A["ada_b"][0:1].rearrange("l (t p) -> (l t) p", p=P), 0),
                  ("ln_g", 72, 48, A["ln_g"].rearrange("l i (t p) -> (l i t) p", p=P), 0),
                  ("ada_b", 0, 72, A["ada_b"][1:2].rearrange("l (t p) -> (l t) p", p=P), 1),
                  ("ln_b", 72, 48, A["ln_b"].rearrange("l i (t p) -> (l i t) p", p=P), 1)]
            for _, at, n, src, s in l0:
                load("ld_par", stage[s][at:at + n, :], src)
            third = [("conv_w", 36, A["hy_conv_w"].rearrange("e j (t p) -> (e j t) p", p=P)),
                     ("conv_b", 12, A["hy_conv_b"].rearrange("e (t p) -> (e t) p", p=P)),
                     ("mu", 15, A["rw_mu"].rearrange("e (t p) -> (e t) p", p=P)),
                     ("w0", 8, A["rw_w0"].rearrange("e d (t p) -> (e d t) p", p=P)),
                     ("a0", 8, A["rw_a0"].rearrange("e d (t p) -> (e d t) p", p=P)),
                     ("k_k", 4, A["rw_k_k"].rearrange("e (t p) -> (e t) p", p=P)),
                     ("k_a", 4, A["rw_k_a"].rearrange("e (t p) -> (e t) p", p=P)),
                     ("r_k", 4, A["rw_r_k"].rearrange("e (t a) n -> (e t) (a n)", a=2)),
                     ("gn_g", 4, A["rw_gn_g"].rearrange("e (t p) -> (e t) p", p=P)),
                     ("gn_b", 4, A["rw_gn_b"].rearrange("e (t p) -> (e t) p", p=P)),
                     ("gla_b", 8, A["gla_g_b"].rearrange("e d (t p) -> (e d t) p", p=P)),
                     ("norm_g", 2, A["gla_norm_g"].rearrange("e (t p) -> (e t) p", p=P)),
                     ("c", 8, A["c"].rearrange("e (t p) -> (e t) p", p=P)),
                     ("c_ctx", 8, A["c_ctx"].rearrange("(t p) -> t p", p=P))]
            for name, n, src in third:
                at = PAR[name] - 2 * P
                load("ld_par", stage[2][at:at + n, :], src)
            for b in range(4):
                src = A["ctx"] if b < 2 else A["x"]
                load("ld_tok", tok_in[:, b, :], src[0, (b % 2) * P:(b % 2 + 1) * P, :])
            load("ld_filt", zT, K["k_zT"])
            load("ld_filt", fw1, A["hy_f_w1"][0])
            load("ld_filt", fw2, A["hy_f_w2"][0])
            for i, name in enumerate(("hy_f_b1", "hy_f_freq1", "hy_f_b2", "hy_f_freq2")):
                load("ld_filt", hyp[0:HY_FO, i:i + 1], A[name].rearrange("e n -> n e"))
            load("ld_filt", w3, A["hy_f_w3"][0])
            load("ld_filt", big[:, 6656:7680], K["k_win"])
            load("ld_filt", skip_row, A["hy_skip"].rearrange("e o c -> e o c"))
            load("ld_filt", extra[:, 7168:8192], K["k_dft"])
            load("ld_filt", extra[:, 8192:8448], K["k_sin0"])
            load("ld_filt", extra[:, 8448:9472], K["k_idft"])
            load("ld_const", mean_w[:, :], K["k_mean"])
            load("ld_const", blk[:, :], K["k_blk"])
            load("ld_const", ones[:, :], K["k_ones"])
            load("ld_const", u[:, 0:NMASK * P], K["k_masks"])

            act.wait_ge(S("par_done"), 1)
            act.activation(sgc[:, :], par[:, PAR["c"]:PAR["c"] + 16], ACT.Silu).then_inc(S("silu_c"), 1)
            for k in range(KT):
                act.wait_ge(S("tok_turned"), k + 1)
                act.activation(hv[:, k], bank[(k + 1) % 8], ACT.Copy).then_inc(S("h_ready"), 1)
            act.wait_ge(S("sin_arg"), 1)
            act.activation(h1, pre, ACT.Sin).then_inc(S("sin_done"), 1)
            act.wait_ge(S("sin_arg"), 2)
            act.activation(h2, pre, ACT.Sin).then_inc(S("sin_done"), 1)
            for o in range(2):
                act.wait_ge(S("filt_dft"), o + 1)
                for i, b in ((0, 0), (1, 1), (2, 3), (3, 4), (4, 0)):
                    act.activation(kf[:, o, i], bank[b], ACT.Copy).then_inc(S("kf_done"), 1)
                act.wait_ge(S("kf_done"), 6 * o + 5)
                act.activation(kf[0:1, o, 4], bank[5][0:1], ACT.Copy).then_inc(S("kf_done"), 1)

            def u_ctx(g):
                for k in range(KT):
                    if k == 0:
                        act.wait_ge(S("mods"), g + 1)
                    if g == 0:
                        act.wait_ge(S("h_ready"), KT)
                    else:
                        act.wait_ge(S("h_ready"), KT * g + k + 1)
                    act.activation(us[:, k, 0], hs[:, k, 0], ACT.Identity, scale=modv[:, 24 * (g % 2) + 8 + k, 0:1],
                                   bias=modv[:, 24 * (g % 2) + k, 0:1]).then_inc(S("u_ctx"), 1)
                if g < 4:
                    act.wait_ge(S("u_ctx"), KT * (g + 1))
                    act.activation(hs[:, :, 0], hs[:, :, 0], ACT.Copy, scale=ALPHA).then_inc(S("scaled_ctx"), 1)

            def ffn_silu(g):
                f = (0, 2, 3, 5).index(g)
                T0, TN = (0, NT) if g < 5 else (SEG, SEG)

                def one(ready, jf):
                    act.wait_ge(S("gu_ready"), ready)
                    act.activation(tmp[:, jf * NT:jf * NT + TN], bank[2 * jf][:, 0:TN], ACT.Silu)\
                       .then_inc(S("silu"), 1)

                with act.Fori(0, FT // 2) as c:
                    for jf in range(2):
                        one(c * 2 + (FT * f + jf + 1), jf)

            def norm(g):
                T0, TN = (0, NT) if g < 4 else (SEG, SEG)
                for k in range(KT):
                    act.wait_ge(S("centred"), KT * g + k + 1)
                    if KT * g + k - 1 > 0:
                        act.wait_ge(S("sq_used"), KT * g + k - 1)
                    act.activation(tmp[:, (k % 2) * NT:(k % 2) * NT + TN], hv[:, k, T0:NT], ACT.Square)\
                       .then_inc(S("sq"), 1)
                act.wait_ge(S("sq_used"), KT * (g + 1))
                act.activation(rs[:, 0:TN], bank[1][:, 0:TN], ACT.Sqrt, bias=eps[:, 0:1]).then_inc(S("std"), 1)
                for k in range(KT):
                    act.wait_ge(S("normed"), KT * g + k + 1)
                    sg, sb_ = col("ln_g", 8 * g + k), col("ln_b", 8 * g + k)
                    if g == 2:
                        act.activation(hs[:, k, 0], us[:, k, 0], ACT.Identity, scale=sg, bias=sb_)
                        act.activation(hs[:, k, 1].rearrange("p (c r) -> p r c", r=ROWS),
                                       us[:, k, 1].rearrange("p (r c) -> p r c", r=ROWS),
                                       ACT.Identity, scale=sg, bias=sb_).then_inc(S("h_ready"), 1)
                    else:
                        act.activation(hv[:, k, T0:NT], uv[:, k, T0:NT], ACT.Identity, scale=sg, bias=sb_)\
                           .then_inc(S("h_ready"), 1)

            def even_mixer():
                for i in range(ZT):
                    act.wait_ge(S("z_psum"), i + 1)
                    act.activation(bigt[:, i], bank[i % 8], ACT.Identity, scale=cfv[:, i, 1:2], bias=cfv[:, i, 3:4])\
                       .then_inc(S("z_main"), 1)
                act.wait_ge(S("z_done"), ZT)
                load("ld_lora", w_up, A["rw_w_up"].rearrange("e d l n -> (e d l) n"))
                load("ld_lora", a_up, A["rw_a_up"].rearrange("e d l n -> (e d l) n"))
                load("ld_lora", g_up, A["rw_g_up"][0])
                act.activation(bigt[:, 24], bigt[:, 24], ACT.Tanh).then_inc(S("lora_in"), 1)
                act.activation(bigt[:, 26], bigt[:, 26], ACT.Sigmoid).then_inc(S("lora_in"), 1)
                for b in range(4):
                    act.wait_ge(S("hy_turned"), 2 * b + 1)
                    act.activation(vtok[:, b], bank[2 * b], ACT.Copy).then_inc(S("vtok"), 1)
                    act.wait_ge(S("hy_turned"), 2 * b + 2)
                    act.activation(x1tok[:, b], bank[2 * b + 1], ACT.Copy).then_inc(S("vtok"), 1)
                act.wait_ge(S("hy_done"), 4)
                for q in range(20):
                    act.wait_ge(S("lora_psum"), q + 1)
                    if q < 8:
                        act.activation(sgw[q // 4][:, (q % 4) * NT:(q % 4 + 1) * NT], bank[q % 8], ACT.Sigmoid,
                                       bias=col("w0", q)).then_inc(S("lora_out"), 1)
                    elif q < 16:
                        e = q - 8
                        act.activation(aa[e // 4][:, (e % 4) * NT:(e % 4 + 1) * NT], bank[q % 8], ACT.Sigmoid,
                                       bias=col("a0", e)).then_inc(S("lora_out"), 1)
                    else:
                        e = q - 16
                        act.activation(gate[:, e * NT:(e + 1) * NT], bank[q % 8], ACT.Copy)\
                           .then_inc(S("lora_out"), 1)
                act.wait_ge(S("kk_raw"), 1)
                act.activation(prep, kk, ACT.Square).then_inc(S("kk_sq"), 1)
                for i in range(4):
                    act.wait_ge(S("kk_sum"), i + 1)
                    act.activation(prep2[:, i * NT:(i + 1) * NT], bank[i], ACT.Sqrt).then_inc(S("kk_norm"), 1)
                for b in range(4):
                    act.wait_ge(S("v_turned"), b + 1)
                    act.activation(vt[:, b], bank[4 + b], ACT.Copy).then_inc(S("vt"), 1)
                for j in range(4):
                    for d in range(2):
                        act.wait_ge(S("expo"), 2 * j + d + 1)
                        up, dn = (-DECAY, DECAY) if d == 0 else (DECAY, -DECAY)
                        incl, excl = (cs, ce) if d == 0 else (ce, cs)
                        act.activation(edec[:, d], half[:, d], ACT.Exp, scale=-DECAY)
                        act.activation(ar[:, d, :, 1], incl, ACT.Exp, scale=up)
                        act.activation(ar[:, d, :, 0], excl, ACT.Exp, scale=up)
                        act.activation(bk[:, d, :, 0], incl, ACT.Exp, scale=dn).then_inc(S("exped"), 1)
                    for q in range(4):
                        act.wait_ge(S("bk_turned"), 4 * j + q + 1)
                        act.activation(bkt[:, q // 2, q % 2], bank[q], ACT.Copy).then_inc(S("bkt"), 1)
                    for hf in range(2):
                        gi = 2 * j + hf
                        for lv in range(1, LEVELS):
                            for d in range(2):
                                act.wait_ge(S("z_mm"), 2 * (LEVELS * gi + lv) + d + 1)
                                act.activation(zs[:, d].rearrange("p h t -> p (h t)"), bank[d], ACT.Copy)\
                                   .then_inc(S("zs"), 1)
                        for d in range(2):
                            act.wait_ge(S("x_mm"), 2 * gi + d + 1)
                            for q in range(2):
                                dst = xs[:, d, 0].rearrange("p (c q) v -> p q c v", q=2)[:, q]
                                ins = act.activation(dst, bank[2 * d + q][:, 0:128].rearrange("p (c v) -> p c v", c=2),
                                                     ACT.Copy)
                            ins.then_inc(S("xs"), 1)
                act.wait_ge(S("gn_centred"), 4)
                act.activation(prep, oacc, ACT.Square).then_inc(S("gn_sq"), 1)
                for i in range(4):
                    act.wait_ge(S("gn_var"), i + 1)
                    act.activation(prep2[:, i * NT:(i + 1) * NT], bank[4 + i], ACT.Sqrt, scale=1 / 64.0,
                                   bias=eps[:, 2:3]).then_inc(S("gn_std"), 1)

            def odd_mixer():
                act.wait_ge(S("gup_zero"), 1)
                load("ld_gla", gup[0:16, 0, :], A["gla_g_up"][0, 0])
                load("ld_gla", gup[16:32, 1, :], A["gla_g_up"][0, 1])
                load("ld_gla", greset, K["k_reset"])
                for i in range(OD_TILES):
                    act.wait_ge(S("z1_psum"), i + 1)
                    kind, j = od_tile(i)
                    if kind == "k":
                        ins = act.activation(gk[:, j], bank[i % 8], ACT.Copy)
                    elif kind == "gd":
                        ins = act.activation(ggd, bank[i % 8][0:32], ACT.Copy)
                    elif kind == "q":
                        ins = act.activation(gq[:, j], bank[i % 8][:, 0:SEG], ACT.Copy)
                    elif kind == "v":
                        ins = act.activation(gvt[:, j % 4, (j // 4) * 512:(j // 4 + 1) * 512], bank[i % 8], ACT.Copy)
                    else:
                        ins = act.activation(gog[:, j], bank[i % 8][:, 0:SEG], ACT.Silu)
                    ins.then_inc(S("z1_done"), 1)
                for q in range(8):
                    d, c = q // 4, q % 4
                    act.wait_ge(S("lg_psum"), q + 1)
                    act.activation(gcs[:, d, c], bank[q], ACT.Abs, bias=col("gla_b", q)).then_inc(S("lg_abs"), 1)
                act.wait_ge(S("lg_abs"), 8)
                act.activation(extra[:, 0:4096], extra[:, 0:4096], ACT.Exp, scale=-1.0).then_inc(S("lg_exp"), 1)
                act.wait_ge(S("lg_exp"), 1)
                act.activation(extra[:, 0:4096], extra[:, 0:4096], ACT.Ln, bias=eps[:, 3:4]).then_inc(S("lg_ln"), 1)
                act.wait_ge(S("ctx_arg"), 1)
                act.activation(kout.rearrange("p d c t -> p (d c t)"), kout.rearrange("p d c t -> p (d c t)"),
                               ACT.Exp, scale=1 / GLA_N).then_inc(S("ctx_exp"), 1)
                act.wait_ge(S("lat_arg"), 1)
                fl = lambda x: x.rearrange("p c t -> p (c t)")
                act.activation(gexp.rearrange("p d c n -> p (d c n)"), ghalf.rearrange("p d c n -> p (d c n)"),
                               ACT.Exp, scale=1 / GLA_N)
                act.activation(fl(qh[:, 0]), fl(sq2[:, 0:4]), ACT.Exp, scale=1 / GLA_N)
                act.activation(fl(kh[:, 0]), fl(sq2[:, 0:4]), ACT.Exp, scale=-1 / GLA_N)
                act.activation(fl(qh[:, 1]), fl(sq2[:, 4:8]), ACT.Exp, scale=-1 / GLA_N)
                act.activation(fl(kh[:, 1]), fl(sq2[:, 4:8]), ACT.Exp, scale=1 / GLA_N).then_inc(S("lat_exp"), 1)
                for q in range(4):
                    act.wait_ge(S("ko_turned"), q + 1)
                    act.activation(kot[:, q // 2, q % 2], bank[q], ACT.Copy).then_inc(S("kot"), 1)
                for q in range(4):
                    act.wait_ge(S("kh_turned"), q + 1)
                    act.activation(kht[:, q // 2, q % 2], bank[4 + q], ACT.Copy).then_inc(S("kht"), 1)
                act.wait_ge(S("go_done"), 4)
                act.activation(sq2.rearrange("p c t -> p (c t)"), go.rearrange("p c t -> p (c t)"), ACT.Square)\
                   .then_inc(S("go_sq"), 1)
                for i in range(2):
                    act.wait_ge(S("go_sum"), i + 1)
                    act.activation(grs[:, 2 * i:2 * i + 2].rearrange("p c t -> p (c t)"), bank[i], ACT.Sqrt,
                                   scale=1.0 / HV, bias=eps[:, 1:2]).then_inc(S("go_std"), 1)

            for g in range(SUBS):
                if g < 5:
                    u_ctx(g)
                if g == 1:
                    even_mixer()
                elif g == 4:
                    odd_mixer()
                else:
                    ffn_silu(g)
                norm(g)
            for i in range(4):
                act.wait_ge(S("out_turned"), i + 1)
                act.activation(big[:, i * 512:(i + 1) * 512], bank[i], ACT.Copy).then_inc(S("rows_out"), 1)

        @block.tensor
        def _(pe):
            def mm(dst, w, x, first_, last):
                return pe.matmul(dst, w, x, start=first_, stop=last, skip_group_check=True)

            pe.wait_ge(S("ld_ident"), 16)
            pe.wait_ge(S("ld_par"), 16 * 18)
            for i, n in enumerate((120, 120, 125)):
                ins = pe.transpose(bank[0][:, i * P:i * P + n], stage[i][0:n, :], ident[0:n, 0:n])
            ins.then_inc(S("par_turned"), 1)
            pe.wait_ge(S("ld_tok"), 64)
            for k in range(KT):
                if k == KT - 1:
                    pe.wait_ge(S("par_done"), 1)
                for b in range(4):
                    ins = pe.transpose(bank[(k + 1) % 8][:, b * P:(b + 1) * P], tok_in[:, b, k * P:(k + 1) * P],
                                       ident[:, :])
                ins.then_inc(S("tok_turned"), 1)

            def ada(g, part):
                for c in part:
                    n = first["ada", g] + c
                    pe.wait_ge(S(f"slot{n % R}"), arrival[n])
                    w = slot(n).rearrange("p (k n) -> p k n", k=KT)
                    for j in range(4):
                        t = 4 * c + j
                        for k in range(KT):
                            ins = mm(bank[2][:, 2 * t:2 * t + 2], w[:, k, j * P:(j + 1) * P],
                                     sc[:, 2 * k:2 * k + 2], k == 0, k == KT - 1)
                    ins.then_inc(S("slot_used"), 1)

            def taps_of(o):
                pe.wait_ge(S("taps_free"), o + 1)
                for dr in range(2):
                    for a in range(2):
                        ins = mm(bank[4 + 2 * dr + a], h2[:, a * P:(a + 1) * P],
                                 w3[:, (2 * o + dr) * HW:(2 * o + dr + 1) * HW], True, True)
                ins.then_inc(S("filt_taps"), 1)

            def response_of(o):
                pe.wait_ge(S("taps"), o + 1)
                if o:
                    pe.wait_ge(S("kf_done"), 6 * o)
                for a in range(2):
                    st, en = a == 0, a == 1
                    mm(bank[0], dft[:, a, 0:P], taps[:, 0, a], st, en)
                    mm(bank[1], dft[:, a, P:2 * P], taps[:, 0, a], st, en)
                    mm(bank[3], sin0[:, a], tap_m[:, a], st, en)
                    mm(bank[4], dft[:, a, 3 * P:4 * P], tap_m[:, a], st, en)
                    ins = mm(bank[5][0:1], dft[:, a, 2 * P:2 * P + 1], taps[:, 0, a], st, en)
                ins.then_inc(S("filt_dft"), 1)

            pe.wait_ge(S("h_ready"), KT)
            pe.wait_ge(S("ld_filt"), 16 * 13)
            mm(bank[3][0:HY_FO, 0:SEG], fw1, zT, True, True).then_inc(S("filt_mm"), 1)
            pe.wait_ge(S("sc_ready"), 1)
            ada(0, (0, 1))
            pe.wait_ge(S("sin_done"), 1)
            mm(bank[4][0:HY_FO, 0:SEG], fw2, h1, True, True).then_inc(S("filt_mm"), 1)
            ada(0, (2, 3))
            pe.wait_ge(S("sin_done"), 2)
            taps_of(0)
            ada(0, (4, 5))
            response_of(0)
            taps_of(1)
            response_of(1)
            pe.wait_ge(S("ld_const"), 64)

            def ffn(g):
                f = (0, 2, 3, 5).index(g)
                T0, TN = (0, NT) if g < 5 else (SEG, SEG)
                pe.wait_ge(S("u_lat"), KT * (g + 1))
                if g < 5:
                    pe.wait_ge(S("u_ctx"), KT * (g + 1))
                n0 = first["up", g]

                def chunk(n, there, freed):
                    pe.wait_ge(S(f"slot{n % R}"), there)
                    w = slot(n).rearrange("p (a k f) -> p a k f", a=2, k=KT)
                    for jf in range(2):
                        pe.wait_ge(S("pairs_free"), freed + jf)
                        for a in range(2):
                            for k in range(KT):
                                ins = mm(bank[2 * jf + a][:, 0:TN], w[:, a, k, jf * P:(jf + 1) * P],
                                         uv[:, k, T0:NT], k == 0, k == KT - 1)
                        ins.then_inc(S("gu_ready"), 1)
                    pe.wait_ge(S("gu_ready"), freed + 1)
                    pe.sem_inc(S("slot_used"), 1)

                full = FT // 2 // R
                with pe.Fori(0, full) as i:
                    for r in range(R):
                        chunk(n0 + r, i * 32 + arrival[n0 + r], i * (2 * R) + (FT * f + 2 * r + 1))
                for c in range(full * R, FT // 2):
                    chunk(n0 + c, arrival[n0 + c], FT * f + 2 * c + 1)
                pe.wait_ge(S("pairs_free"), FT * (f + 1) + 2)
                for c in range(6):
                    n = first["down", g] + c
                    m = min(4, FT - 4 * c)
                    pe.wait_ge(S(f"slot{n % R}"), arrival[n])
                    w = slot(n)[:, 0:m * D].rearrange("p (k d) -> p k d", k=m)
                    for j in range(m):
                        kt = 4 * c + j
                        for t in range(KT):
                            ins = mm(bank[t][:, 0:TN], w[:, j, t * P:(t + 1) * P], bigt[:, kt, 0:TN],
                                     kt == 0, kt == FT - 1)
                            if kt == FT - 1:
                                ins.then_inc(S("y_done"), 1)
                    if kt == FT - 1:
                        pe.wait_ge(S("y_done"), KT * (g + 1))
                        pe.sem_inc(S("slot_used"), 1)
                    else:
                        ins.then_inc(S("slot_used"), 1)

            def norm(g):
                T0, TN = (0, NT) if g < 4 else (SEG, SEG)
                for k in range(KT):
                    pe.wait_ge(S("resid"), resid_base[g] + len(segments(g)) * (k + 1))
                    ins = mm(bank[0][:, 0:TN], mean_w[:, :], hv[:, k, T0:NT], k == 0, k == KT - 1)
                ins.then_inc(S("mean"), 1)
                if g + 1 < SUBS:
                    ada(g + 1, range(3))
                for k in range(KT):
                    pe.wait_ge(S("sq"), KT * g + k + 1)
                    mm(bank[1][:, 0:TN], mean_w[:, :], tmp[:, (k % 2) * NT:(k % 2) * NT + TN], k == 0,
                       k == KT - 1).then_inc(S("sq_used"), 1)
                if g + 1 < SUBS:
                    ada(g + 1, range(3, 6))

            def project_out(g, phase, left, right, TN):
                for c in range(2):
                    n = first[phase, g] + c
                    pe.wait_ge(S(f"slot{n % R}"), arrival[n])
                    w = slot(n).rearrange("p (k n) -> p k n", k=KT)
                    for j in range(4):
                        for k in range(KT):
                            src = left[:, k, 0:TN] if k < 4 else right[:, k - 4, 0:TN]
                            ins = mm(bank[4 * c + j][:, 0:TN], w[:, k, j * P:(j + 1) * P], src, k == 0, k == KT - 1)
                        ins.then_inc(S("y_done"), 1)
                    pe.wait_ge(S("y_done"), KT * g + 4 * (c + 1))
                    pe.sem_inc(S("slot_used"), 1)

            def even_mixer():
                pe.wait_ge(S("u_lat"), KT * 2)
                pe.wait_ge(S("u_ctx"), KT * 2)
                for c in range(7):
                    n = first["even_in", 1] + c
                    pe.wait_ge(S(f"slot{n % R}"), arrival[n])
                    m = min(4, ZT - 4 * c)
                    w = slot(n)[:, 0:KT * m * P].rearrange("p (k n) -> p k n", k=KT)
                    for j in range(m):
                        i = 4 * c + j
                        if i >= 8:
                            pe.wait_ge(S("z_done"), i - 7)
                        for k in range(KT):
                            ins = mm(bank[i % 8], w[:, k, j * P:(j + 1) * P], uv[:, k], k == 0, k == KT - 1)
                        ins.then_inc(S("z_psum"), 1)
                    pe.wait_ge(S("z_psum"), i + 1)
                    pe.sem_inc(S("slot_used"), 1)
                pe.wait_ge(S("z_done"), ZT)
                for b in range(4):
                    for q in range(2):
                        for c in range(CT):
                            ins = pe.transpose(bank[2 * b + q][:, c * P:(c + 1) * P],
                                               bigt[:, 4 * q + c, b * P:(b + 1) * P], ident[:, :])
                        ins.then_inc(S("hy_turned"), 1)
                pe.wait_ge(S("vtok"), 8)
                for o in range(2):
                    for s in range(2):
                        if o:
                            pe.wait_ge(S("hy_y1"), 2 * s + 2)
                        for i in range(4):
                            for a in range(2):
                                ins = mm(bank[4 * s + i], dft[:, a, i * P:(i + 1) * P], vtok[:, 2 * s + a],
                                         a == 0, a == 1)
                        ins.then_inc(S("hy_f"), 1)
                    for s in range(2):
                        pe.wait_ge(S("hy_mul"), 2 * o + s + 1)
                        if o == 0:
                            for a in range(2):
                                for i in range(4):
                                    ins = mm(bank[4 * s + a], idft[:, i, a * P:(a + 1) * P], yf[:, s, i],
                                             i == 0, i == 3)
                        else:
                            for c in range(CT):
                                for i in range(4):
                                    ins = mm(bank[4 * s + c // 2][:, (c % 2) * SEG:(c % 2 + 1) * SEG],
                                             yf[:, s, i, c * P:(c + 1) * P], idft[:, i], i == 0, i == 3)
                        ins.then_inc(S("hy_i"), 1)
                pe.wait_ge(S("hy_done"), 4)
                pe.wait_ge(S("lora_in"), 2)
                pe.wait_ge(S("ld_lora"), 48)
                for q in range(20):
                    if q >= 8:
                        pe.wait_ge(S("lora_out"), q - 7)
                    d, c = q // 4, q % 4
                    lo = 64 * (d % 2)
                    if q < 16:
                        w = (w_up if q < 8 else a_up)[lo:lo + 64, c * P:(c + 1) * P]
                        x = bigt[lo:lo + 64, 24 if q < 8 else 25]
                    else:
                        w, x = g_up[:, c * P:(c + 1) * P], bigt[:, 26]
                    mm(bank[q % 8], w, x, True, True).then_inc(S("lora_psum"), 1)
                pe.wait_ge(S("lora_out"), 20)
                pe.wait_ge(S("kk_sq"), 1)
                for i in range(4):
                    mm(bank[i], blk[:, :], prep[:, i * NT:(i + 1) * NT], True, True).then_inc(S("kk_sum"), 1)
                for b in range(4):
                    for c in range(CT):
                        ins = pe.transpose(bank[4 + b][:, c * P:(c + 1) * P], zv[:, c * NT + b * P:c * NT + (b + 1) * P],
                                           ident[:, :])
                    ins.then_inc(S("v_turned"), 1)
                pe.wait_ge(S("bonus_in"), 1)
                for i in range(4):
                    mm(bank[i], blk[:, :], prep[:, i * NT:(i + 1) * NT], True, True).then_inc(S("bonus_sum"), 1)
                pe.wait_ge(S("vt"), 4)
                pe.wait_ge(S("prepared"), 1)
                pe.wait_ge(S("zeroed"), 1)
                for j in range(4):
                    for d in range(2):
                        pe.wait_ge(S("slots"), 2 * j + d + 1)
                        if d == 0 and j:
                            pe.wait_ge(S("o_add"), 8 * j)
                            pe.wait_ge(S("state_new"), 4 * j)
                        for q in range(2):
                            for c in range(CT):
                                ins = pe.transpose(bank[2 * d + q][:, c * P:(c + 1) * P], bk[:, d, c, q], ident[:, :])
                            ins.then_inc(S("bk_turned"), 1)
                    pe.wait_ge(S("bkt"), 4 * (j + 1))
                    for hf in range(2):
                        gi = 2 * j + hf
                        if hf:
                            pe.wait_ge(S("o_add"), 4 * gi)
                            pe.wait_ge(S("state_new"), 4 * j + 2)
                        for d in range(2):
                            for hh in range(4):
                                c, lo = 2 * hf + hh // 2, 64 * (hh % 2)
                                rhs = ar[lo:lo + 64, d, c].rearrange("p a t -> p (a t)")
                                for q in range(2):
                                    ins = mm(bank[4 * d + hh][:, 256 * q:256 * q + 256], bk[lo:lo + 64, d, c, q],
                                             rhs, True, True)
                                ins.then_inc(S("n_mm"), 1)
                        for lv in range(LEVELS):
                            for d in range(2):
                                if lv == 0:
                                    pe.wait_ge(S("n_done"), 8 * gi + 4 * (d + 1))
                                    if d == 0:
                                        pe.wait_ge(S("n_done"), 8 * gi + 8)
                                else:
                                    pe.wait_ge(S("tu"), (2 * (gi * LEVELS + lv - 1) + d + 1) * 2)
                                for hh in range(4):
                                    ins = mm(bank[d][:, hh * P:(hh + 1) * P], nm[:, d, hh, 0],
                                             ident[:, :] if lv == 0 else tu[:, d, 0, hh], True, True)
                                ins.then_inc(S("z_mm"), 1)
                            if lv == 0:
                                continue
                            for d in range(2):
                                pe.wait_ge(S("zs"), 2 * (gi * (LEVELS - 1) + lv - 1) + d + 1)
                                if lv < LEVELS - 1:
                                    for hh in range(4):
                                        mm(bank[2 + d][:, hh * P:(hh + 1) * P], tu[:, d, 1, hh], zs[:, d, hh],
                                           True, True)
                                for hh in range(4):
                                    ins = mm(bank[4 + d][:, hh * P:(hh + 1) * P], zs[:, d, hh], tu[:, d, 1, hh],
                                             True, True)
                                ins.then_inc(S("d_mm"), 1)
                        vcol = lambda hh: (4 * hf + hh) * 64
                        for d in range(2):
                            pe.wait_ge(S("tu"), 2 * LEVELS * 2 * (gi + 1))
                            ch = chunk_of(d, j)
                            if hf == 0 and d == 0:
                                pe.wait_ge(S("state_in"), 2 * (j + 1))
                            for hh in range(4):
                                c, lo = 2 * hf + hh // 2, 64 * (hh % 2)
                                dst = bank[2 * d + hh % 2][:, (hh // 2) * 64:(hh // 2 + 1) * 64]
                                mm(dst, ar[lo:lo + 64, d, c, 0], state[lo:lo + 64, d, c], True, False)
                                ins = mm(dst, nm[:, d, hh, 2], vt[:, ch, vcol(hh):vcol(hh) + 64], False, True)
                            ins.then_inc(S("x_mm"), 1)
                        for d in range(2):
                            pe.wait_ge(S("xs"), 2 * gi + d + 1)
                            for hh in range(4):
                                ins = mm(bank[4 + d][:, hh * 64:(hh + 1) * 64], tu[:, d, 1, hh], xs[:, d, 0, hh],
                                         True, True)
                            ins.then_inc(S("sa_mm"), 1)
                        for d in range(2):
                            pe.wait_ge(S("sa"), 2 * gi + d + 1)
                            ch = chunk_of(d, j)
                            for hh in range(4):
                                c, lo = 2 * hf + hh // 2, 64 * (hh % 2)
                                v = vt[:, ch, vcol(hh):vcol(hh) + 64]
                                dst = bank[6 + hh % 2][lo:lo + 64, (2 * d + hh // 2) * P:(2 * d + hh // 2 + 1) * P]
                                mm(dst, xs[:, d, 1, hh], nm[:, d, hh, 1], True, False)
                                mm(dst, v, nm[:, d, hh, 3], False, False)
                                mm(dst, state[lo:lo + 64, d, c], ar[lo:lo + 64, d, c, 1], False, True)
                                dst = bank[d][lo:lo + 64, (hh // 2) * 64:(hh // 2 + 1) * 64]
                                mm(dst, bkt[:, d, 0, vcol(hh):vcol(hh) + 64], xs[:, d, 1, hh], True, False)
                                ins = mm(dst, bkt[:, d, 1, vcol(hh):vcol(hh) + 64], v, False, True)
                            ins.then_inc(S("os_mm"), 1)
                pe.wait_ge(S("o_add"), 32)
                pe.wait_ge(S("state_new"), 16)
                for i in range(4):
                    mm(bank[i], blk[:, :], oacc[:, i * NT:(i + 1) * NT], True, True).then_inc(S("gn_mean"), 1)
                pe.wait_ge(S("gn_sq"), 1)
                for i in range(4):
                    mm(bank[4 + i], blk[:, :], prep[:, i * NT:(i + 1) * NT], True, True).then_inc(S("gn_var"), 1)
                pe.wait_ge(S("mixed"), 1)
                project_out(1, "even_out", yhy, three(oacc), NT)

            def odd_mixer():
                pe.wait_ge(S("u_lat"), KT * 5)
                pe.wait_ge(S("u_ctx"), KT * 5)
                i = 0
                for c, (kind, cols) in enumerate(OD_CHUNKS):
                    n = first["odd_in", 4] + c
                    pe.wait_ge(S(f"slot{n % R}"), arrival[n])
                    w = slot(n)[:, 0:KT * cols].rearrange("p (k n) -> p k n", k=KT)
                    for j in range(1 if kind == "gd" else 4):
                        if i >= 8:
                            pe.wait_ge(S("z1_done"), i - 7)
                        for k in range(KT):
                            st, en = k == 0, k == KT - 1
                            if kind == "gd":
                                ins = mm(bank[i % 8][0:32], w[:, k, 0:32], uv[:, k], st, en)
                            elif kind == "v":
                                ins = mm(bank[i % 8], uv[:, k, j * P:(j + 1) * P], w[:, k], st, en)
                            elif kind == "k":
                                ins = mm(bank[i % 8], w[:, k, j * P:(j + 1) * P], uv[:, k], st, en)
                            else:
                                ins = mm(bank[i % 8][:, 0:SEG], w[:, k, j * P:(j + 1) * P], uv[:, k, SEG:NT], st, en)
                        ins.then_inc(S("z1_psum"), 1)
                        i += 1
                    pe.wait_ge(S("z1_psum"), i)
                    pe.sem_inc(S("slot_used"), 1)
                pe.wait_ge(S("z1_done"), OD_TILES)
                pe.wait_ge(S("ld_gla"), 48)
                for q in range(8):
                    mm(bank[q], gup[:, q // 4, (q % 4) * P:(q % 4 + 1) * P], ggd, True, True)\
                        .then_inc(S("lg_psum"), 1)
                pe.wait_ge(S("kout"), 1)
                for q in range(4):
                    for c in range(4):
                        ins = pe.transpose(bank[q][:, c * P:(c + 1) * P], kout[:, q // 2, c, (q % 2) * P:(q % 2 + 1) * P],
                                           ident[:, :])
                    ins.then_inc(S("ko_turned"), 1)
                pe.wait_ge(S("lat_in"), 1)
                for q in range(4):
                    for c in range(4):
                        ins = pe.transpose(bank[4 + q][:, c * P:(c + 1) * P], kh[:, q // 2, c, (q % 2) * P:(q % 2 + 1) * P],
                                           ident[:, :])
                    ins.then_inc(S("kh_turned"), 1)
                pe.wait_ge(S("kot"), 4)
                for d in range(2):
                    for c in range(4):
                        for b in range(2):
                            ins = mm(bank[2 * d + c // 2][:, (c % 2) * HV:(c % 2 + 1) * HV],
                                     kot[:, d, b, c * P:(c + 1) * P], gvt[:, b, c * HV:(c + 1) * HV], b == 0, b == 1)
                ins.then_inc(S("gs_mm"), 1)
                pe.wait_ge(S("kht"), 4)
                for d in range(2):
                    for b in range(2):
                        for c in range(4):
                            ins = mm(bank[4 + 2 * d + b][:, c * P:(c + 1) * P], kh[:, d, c, b * P:(b + 1) * P],
                                     qh[:, d, c, b * P:(b + 1) * P], True, True)
                        ins.then_inc(S("sc_mm"), 1)
                pe.wait_ge(S("pm"), 4)
                for n in range(3):
                    pe.wait_ge(S("gst"), n + 1)
                    for d in range(2):
                        ch = XCHUNK(d, n)
                        lo = 64 * (ch % 2)
                        for c in range(4):
                            ins = mm(bank[4 * ((n + 1) % 2) + 2 * d + c // 2][:, (c % 2) * HV:(c % 2 + 1) * HV],
                                     kht[lo:lo + 64, d, ch // 2, c * P:(c + 1) * P],
                                     gvt[lo:lo + 64, 2 + ch // 2, c * HV:(c + 1) * HV], True, True)
                    ins.then_inc(S("gs_mm"), 1)
                pe.wait_ge(S("gst"), 4)
                for vt_ in range(8):
                    c, at = vt_ // 2, vt_ * P
                    for ch in range(4):
                        b = ch // 2
                        dst = bank[vt_ // 2][:, (vt_ % 2) * SEG + 64 * ch:(vt_ % 2) * SEG + 64 * ch + 64]
                        off = 64 * (ch % 2)
                        for d in range(2):
                            mm(dst, gvt[:, 2 + b, at:at + P], pm[:, d, b, c, off:off + 64], d == 0, False)
                            ins = mm(dst, gst[:, d, ch if d == 0 else 3 - ch, c, (vt_ % 2) * P:(vt_ % 2 + 1) * P],
                                     qh[:, d, c, 64 * ch:64 * ch + 64], False, d == 1)
                    if vt_ % 2:
                        ins.then_inc(S("go_mm"), 1)
                pe.wait_ge(S("go_sq"), 1)
                for c in range(4):
                    for i_ in range(2):
                        ins = mm(bank[c // 2][:, (c % 2) * SEG:(c % 2 + 1) * SEG], ones[:, :], sq2[:, 2 * c + i_],
                                 i_ == 0, i_ == 1)
                    if c % 2:
                        ins.then_inc(S("go_sum"), 1)
                pe.wait_ge(S("mixed"), 2)
                project_out(4, "odd_out", go, go[:, 4:8], SEG)

            for g in range(SUBS):
                if g == 1:
                    even_mixer()
                elif g == 4:
                    odd_mixer()
                else:
                    ffn(g)
                norm(g)
            pe.wait_ge(S("h_ready"), KT * (SUBS + 1))
            for b in range(2):
                for q in range(2):
                    for c in range(4):
                        k = 4 * q + c
                        ins = pe.transpose(bank[2 * b + q][:, c * P:(c + 1) * P],
                                           hv[:, k, SEG + b * P:SEG + (b + 1) * P], ident[:, :])
                    ins.then_inc(S("out_turned"), 1)

        @block.vector
        def _(ve):
            v = Count()

            for i, val in enumerate((LN_EPS, GLA_EPS, GN_EPS, 1.0)):
                ve.memset(eps[:, i:i + 1], val).then_inc(S("ve_steps"), v.step())
            ve.wait_ge(S("ve_steps"), v.n)
            ve.wait_ge(S("par_turned"), 1)
            for i, n in enumerate((120, 120, 125)):
                ve.tensor_copy(par[:, i * P:i * P + n], bank[0][:, i * P:i * P + n]).then_inc(S("ve_steps"), v.step())
            ve.wait_ge(S("ve_steps"), v.n)
            ve.tensor_copy(cfv[:, 0:12, 0:3].rearrange("p i j -> p j i"),
                                 par[:, PAR["conv_w"]:PAR["conv_w"] + 36].rearrange("p (j i) -> p j i", j=3)).then_inc(S("ve_steps"), v.step())
            ve.tensor_copy(cfv[:, 0:12, 3], par[:, PAR["conv_b"]:PAR["conv_b"] + 12]).then_inc(S("ve_steps"), v.step())
            mu = par[:, PAR["mu"]:PAR["mu"] + 15]
            ve.tensor_scalar(cfv[:, 12:27, 0], mu, 0.5, None, ALU.mult).then_inc(S("ve_steps"), v.step())
            ve.tensor_scalar(cfv[:, 12:27, 2], mu, 0.5, None, ALU.mult).then_inc(S("ve_steps"), v.step())
            ve.tensor_scalar(cfv[:, 12:27, 1], mu, -1.0, 1.0, ALU.mult, ALU.add).then_inc(S("ve_steps"), v.step())
            ve.memset(cfv[:, 12:27, 3], 0.0).then_inc(S("ve_steps"), v.step())
            ve.wait_ge(S("ve_steps"), v.n)
            ve.sem_inc(S("par_done"), 1)
            ve.sem_inc(S("pairs_free"), 1)
            ve.sem_inc(S("pairs_free"), 1)
            ve.wait_ge(S("silu_c"), 1)
            sc2 = sc[:, :].rearrange("p (k s) -> p k s", s=2)
            ve.tensor_copy(sc2[:, :, 1], sgc[:, 0:8]).then_inc(S("ve_steps"), v.step())
            ve.tensor_copy(sc2[:, :, 0], sgc[:, 8:16]).then_inc(S("ve_steps"), v.step())
            ve.wait_ge(S("ve_steps"), v.n)
            ve.sem_inc(S("sc_ready"), 1)

            for i in range(2):
                ve.wait_ge(S("filt_mm"), i + 1)
                if i:
                    ve.wait_ge(S("sin_done"), 1)
                ve.tensor_scalar(pre, bank[3 + i][0:HY_FO, 0:SEG], hyp[0:HY_FO, 2 * i:2 * i + 1],
                                       hyp[0:HY_FO, 2 * i + 1:2 * i + 2], ALU.add, ALU.mult).then_inc(S("ve_steps"), v.step())
                ve.wait_ge(S("ve_steps"), v.n)
                ve.tensor_scalar(turns, pre, 1 / TWO_PI, MAGIC, ALU.mult, ALU.add).then_inc(S("ve_steps"), v.step())
                ve.wait_ge(S("ve_steps"), v.n)
                ve.tensor_scalar(turns, turns, MAGIC, None, ALU.subtract).then_inc(S("ve_steps"), v.step())
                ve.wait_ge(S("ve_steps"), v.n)
                for part in (PI_A, PI_B, PI_C):
                    ve.scalar_tensor_tensor(out=pre, in0=turns, scalar=-part, in1=pre, op0=ALU.mult,
                                                  op1=ALU.add).then_inc(S("ve_steps"), v.step())
                    ve.wait_ge(S("ve_steps"), v.n)
                ve.tensor_scalar(pre, pre, 3.1415925, -3.1415925, ALU.min, ALU.max).then_inc(S("sin_arg"), 1)
            ve.sem_inc(S("taps_free"), 1)
            for o in range(2):
                ve.wait_ge(S("filt_taps"), o + 1)
                for dr in range(2):
                    for a in range(2):
                        ve.tensor_tensor(taps[:, dr, a], bank[4 + 2 * dr + a], win[:, a], ALU.mult).then_inc(S("ve_steps"), v.step())
                ve.wait_ge(S("ve_steps"), v.n)
                ve.memset(taps[0:1, 1, 0], 0.0).then_inc(S("ve_steps"), v.step())
                ve.tensor_tensor(taps[0:1, 0, 0], taps[0:1, 0, 0], skip_row[:, o], ALU.add).then_inc(S("ve_steps"), v.step())
                ve.wait_ge(S("ve_steps"), v.n)
                ve.tensor_tensor(tap_m, taps[:, 0], taps[:, 1], ALU.subtract).then_inc(S("ve_steps"), v.step())
                ve.wait_ge(S("ve_steps"), v.n)
                ve.tensor_tensor(taps[:, 0], taps[:, 0], taps[:, 1], ALU.add).then_inc(S("taps"), 1)
                ve.wait_ge(S("filt_dft"), o + 1)
                if o == 0:
                    ve.wait_ge(S("kf_done"), 6)
                    ve.sem_inc(S("taps_free"), 1)

            def modulation(g):
                ve.wait_ge(S("slot_used"), first["ada", g] + 6)
                m = modv[:, 24 * (g % 2):24 * (g % 2) + 24]
                at = PAR[f"ada_b{g // 3}"] + 24 * (g % 3)
                ve.tensor_tensor(m, bank[2][:, 0:48].rearrange("p (b s) -> p b s", s=2),
                                       par[:, at:at + 24].unsqueeze(2).to_broadcast([P, 24, 2]), ALU.add).then_inc(S("ve_steps"), v.step())
                ve.wait_ge(S("ve_steps"), v.n)
                ve.tensor_scalar(m[:, 8:16], m[:, 8:16], 1.0, None, ALU.add).then_inc(S("ve_steps"), v.step())
                ve.wait_ge(S("ve_steps"), v.n)
                ve.tensor_scalar(m[:, 16:24], m[:, 16:24], 1.0 if g % 3 == 1 else 0.5, None, ALU.mult)\
                    .then_inc(S("mods"), 1)

            def u_lat(g):
                ve.wait_ge(S("mods"), g + 1)
                for k in range(KT):
                    ve.wait_ge(S("h_ready"), KT * g + k + 1)
                    ve.tensor_scalar(us[:, k, 1], hs[:, k, 1], modv[:, 24 * (g % 2) + 8 + k, 1:2],
                                     modv[:, 24 * (g % 2) + k, 1:2], ALU.mult, ALU.add).then_inc(S("u_lat"), 1)
                ve.wait_ge(S("u_lat"), KT * (g + 1))
                ve.tensor_scalar(hs[:, :, 1], hs[:, :, 1], ALPHA, None, ALU.mult).then_inc(S("ve_steps"), v.step())

            def ffn_gate(g):
                f = (0, 2, 3, 5).index(g)
                TN = NT if g < 5 else SEG

                with ve.Fori(0, FT // 2) as c:
                    for jf in range(2):
                        ve.wait_ge(S("silu"), c * 2 + (FT * f + jf + 1))
                        ve.tensor_tensor(big[:, bass.ds(c * (2 * NT) + jf * NT, TN)],
                                         bank[2 * jf + 1][:, 0:TN], tmp[:, jf * NT:jf * NT + TN], ALU.mult)\
                            .then_inc(S("pairs_free"), 1)

            def norm(g):
                T0, TN = (0, NT) if g < 4 else (SEG, SEG)
                ve.wait_ge(S("ve_steps"), v.n)
                if g < 4:
                    ve.wait_ge(S("scaled_ctx"), g + 1)
                for k in range(KT):
                    ve.wait_ge(S("y_done"), KT * g + k + 1)
                    for s in segments(g):
                        lo = s * SEG if g < 4 else 0
                        ve.scalar_tensor_tensor(out=hs[:, k, s], in0=bank[k][:, lo:lo + SEG],
                                                scalar=modv[:, 24 * (g % 2) + 16 + k, s:s + 1], in1=hs[:, k, s],
                                                op0=ALU.mult, op1=ALU.add).then_inc(S("resid"), 1)
                ve.wait_ge(S("resid"), resid_base[g + 1])
                ve.wait_ge(S("mean"), g + 1)
                for k in range(KT):
                    ve.tensor_tensor(hv[:, k, T0:NT], hv[:, k, T0:NT], bank[0][:, 0:TN], ALU.subtract)\
                        .then_inc(S("centred"), 1)
                ve.wait_ge(S("centred"), KT * (g + 1))
                ve.wait_ge(S("std"), g + 1)
                ve.reciprocal(rs[:, 0:TN], rs[:, 0:TN]).then_inc(S("ve_steps"), v.step())
                ve.wait_ge(S("ve_steps"), v.n)
                for k in range(KT):
                    ve.tensor_tensor(uv[:, k, T0:NT], hv[:, k, T0:NT], rs[:, 0:TN], ALU.mult)\
                        .then_inc(S("normed"), 1)
                if g + 1 < SUBS:
                    modulation(g + 1)

            def even_mixer():
                for i in range(ZT):
                    ve.wait_ge(S("z_main"), i + 1)
                    z = bank[i % 8].rearrange("p (s t) -> p s t", s=2)
                    o = bigt[:, i].rearrange("p (s t) -> p s t", s=2)
                    ve.scalar_tensor_tensor(out=o[:, :, 1:SEG], in0=z[:, :, 0:SEG - 1], scalar=cfv[:, i, 0:1],
                                                  in1=o[:, :, 1:SEG], op0=ALU.mult, op1=ALU.add).then_inc(S("ve_steps"), v.step())
                    ve.wait_ge(S("ve_steps"), v.n)
                    ve.scalar_tensor_tensor(out=o[:, :, 0:SEG - 1], in0=z[:, :, 1:SEG], scalar=cfv[:, i, 2:3],
                                            in1=o[:, :, 0:SEG - 1], op0=ALU.mult, op1=ALU.add)\
                        .then_inc(S("z_done"), 1)
                for o in range(2):
                    for s in range(2):
                        ve.wait_ge(S("hy_f"), 2 * o + s + 1)
                        if o == 0 and s == 0:
                            ve.wait_ge(S("vtok"), 8)
                        else:
                            ve.wait_ge(S("hy_mul"), 2 * o + s)
                        for i in range(2):
                            re, im = bank[4 * s + i], bank[4 * s + 2 + i]
                            kre, kim, kre2 = kf[:, o, i], kf[:, o, 2 + i], kf[:, o, 4 if i == 0 else i]
                            ve.tensor_tensor(ft[0], re, kre, ALU.mult).then_inc(S("ve_steps"), v.step())
                            ve.tensor_tensor(ft[1], im, kim, ALU.mult).then_inc(S("ve_steps"), v.step())
                            ve.wait_ge(S("ve_steps"), v.n)
                            ve.tensor_tensor(yf[:, s, i], ft[0], ft[1], ALU.subtract).then_inc(S("ve_steps"), v.step())
                            ve.wait_ge(S("ve_steps"), v.n)
                            ve.tensor_tensor(ft[0], re, kim, ALU.mult).then_inc(S("ve_steps"), v.step())
                            ve.tensor_tensor(ft[1], im, kre2, ALU.mult).then_inc(S("ve_steps"), v.step())
                            ve.wait_ge(S("ve_steps"), v.n)
                            ins = ve.tensor_tensor(yf[:, s, 2 + i], ft[0], ft[1], ALU.add)
                            if i == 0:
                                ins.then_inc(S("ve_steps"), v.step())
                                ve.wait_ge(S("ve_steps"), v.n)
                        ins.then_inc(S("hy_mul"), 1)
                    for s in range(2):
                        ve.wait_ge(S("hy_i"), 2 * o + s + 1)
                        for a in range(2):
                            if o == 0:
                                ve.tensor_tensor(vtok[:, 2 * s + a], bank[4 * s + a], x1tok[:, 2 * s + a], ALU.mult)\
                                    .then_inc(S("hy_y1"), 1)
                            else:
                                ve.tensor_tensor(yhy[:, 2 * a:2 * a + 2, s * SEG:(s + 1) * SEG],
                                                 bank[4 * s + a].rearrange("p (c t) -> p c t", c=2),
                                                 bigt[:, 8 + 2 * a:10 + 2 * a, s * SEG:(s + 1) * SEG], ALU.mult)\
                                    .then_inc(S("hy_done"), 1)
                tile_of = lambda ap, c: ap[:, c * NT:(c + 1) * NT]
                ve.wait_ge(S("hy_done"), 4)
                for c in range(CT):
                    ve.tensor_scalar(tile_of(kk, c), tile_of(zk, c), col("k_k", c), None, ALU.mult).then_inc(S("ve_steps"), v.step())
                ve.wait_ge(S("ve_steps"), v.n)
                ve.sem_inc(S("kk_raw"), 1)
                ve.wait_ge(S("kk_norm"), 4)
                ve.tensor_scalar(prep2, prep2, 1e-12, None, ALU.max).then_inc(S("ve_steps"), v.step())
                ve.wait_ge(S("ve_steps"), v.n)
                ve.reciprocal(prep2, prep2).then_inc(S("ve_steps"), v.step())
                ve.wait_ge(S("ve_steps"), v.n)
                ve.tensor_tensor(kk, kk, prep2, ALU.mult).then_inc(S("ve_steps"), v.step())
                ve.wait_ge(S("ve_steps"), v.n)
                ve.wait_ge(S("lora_out"), 20)
                ve.tensor_tensor(prep, aa[0], aa[1], ALU.add).then_inc(S("ve_steps"), v.step())
                ve.tensor_scalar(small[:, 20:24], par[:, PAR["k_a"]:PAR["k_a"] + 4], -1.0, 1.0, ALU.mult, ALU.add).then_inc(S("ve_steps"), v.step())
                ve.wait_ge(S("ve_steps"), v.n)
                ve.tensor_scalar(small[:, 24:28], small[:, 20:24], 2.0, None, ALU.mult).then_inc(S("ve_steps"), v.step())
                ve.wait_ge(S("ve_steps"), v.n)
                for c in range(CT):
                    ve.tensor_scalar(tile_of(prep, c), tile_of(prep, c), col("k_a", c), small[:, 24 + c:25 + c],
                                           ALU.mult, ALU.add).then_inc(S("ve_steps"), v.step())
                ve.wait_ge(S("ve_steps"), v.n)
                ve.tensor_tensor(prep, prep, zk, ALU.mult).then_inc(S("ve_steps"), v.step())
                ve.wait_ge(S("ve_steps"), v.n)
                for c in range(CT):
                    ve.scalar_tensor_tensor(out=tile_of(prep, c), in0=tile_of(prep, c), scalar=col("r_k", c),
                                                  in1=tile_of(zr, c), op0=ALU.mult, op1=ALU.mult).then_inc(S("ve_steps"), v.step())
                ve.wait_ge(S("ve_steps"), v.n)
                ve.sem_inc(S("bonus_in"), 1)
                for d in range(2):
                    for c in range(CT):
                        dst = tile_of(kd[0] if d == 0 else prep2, c)
                        ve.tensor_scalar(dst, tile_of(aa[d], c), col("k_a", c), small[:, 20 + c:21 + c],
                                               ALU.mult, ALU.add).then_inc(S("ve_steps"), v.step())
                ve.wait_ge(S("ve_steps"), v.n)
                ve.tensor_tensor(kd[0], kd[0], zk, ALU.mult).then_inc(S("ve_steps"), v.step())
                ve.wait_ge(S("ve_steps"), v.n)
                ve.tensor_tensor(zk, zk, prep2, ALU.mult).then_inc(S("ve_steps"), v.step())
                ve.tensor_tensor(aa[0], aa[0], kk, ALU.mult).then_inc(S("ve_steps"), v.step())
                ve.tensor_tensor(aa[1], aa[1], kk, ALU.mult).then_inc(S("ve_steps"), v.step())
                ve.wait_ge(S("v_turned"), 4)
                for c in range(CT):
                    ve.wait_ge(S("bonus_sum"), c + 1)
                    ve.tensor_tensor(tile_of(zv, c), bank[c], tile_of(zv, c), ALU.mult).then_inc(S("ve_steps"), v.step())
                ve.memset(extra[:, 8448:8960], 0.0).then_inc(S("ve_steps"), v.step())
                ve.wait_ge(S("ve_steps"), v.n)
                ve.sem_inc(S("prepared"), 1)
                ve.wait_ge(S("zeroed"), 1)
                chunk = lambda ap, ch: three(ap)[:, :, ch * P:(ch + 1) * P]
                for j in range(4):
                    for d in range(2):
                        ch = chunk_of(d, j)
                        sg = chunk(sgw[d], ch)
                        for c in range(CT):
                            ve.tensor_tensor_scan(cs[:, c], ones[:, :], sg[:, c], 0.0, ALU.mult, ALU.add).then_inc(S("ve_steps"), v.step())
                        ve.wait_ge(S("ve_steps"), v.n)
                        ve.tensor_tensor(ce, cs, sg, ALU.subtract).then_inc(S("ve_steps"), v.step())
                        ve.tensor_scalar(half[:, d], cs[:, :, P - 1], 0.5, None, ALU.mult).then_inc(S("ve_steps"), v.step())
                        ve.wait_ge(S("ve_steps"), v.n)
                        hb = half[:, d].unsqueeze(2).to_broadcast([P, CT, P])
                        ve.tensor_tensor(cs, cs, hb, ALU.subtract).then_inc(S("ve_steps"), v.step())
                        ve.tensor_tensor(ce, ce, hb, ALU.subtract).then_inc(S("expo"), 1)
                        ve.wait_ge(S("ve_steps"), v.n)
                        ve.wait_ge(S("exped"), 2 * j + d + 1)
                        ve.scalar_tensor_tensor(out=ar[:, d, :, 0], in0=chunk(kk, ch), scalar=-1.0,
                                                      in1=ar[:, d, :, 0], op0=ALU.mult, op1=ALU.mult).then_inc(S("ve_steps"), v.step())
                        ve.tensor_tensor(ar[:, d, :, 1], chunk(zr, ch), ar[:, d, :, 1], ALU.mult).then_inc(S("ve_steps"), v.step())
                        ve.tensor_tensor(bk[:, d, :, 1], chunk(kd[d], ch), bk[:, d, :, 0], ALU.mult).then_inc(S("ve_steps"), v.step())
                        ve.wait_ge(S("ve_steps"), v.n)
                        ve.tensor_tensor(bk[:, d, :, 0], chunk(aa[d], ch), bk[:, d, :, 0], ALU.mult).then_inc(S("ve_steps"), v.step())
                        ve.tensor_tensor(state[:, d], state[:, d], edec[:, d].unsqueeze(2).to_broadcast([P, CT, 64]),
                                         ALU.mult).then_inc(S("state_in"), 1)
                        ve.wait_ge(S("ve_steps"), v.n)
                        ve.sem_inc(S("slots"), 1)
                    ve.wait_ge(S("state_in"), 2 * (j + 1))
                    for hf in range(2):
                        gi = 2 * j + hf
                        for d in range(2):
                            mk = maskv[:, M_STRICT + 2 * d:M_STRICT + 2 * d + 2].rearrange("p m t -> p (m t)")\
                                .unsqueeze(1).to_broadcast([P, 2, 2 * P])
                            for hh in range(4):
                                ve.wait_ge(S("n_mm"), 8 * gi + 4 * d + hh + 1)
                                ve.copy_predicated(nm[:, d, hh].rearrange("p (b a) t -> p b (a t)", b=2), mk,
                                                   bank[4 * d + hh].rearrange("p (b t) -> p b t", b=2))\
                                    .then_inc(S("n_done"), 1)
                        for lv in range(LEVELS):
                            for d in range(2):
                                um, tm = (M_UP, M_LO) if d == 0 else (M_LO, M_UP)
                                mask = lambda m: maskv[:, m + lv].unsqueeze(1).to_broadcast([P, 4, P])
                                if lv == 0:
                                    ve.wait_ge(S("z_mm"), 2 * LEVELS * gi + d + 1)
                                    ve.wait_ge(S("tu_reset"), 2 * gi + d + 1)
                                    if d == 0:
                                        ve.wait_ge(S("n_done"), 8 * (gi + 1))
                                    tsrc = bank[d]
                                    usrc = nm[:, d, :, 0]
                                else:
                                    ve.wait_ge(S("d_mm"), 2 * (gi * (LEVELS - 1) + lv - 1) + d + 1)
                                    tsrc = bank[2 + d]
                                    usrc = bank[4 + d].rearrange("p (h t) -> p h t", h=4)
                                if lv < LEVELS - 1:
                                    ve.copy_predicated(tu[:, d, 0], mask(tm), tsrc.rearrange("p (h t) -> p h t", h=4))\
                                        .then_inc(S("tu"), 1)
                                    ve.copy_predicated(tu[:, d, 1], mask(um), usrc).then_inc(S("tu"), 1)
                                else:
                                    ve.copy_predicated(tu[:, d, 1], mask(um), usrc).then_inc(S("tu"), 2)
                        for d in range(2):
                            ve.wait_ge(S("sa_mm"), 2 * gi + d + 1)
                            ve.tensor_copy(xs[:, d, 1].rearrange("p h v -> p (h v)"), bank[4 + d][:, 0:256])\
                                .then_inc(S("sa"), 1)
                        ve.wait_ge(S("os_mm"), 2 * gi + 2)
                        for d in range(2):
                            ch = chunk_of(d, j)
                            for q in range(2):
                                lo = 64 * q
                                dst = three(oacc)[lo:lo + 64, 2 * hf:2 * hf + 2, ch * P:(ch + 1) * P]
                                src = bank[6 + q][lo:lo + 64, 2 * d * P:2 * (d + 1) * P]\
                                    .rearrange("p (c t) -> p c t", c=2)
                                if j % 2 == 0:
                                    ve.tensor_copy(dst, src).then_inc(S("o_add"), 1)
                                else:
                                    ve.tensor_tensor(dst, dst, src, ALU.add).then_inc(S("o_add"), 1)
                            st = state[:, d, 2 * hf:2 * hf + 2]
                            ve.tensor_tensor(st, st, bank[d][:, 0:128].rearrange("p (c v) -> p c v", c=2), ALU.add).then_inc(S("ve_steps"), v.step())
                            ve.wait_ge(S("ve_steps"), v.n)
                            ve.tensor_tensor(st, st, edec[:, d, 2 * hf:2 * hf + 2].unsqueeze(2).to_broadcast([P, 2, 64]),
                                             ALU.mult).then_inc(S("state_new"), 1)
                    ve.wait_ge(S("state_new"), 4 * (j + 1))
                ve.wait_ge(S("o_add"), 32)
                for c in range(CT):
                    ve.wait_ge(S("gn_mean"), c + 1)
                    o = tile_of(oacc, c)
                    ve.scalar_tensor_tensor(out=o, in0=bank[c], scalar=-1 / 64.0, in1=o, op0=ALU.mult, op1=ALU.add)\
                        .then_inc(S("gn_centred"), 1)
                ve.wait_ge(S("gn_centred"), 4)
                ve.wait_ge(S("gn_std"), 4)
                ve.reciprocal(prep2, prep2).then_inc(S("ve_steps"), v.step())
                ve.wait_ge(S("ve_steps"), v.n)
                ve.tensor_tensor(oacc, oacc, prep2, ALU.mult).then_inc(S("ve_steps"), v.step())
                ve.wait_ge(S("ve_steps"), v.n)
                for c in range(CT):
                    ve.tensor_scalar(tile_of(oacc, c), tile_of(oacc, c), col("gn_g", c), col("gn_b", c),
                                           ALU.mult, ALU.add).then_inc(S("ve_steps"), v.step())
                ve.wait_ge(S("ve_steps"), v.n)
                ve.tensor_tensor(oacc, oacc, zv, ALU.add).then_inc(S("ve_steps"), v.step())
                ve.wait_ge(S("ve_steps"), v.n)
                ve.tensor_tensor(oacc, oacc, gate, ALU.mult).then_inc(S("ve_steps"), v.step())
                ve.wait_ge(S("ve_steps"), v.n)
                ve.sem_inc(S("mixed"), 1)
                ve.sem_inc(S("scratch_free"), 1)

            def odd_mixer():
                ve.wait_ge(S("z1_done"), OD_TILES)
                for q in range(8):
                    ve.wait_ge(S("lg_abs"), q + 1)
                    ve.tensor_scalar(gg[:, q // 4, q % 4], bank[q], col("gla_b", q), 0.0, ALU.add, ALU.min).then_inc(S("ve_steps"), v.step())
                ve.wait_ge(S("ve_steps"), v.n)
                ve.wait_ge(S("lg_ln"), 1)
                ggf = ring[:, 8192:12288]
                ve.tensor_tensor(ggf, ggf, extra[:, 0:4096], ALU.subtract).then_inc(S("ve_steps"), v.step())
                ve.wait_ge(S("ve_steps"), v.n)
                ve.wait_ge(S("ld_gla"), 48)
                for q in range(8):
                    ve.tensor_tensor_scan(gcs[:, q // 4, q % 4], greset, gg[:, q // 4, q % 4], 0.0, ALU.mult,
                                                ALU.add).then_inc(S("ve_steps"), v.step())
                ve.wait_ge(S("ve_steps"), v.n)
                tot = gcs[:, 0, :, SEG - 1].unsqueeze(2).to_broadcast([P, 4, SEG])
                ve.tensor_tensor(kout[:, 0], tot, gcs[:, 0, :, 0:SEG], ALU.subtract).then_inc(S("ve_steps"), v.step())
                ve.tensor_tensor(kout[:, 1], gcs[:, 1, :, 0:SEG], gg[:, 1, :, 0:SEG], ALU.subtract).then_inc(S("ve_steps"), v.step())
                ve.wait_ge(S("ve_steps"), v.n)
                ve.sem_inc(S("ctx_arg"), 1)
                for d in range(2):
                    ve.tensor_scalar(ghalf[:, d], gcs[:, d, :, SEG + 63:NT:64], 0.5, None, ALU.mult).then_inc(S("ve_steps"), v.step())
                ve.wait_ge(S("ve_steps"), v.n)
                for c in range(4):
                    hb = lambda d: ghalf[:, d, c].unsqueeze(2).to_broadcast([P, 4, 64])
                    cv = lambda ap: ap.rearrange("p (n t) -> p n t", n=4)
                    ve.tensor_tensor(cv(sq2[:, c]), cv(gcs[:, 0, c, SEG:NT]), hb(0), ALU.subtract).then_inc(S("ve_steps"), v.step())
                    ve.tensor_tensor(sq2[:, 4 + c], gcs[:, 1, c, SEG:NT], gg[:, 1, c, SEG:NT], ALU.subtract).then_inc(S("ve_steps"), v.step())
                    ve.wait_ge(S("ve_steps"), v.n)
                    ve.tensor_tensor(cv(sq2[:, 4 + c]), cv(sq2[:, 4 + c]), hb(1), ALU.subtract).then_inc(S("ve_steps"), v.step())
                ve.wait_ge(S("ve_steps"), v.n)
                ve.wait_ge(S("ctx_exp"), 1)
                ve.sem_inc(S("lat_arg"), 1)
                for d in range(2):
                    ve.tensor_tensor(kout[:, d], kout[:, d], gk[:, :, 0:SEG], ALU.mult).then_inc(S("ve_steps"), v.step())
                ve.wait_ge(S("ve_steps"), v.n)
                ve.sem_inc(S("kout"), 1)
                ve.wait_ge(S("lat_exp"), 1)
                for d in range(2):
                    ve.scalar_tensor_tensor(out=qh[:, d], in0=gq, scalar=HK ** -0.5, in1=qh[:, d],
                                                  op0=ALU.mult, op1=ALU.mult).then_inc(S("ve_steps"), v.step())
                    ve.tensor_tensor(kh[:, d], gk[:, :, SEG:NT], kh[:, d], ALU.mult).then_inc(S("ve_steps"), v.step())
                ve.wait_ge(S("ve_steps"), v.n)
                ve.sem_inc(S("lat_in"), 1)
                ve.wait_ge(S("pm_zero"), 1)
                eb = lambda d, n: gexp[:, d, :, XCHUNK(d, n)].unsqueeze(2).to_broadcast([P, 4, HV])
                ve.wait_ge(S("gs_mm"), 1)
                for d in range(2):
                    ins = ve.tensor_tensor(gst[:, d, 0], psum[:, 2 * d:2 * d + 2, :].rearrange("p b (c v) -> p (b c) v", c=2),
                                           eb(d, 0), ALU.mult)
                    if d == 0:
                        ins.then_inc(S("ve_steps"), v.step())
                ins.then_inc(S("gst"), 1)
                for d in range(2):
                    for b in range(2):
                        ve.wait_ge(S("sc_mm"), 2 * d + b + 1)
                        ve.copy_predicated(pm[:, d, b], maskv[:, M_GLA + d].unsqueeze(1).to_broadcast([P, 4, P]),
                                           bank[4 + 2 * d + b].rearrange("p (c t) -> p c t", c=4))\
                            .then_inc(S("pm"), 1)
                for n in range(3):
                    ve.wait_ge(S("gs_mm"), n + 2)
                    ve.wait_ge(S("gst"), n + 1)
                    b0 = 4 * ((n + 1) % 2)
                    for d in range(2):
                        nxt = gst[:, d, n + 1]
                        ve.tensor_tensor(nxt, psum[:, b0 + 2 * d:b0 + 2 * d + 2, :]
                                               .rearrange("p b (c v) -> p (b c) v", c=2), gst[:, d, n], ALU.add).then_inc(S("ve_steps"), v.step())
                        ve.wait_ge(S("ve_steps"), v.n)
                        ve.tensor_tensor(nxt, nxt, eb(d, n), ALU.mult).then_inc(S("ve_steps"), v.step())
                        ve.wait_ge(S("ve_steps"), v.n)
                        ins = ve.tensor_tensor(nxt, nxt, eb(d, n + 1), ALU.mult)
                        if d == 0:
                            ins.then_inc(S("ve_steps"), v.step())
                    ve.wait_ge(S("ve_steps"), v.n)
                    ins.then_inc(S("gst"), 1)
                for b in range(4):
                    ve.wait_ge(S("go_mm"), b + 1)
                    ve.tensor_copy(go[:, 2 * b:2 * b + 2].rearrange("p c t -> p (c t)"), bank[b])\
                        .then_inc(S("go_done"), 1)
                ve.wait_ge(S("go_done"), 4)
                ve.wait_ge(S("go_std"), 2)
                ve.reciprocal(grs.rearrange("p c t -> p (c t)"), grs.rearrange("p c t -> p (c t)")).then_inc(S("ve_steps"), v.step())
                ve.wait_ge(S("ve_steps"), v.n)
                g2 = go.rearrange("p (c a) t -> p c a t", a=2)
                for a in range(2):
                    ve.scalar_tensor_tensor(out=g2[:, :, a], in0=g2[:, :, a], scalar=col("norm_g", a),
                                                  in1=grs, op0=ALU.mult, op1=ALU.mult).then_inc(S("ve_steps"), v.step())
                ve.wait_ge(S("ve_steps"), v.n)
                ve.tensor_tensor(go, go, gog, ALU.mult).then_inc(S("ve_steps"), v.step())
                ve.wait_ge(S("ve_steps"), v.n)
                ve.sem_inc(S("mixed"), 1)
                ve.sem_inc(S("scratch_free"), 1)

            ve.wait_ge(S("ld_const"), 64)
            ve.tensor_copy(masks[:, :], u[:, 0:NMASK * P]).then_inc(S("ve_steps"), v.step())
            ve.wait_ge(S("ve_steps"), v.n)
            modulation(0)
            for g in range(SUBS):
                u_lat(g)
                if g == 1:
                    even_mixer()
                elif g == 4:
                    odd_mixer()
                else:
                    ffn_gate(g)
                norm(g)

        @block.gpsimd
        def _(pool):
            pool.wait_ge(S("hy_done"), 4)
            pool.wait_ge(S("lora_psum"), 20)
            pool.memset(ring[:, 6144:10240], 0.0).then_inc(S("nm_zero"), 1)
            pool.wait_ge(S("lora_psum"), 20)
            pool.wait_ge(S("ld_ident"), 16)
            for gi in range(8):
                for d in range(2):
                    if gi:
                        pool.wait_ge(S("sa_mm"), 2 * gi)
                    ins = pool.tensor_copy(tu[:, d].rearrange("p a h t -> p (a h) t"),
                                           ident[:, :].unsqueeze(1).to_broadcast([P, 8, P]))
                    ins.then_inc(S("tu_reset"), 1)
                if gi == 0:
                    pool.wait_ge(S("nm_zero"), 1)
                    pool.sem_inc(S("zeroed"), 1)
            pool.wait_ge(S("y_done"), KT * 4)
            pool.memset(extra[0:32, 4096:5120], 0.0).then_inc(S("gup_zero"), 1)
            pool.memset(big[:, 11776:13824], 0.0).then_inc(S("pm_zero"), 1)


OD_CHUNKS = [("k", 512), ("gd", 32), ("q", 512), ("v", 512), ("v", 512), ("og", 512), ("og", 512)]
OD_TILES = 25


def od_tile(i):
    if i < 4:
        return "k", i
    if i == 4:
        return "gd", 0
    if i < 9:
        return "q", i - 5
    if i < 17:
        return "v", i - 9
    return "og", i - 17


def kernel(**inputs):
    import concourse.bacc as bacc
    from concourse.bass_utils import run_bass_kernel_spmd as run

    nc = bacc.Bacc("TRN2", target_bir_lowering=False, num_devices=1)
    arrays, A, K = {}, {}, {}
    for name, value in inputs.items():
        arr = np.ascontiguousarray(value)
        arrays["in_" + name] = arr
        A[name] = nc.dram_tensor("in_" + name, arr.shape, mybir.dt.from_np(arr.dtype), kind="ExternalInput").ap()
    for name, arr in constants().items():
        arrays[name] = arr
        K[name] = nc.dram_tensor(name, arr.shape, mybir.dt.from_np(arr.dtype), kind="ExternalInput").ap()
    out = nc.dram_tensor("out", (1, SEG, D), F32, kind="ExternalOutput").ap()
    program(nc, A, K, out)
    r = run(nc, [arrays], core_ids=[0])
    return r.results[0]["out"]
```

```python
import math
from contextlib import ExitStack

import numpy as np
import concourse.bass as bass
from concourse import mybir

F32 = mybir.dt.float32
F32R = mybir.dt.float32r
U8 = mybir.dt.uint8
ALU = mybir.AluOpType
ACT = mybir.ActivationFunctionType

P = 128
D = 1024
KT = D // P
SEG = 256
NT = 2 * SEG
DEPTH = 2
F = 2816
FT = F // P
GRID_W = 64
ROWS = SEG // GRID_W
ALPHA = (2 * DEPTH) ** 0.25
LN_EPS = 1e-6
HW = 512
CT = HW // P
ZT = 27
HY_EMB, HY_FO = 33, 64
GN_EPS = 64e-5
GLA_EPS = 1e-5
GLA_N = 16.0
HK, HV = 128, 256
DECAY = math.exp(-0.5)

R = 2
HALF = 2048
FA = 12
SLOT = 4096
SUBS = 3 * DEPTH
ARENA = 45568
LEVELS = 7

PAR = {}


def _columns():
    at = 0
    for name, n in (("ada_b0", 72), ("ln_g", 48)):
        PAR[name] = at
        at += n
    at = P
    for name, n in (("ada_b1", 72), ("ln_b", 48)):
        PAR[name] = at
        at += n
    at = 2 * P
    for name, n in (("conv_w", 36), ("conv_b", 12), ("mu", 15), ("w0", 8), ("a0", 8), ("k_k", 4), ("k_a", 4),
                    ("r_k", 4), ("gn_g", 4), ("gn_b", 4), ("gla_b", 8), ("norm_g", 2), ("c", 8), ("c_ctx", 8)):
        PAR[name] = at
        at += n


_columns()

M_UP, M_LO, M_STRICT, M_GLA = 0, LEVELS, 2 * LEVELS, 2 * LEVELS + 4


def constants():
    i = np.arange(P)
    row, col = i[:, None], i[None, :]
    masks = []
    for lv in range(LEVELS):
        m = 1 << lv
        masks.append((row // (2 * m) == col // (2 * m)) & (row // m % 2 == 0) & (col // m % 2 == 1))
    masks += [m.T for m in masks]
    masks += [row < col, row <= col, row > col, row >= col]
    same = row // 64 == col // 64
    masks += [same & (row <= col), same & (row >= col)]
    t = np.arange(SEG)
    f = np.arange(SEG)
    w = 2 * np.pi * np.outer(t, f) / (2 * SEG)
    fwd = np.concatenate([np.cos(w), -np.sin(w)], 1)
    fwd[:, SEG] = np.cos(np.pi * t)
    s0 = -np.sin(w[:, :P])
    inv = np.concatenate([2 * np.cos(w.T), -2 * np.sin(w.T)], 0) / (2 * SEG)
    inv[0] = 1 / (2 * SEG)
    inv[SEG] = np.cos(np.pi * t) / (2 * SEG)
    tt = np.linspace(0.0, 1.0, SEG)[:, None]
    bands = (HY_EMB - 1) // 2
    fr = np.linspace(1e-4, bands - 1, bands)[None, :]
    ww = 2 * np.pi * t[:, None] / SEG
    z = np.concatenate([tt, np.cos(fr * ww), -np.sin(fr * ww)], 1)
    deltas = np.linspace(math.log(1e-2) / 1.5, math.log(1e-2) / 0.3, HW)
    win = np.exp(-tt * np.abs(deltas))
    reset = np.ones((P, NT))
    reset[:, [0, 256, 320, 384, 448]] = 0
    tile = lambda a, n: a.reshape(n, P, -1).transpose(1, 0, 2).reshape(P, -1)
    blk = np.kron(np.eye(2), np.ones((64, 64)))
    f32 = lambda a: np.ascontiguousarray(a, dtype=np.float32)
    return {
        "k_ident": f32(np.eye(P)), "k_mean": f32(np.full((P, P), 1 / D)), "k_blk": f32(blk),
        "k_ones": f32(np.ones((P, P))),
        "k_masks": f32(np.stack(masks, 1).reshape(P, -1)),
        "k_dft": f32(tile(fwd, 2)), "k_sin0": f32(tile(s0, 2)), "k_idft": f32(tile(inv, 4)),
        "k_zT": f32(z.T), "k_win": f32(tile(win, 2)), "k_reset": f32(reset),
    }


NMASK = 2 * LEVELS + 6


def _round_bits(x, bits):
    e = math.floor(math.log2(abs(x)))
    s = 2.0 ** (bits - 1 - e)
    return math.floor(x * s) / s


TWO_PI = 2 * math.pi
PI_A = _round_bits(TWO_PI, 10)
PI_B = _round_bits(TWO_PI - PI_A, 11)
PI_C = TWO_PI - PI_A - PI_B
MAGIC = 1.5 * 2.0 ** 23


def plan():
    items = []

    def add(phase, halves, each=16):
        items.extend((phase, n, each) for n in halves)

    add(("ada", 0), [0] * 6)
    for g in range(SUBS):
        if g % 3 != 1:
            add(("up_a", g), [2] * (FA // 2), 32)
            add(("down_a", g), [2] * (FA // 4))
            add(("up_b", g), [2] * ((FT - FA) // 2), 32)
            add(("down_b", g), [2, 2, 2])
        elif g == 1:
            add(("even_in", g), [2] * 7)
            add(("even_out", g), [2, 2])
        else:
            add(("odd_in", g), [2, 1, 2, 2, 2, 2, 2])
            add(("odd_out", g), [2, 2])
        if g + 1 < SUBS:
            add(("ada", g + 1), [0] * 6)
    first, half0, arrival, holder, slot_total = {}, {}, [], [], [0] * R
    ada = split = halves = 0
    done = []
    for n, (phase, hn, each) in enumerate(items):
        first.setdefault(phase, n)
        half0.setdefault(phase, halves)
        halves += hn
        slot_total[n % R] += each
        arrival.append(slot_total[n % R])
        if hn:
            split += 1
            done.append(("chunk_split", split))
        else:
            ada += 1
            done.append(("ada_used", ada))
        holder.append(done[n - R] if n >= R else None)
    return first, half0, arrival, holder


def program(nc, A, K, out):
    first, half0, arrival, holder = plan()
    with ExitStack() as ctx:
        def sb(name, n, dt=F32, parts=P):
            return ctx.enter_context(nc.sbuf_tensor(name, [parts, n], dt))

        h = sb("h", KT * NT)
        tmp = sb("tmp", 2 * NT)
        rs = sb("rs", NT)
        par = sb("par", 3 * P)
        masks = sb("masks", NMASK * P, U8)
        ident = sb("ident", P)
        mean_w = sb("mean_w", P)
        blk = sb("blk", P)
        ones = sb("ones", P)
        sc = sb("sc", 2 * KT)
        sgc = sb("sgc", 2 * KT)
        mods = sb("mods", 2 * 48)
        cf = sb("cf", ZT * 4)
        hyp = sb("hyp", 4)
        eps = sb("eps", 4)
        small = sb("small", 128)
        arena = sb("arena", ARENA)
        base = nc.sbuf_base - 4 * ARENA

        def rounded(name, at, n):
            return nc.alloc_sbuf_tensor_at(name, [P, n], F32R, offset=base + 4 * at)

        w_hi = rounded("w_hi", 8192, 2 * HALF)
        w_lo = rounded("w_lo", 12288, 2 * HALF)
        u_hi = rounded("u_hi", 16384, KT * NT)
        u_lo = rounded("u_lo", 20480, KT * NT)
        hid_hi = rounded("hid_hi", 24576, FA * NT)
        hid_lo = rounded("hid_lo", 30720, FA * NT)
        big = arena[:, 26624:40448]
        u = arena[:, 24576:28672]
        psum = ctx.enter_context(nc.psum_tensor("psum", [P, 8, 512], F32))

        hv = h[:, :].rearrange("p (k t) -> p k t", k=KT)
        uv = u.rearrange("p (k t) -> p k t", k=KT)
        uhv = u_hi[:, :].rearrange("p (k t) -> p k t", k=KT)
        ulv = u_lo[:, :].rearrange("p (k t) -> p k t", k=KT)
        uhf = u_hi[:, :].bitcast(F32).rearrange("p (k t) -> p k t", k=KT)
        hidh = hid_hi[:, :].rearrange("p (k t) -> p k t", t=NT)
        hidl = hid_lo[:, :].rearrange("p (k t) -> p k t", t=NT)
        hs = h[:, :].rearrange("p (k s t) -> p k s t", k=KT, s=2)
        us = u.rearrange("p (k s t) -> p k s t", k=KT, s=2)
        modv = mods[:, :].rearrange("p (b s) -> p b s", s=2)
        bank = [psum[:, b, :] for b in range(8)]
        bigt = big.rearrange("p (i t) -> p i t", t=NT)
        maskv = masks[:, :].rearrange("p (m t) -> p m t", t=P)
        cfv = cf[:, :].rearrange("p (i j) -> p i j", j=4)

        sems = {}

        def S(name):
            if name not in sems:
                sems[name] = ctx.enter_context(nc.semaphore(name))
            return sems[name]

        def col(name, i=0):
            return par[:, PAR[name] + i:PAR[name] + i + 1]

        def slot(n):
            return arena[:, (n % R) * SLOT:(n % R + 1) * SLOT]

        def split_hi(q):
            return w_hi[:, (q % 2) * HALF:(q % 2 + 1) * HALF]

        def split_lo(q):
            return w_lo[:, (q % 2) * HALF:(q % 2 + 1) * HALF]

        def ada_row(g):
            at = 11264 if g == 0 else 34816
            return arena[0:2, at:at + 3 * D]

        class Count:
            n = 0

            def step(self):
                self.n += 1
                return 1

        tok_in = big[:, 0:4096].rearrange("p (b d) -> p b d", b=4)
        stage = [big[:, 4096 + i * P:4096 + (i + 1) * P] for i in range(3)]
        w3 = big[0:HY_FO, 4608:6656]
        win = big[:, 6656:7680].rearrange("p (a c) -> p a c", a=2)
        taps = big[:, 7680:9728].rearrange("p (d a c) -> p d a c", d=2, a=2)
        tap_m = big[:, 9728:10752].rearrange("p (a c) -> p a c", a=2)
        zT = big[0:HY_EMB, 10752:11008]
        fw1 = big[0:HY_EMB, 11008:11072]
        fw2 = big[0:HY_FO, 11072:11136]
        pre = big[0:HY_FO, 11136:11392]
        turns = big[0:HY_FO, 11392:11648]
        h1 = big[0:HY_FO, 11648:11904]
        h2 = big[0:HY_FO, 11904:12160]
        skip_row = big[0:1, 12160:13184].rearrange("p (o c) -> p o c", o=2)
        yhy = arena[:, 24576:26624].rearrange("p (c t) -> p c t", t=NT)
        kf = arena[:, 40448:45568].rearrange("p (o i c) -> p o i c", o=2, i=5)
        dft = arena[:, 16384:17408].rearrange("p (a f) -> p a f", a=2)
        sin0 = arena[:, 18432:18688].rearrange("p (a f) -> p a f", a=2)
        idft = arena[:, 17408:18432].rearrange("p (f t) -> p f t", f=4)
        vtok = arena[:, 0:2048].rearrange("p (b c) -> p b c", b=4)
        x1tok = arena[:, 2048:4096].rearrange("p (b c) -> p b c", b=4)
        yf = arena[:, 4096:8192].rearrange("p (s i c) -> p s i c", s=2, i=4)
        ft = [arena[:, 8192 + i * 512:8704 + i * 512] for i in range(2)]
        w_up = arena[:, 9216:9728]
        a_up = arena[:, 9728:10240]
        g_up = arena[:, 10240:10752]
        prep = arena[:, 0:2048]
        prep2 = arena[:, 2048:4096]
        three = lambda ap: ap.rearrange("p (c t) -> p c t", t=NT)
        zr, zk, zv = big[:, 12 * NT:16 * NT], big[:, 16 * NT:20 * NT], big[:, 20 * NT:24 * NT]
        sgw = [big[:, 0:2048], big[:, 2048:4096]]
        aa = [big[:, 4096:6144], arena[:, 20480:22528]]
        kd = [arena[:, 22528:24576], zk]
        oacc = arena[:, 40448:42496]
        state = arena[:, 42496:43008].rearrange("p (d c v) -> p d c v", d=2, c=CT)
        gate, kk = arena[:, 43008:45056], arena[:, 16384:18432]
        ar = arena[:, 0:4096].rearrange("p (d c e a t) -> p d c e a t", d=2, c=CT, e=2, a=2)
        bk = arena[:, 18432:20480].rearrange("p (d c a t) -> p d c a t", d=2, c=CT, a=2)
        bkt = arena[:, 4096:6144].rearrange("p (d a c) -> p d a c", d=2, a=2)
        nm = arena[:, 6144:10240].rearrange("p (d h a t) -> p d h a t", d=2, h=4, a=4)
        tu = arena[:, 10240:12288].rearrange("p (d a h t) -> p d a h t", d=2, a=2, h=4)
        zs = arena[:, 12288:13312].rearrange("p (d h t) -> p d h t", d=2, h=4)
        xs = arena[:, 13312:14336].rearrange("p (d a h v) -> p d a h v", d=2, a=2, h=4)
        vt = arena[:, 14336:16384].rearrange("p (b c) -> p b c", b=4)
        decays = [[arena[:, 38912 + 512 * i:39424 + 512 * i].rearrange("p (c t) -> p c t", c=CT) for i in range(3)],
                  [at.rearrange("p (c t) -> p c t", c=CT) for at in (tmp[:, 0:512], tmp[:, 512:1024],
                                                                      arena[:, 45056:45568])]]
        half = small[:, 64:96].rearrange("p (d c n) -> p d c n", d=2, c=CT)
        edec = small[:, 96:128].rearrange("p (d c n) -> p d c n", d=2, c=CT)

        def blocks(ap, m, which):
            lead = " ".join("abc"[:len(ap.shape) - 2])
            return ap.rearrange(f"p {lead} (g s m) -> p {lead} g s m", s=2, m=m)[(slice(None),) * (len(ap.shape)) + (which,)]

        def packed(ap, m):
            return ap.rearrange("p (g m) -> p g m", m=m)

        gq = big[:, 0:1024].rearrange("p (c t) -> p c t", c=4)
        gk = big[:, 1024:3072].rearrange("p (c t) -> p c t", c=4)
        gvt = big[:, 3072:7168].rearrange("p (b c) -> p b c", b=4)
        gog = big[:, 7168:9216].rearrange("p (c t) -> p c t", c=8)
        ggd = big[0:32, 9216:9728]
        kout = big[:, 9728:11776].rearrange("p (d c t) -> p d c t", d=2, c=4)
        go = big[:, 9728:11776].rearrange("p (c t) -> p c t", c=8)
        pm = big[:, 11776:13824].rearrange("p (d b h t) -> p d b h t", d=2, b=2, h=4)
        gcs = arena[:, 16384:20480].rearrange("p (d c t) -> p d c t", d=2, c=4)
        gup = arena[0:32, 40448:41472].rearrange("p (d c) -> p d c", d=2)
        greset = arena[:, 41472:41984]
        grs = arena[:, 41984:43008].rearrange("p (c t) -> p c t", c=4)
        sq2 = arena[:, 43008:45056].rearrange("p (c t) -> p c t", c=8)
        gg = arena[:, 8192:12288].rearrange("p (d c t) -> p d c t", d=2, c=4)
        gst = arena[:, 0:8192].rearrange("p (d n c v) -> p d n c v", d=2, n=4, c=4)
        qh = arena[:, 8192:10240].rearrange("p (d c t) -> p d c t", d=2, c=4)
        kh = arena[:, 10240:12288].rearrange("p (d c t) -> p d c t", d=2, c=4)
        kht = arena[:, 12288:14336].rearrange("p (d b c) -> p d b c", d=2, b=2)
        kot = arena[:, 14336:16384].rearrange("p (d b c) -> p d b c", d=2, b=2)
        ghalf = small[:, 0:32].rearrange("p (d c n) -> p d c n", d=2, c=4)
        gexp = small[:, 32:64].rearrange("p (d c n) -> p d c n", d=2, c=4)

        def half_src(phase, g, q, tiles):
            if phase == "odd_in" and q == 2:
                return slot(first[phase, g] + 1)[:, 0:KT * P]
            qq = q + 1 if phase == "odd_in" and q > 2 else q
            s_ = slot(first[phase, g] + qq // 2)
            if phase.startswith("up"):
                return s_.rearrange("p (a k f) -> p a k f", a=2, k=KT)[:, :, :, (qq % 2) * P:(qq % 2 + 1) * P]
            if phase.startswith("down"):
                m = min(4, tiles - 4 * (qq // 2)) // 2
                return s_[:, (qq % 2) * m * D:(qq % 2 + 1) * m * D]
            cols = 384 if phase == "even_in" and qq >= 12 else 512
            v_ = s_[:, 0:KT * cols].rearrange("p (k n) -> p k n", k=KT)
            return v_[:, :, (qq % 2) * 256:min(cols, (qq % 2 + 1) * 256)]

        def half_shape(buf, src):
            if len(src.shape) == 2:
                return buf[:, 0:src.shape[1]]
            if len(src.shape) == 3:
                k, n = src.shape[1:]
                return buf[:, 0:k * n].rearrange("p (k n) -> p k n", k=k)
            a_, k, n = src.shape[1:]
            return buf[:, 0:a_ * k * n].rearrange("p (a k n) -> p a k n", a=a_, k=k)

        def chunk_of(d, j):
            return j if d == 0 else j ^ 1

        def n_bank(d, cc, q):
            return (2, 3, 4, 5)[2 * cc + q] if d == 0 else (0, 1, 6, 7)[2 * cc + q]

        XCHUNK = lambda d, n: n if d == 0 else 3 - n

        def segments(g):
            return (0, 1) if g < 4 else (1,)

        resid_base = [0]
        for g in range(SUBS):
            resid_base.append(resid_base[-1] + KT * len(segments(g)))

        U_BASE = [KT * (g + (g > 1) + (g > 4)) for g in range(SUBS)]
        FFN = (0, 2, 3, 5)

        block = ctx.enter_context(nc.Block())

        @block.sync
        def _(sp):
            def free(n):
                if holder[n]:
                    sp.wait_ge(S(holder[n][0]), holder[n][1])

            def load_ada(g):
                w = A["ada_w"][g // 3].rearrange("(k p) n -> p k n", p=P)
                for c in range(6):
                    n = first["ada", g] + c
                    free(n)
                    at = 3 * D * (g % 3) + 512 * c
                    sp.dma_start(slot(n).rearrange("p (k n) -> p k n", k=KT),
                                 w[:, :, at:at + 512]).then_inc(S(f"slot{n % R}"), 16)

            def load_up(phase, g, c0, chunks):
                l, i = g // 3, (g % 3) // 2
                wg = A["ffn_wg"][l, i].rearrange("(k p) f -> p k f", p=P)
                wu = A["ffn_wu"][l, i].rearrange("(k p) f -> p k f", p=P)
                n0 = first[phase, g]

                def pair(n, c, gone, value):
                    dst = slot(n).rearrange("p (a k f) -> p a k f", a=2, k=KT)
                    sp.wait_ge(S(gone), value)
                    sp.dma_start(dst[:, 0], wg[:, :, bass.ds(c * 256, 256)]).then_inc(S(f"slot{n % R}"), 16)
                    sp.dma_start(dst[:, 1], wu[:, :, bass.ds(c * 256, 256)]).then_inc(S(f"slot{n % R}"), 16)

                for c in range(R):
                    pair(n0 + c, c0 + c, *holder[n0 + c])
                loops = (chunks - R) // R
                with sp.Fori(0, loops) as it:
                    for r in range(R, 2 * R):
                        pair(n0 + r, it * R + (c0 + r), "chunk_split", it * R + holder[n0 + r][1])
                for c in range(R + loops * R, chunks):
                    pair(n0 + c, c0 + c, *holder[n0 + c])

            def load_down(phase, g, k0, k1):
                wd = A["ffn_wd"][g // 3, (g % 3) // 2].rearrange("(k p) d -> p k d", p=P)
                for c, k in enumerate(range(k0, k1, 4)):
                    n = first[phase, g] + c
                    m = min(4, k1 - k)
                    free(n)
                    sp.dma_start(slot(n)[:, 0:m * D].rearrange("p (k d) -> p k d", k=m),
                                 wd[:, k:k + m, :]).then_inc(S(f"slot{n % R}"), 16)

            def load_cols(phase, g, w, blocks):
                v = w.rearrange("(k p) n -> p k n", p=P)
                for c, (at, m) in enumerate(blocks):
                    n = first[phase, g] + c
                    free(n)
                    sp.dma_start(slot(n)[:, 0:KT * m].rearrange("p (k n) -> p k n", k=KT),
                                 v[:, :, at:at + m]).then_inc(S(f"slot{n % R}"), 16)

            load_ada(0)
            for g in range(SUBS):
                if g == 1:
                    load_cols("even_in", g, A["ev_w_in"][0], [(512 * c, min(512, ZT * P - 512 * c)) for c in range(7)])
                    sp.wait_ge(S("scratch_free"), 1)
                    load_cols("even_out", g, A["ev_w_out"][0], [(0, 512), (512, 512)])
                elif g == 4:
                    load_cols("odd_in", g, A["od_w_in"][0],
                              [(512, 512), (2048, 128), (0, 512), (1024, 512), (1536, 512), (2080, 512), (2592, 512)])
                    sp.wait_ge(S("scratch_free"), 2)
                    load_cols("odd_out", g, A["od_w_out"][0], [(0, 512), (512, 512)])
                else:
                    load_up("up_a", g, 0, FA // 2)
                    load_down("down_a", g, 0, FA)
                    load_up("up_b", g, FA // 2, (FT - FA) // 2)
                    load_down("down_b", g, FA, FT)
                if g + 1 < SUBS:
                    load_ada(g + 1)
            sp.wait_ge(S("rows_out"), 4)
            rows = out[0].rearrange("(r c) d -> r c d", r=ROWS)
            o_sb = big[:, 0:2048].rearrange("p (b d) -> p b d", b=2)
            for b in range(2):
                for r in range(ROWS):
                    sp.dma_start(rows[r, 32 * b:32 * b + 32, :], o_sb[r:P:ROWS, b, :]).then_inc(S("stored"), 16)
            sp.wait_ge(S("stored"), 16 * 8)

        @block.scalar
        def _(act):
            def load(name, dst, src):
                act.dma_start(dst, src).then_inc(S(name), 16)

            load("ld_ident", ident[:, :], K["k_ident"])
            l0 = [("ada_b", 0, 72, A["ada_b"][0:1].rearrange("l (t p) -> (l t) p", p=P), 0),
                  ("ln_g", 72, 48, A["ln_g"].rearrange("l i (t p) -> (l i t) p", p=P), 0),
                  ("ada_b", 0, 72, A["ada_b"][1:2].rearrange("l (t p) -> (l t) p", p=P), 1),
                  ("ln_b", 72, 48, A["ln_b"].rearrange("l i (t p) -> (l i t) p", p=P), 1)]
            for _, at, n, src, s in l0:
                load("ld_par", stage[s][at:at + n, :], src)
            third = [("conv_w", 36, A["hy_conv_w"].rearrange("e j (t p) -> (e j t) p", p=P)),
                     ("conv_b", 12, A["hy_conv_b"].rearrange("e (t p) -> (e t) p", p=P)),
                     ("mu", 15, A["rw_mu"].rearrange("e (t p) -> (e t) p", p=P)),
                     ("w0", 8, A["rw_w0"].rearrange("e d (t p) -> (e d t) p", p=P)),
                     ("a0", 8, A["rw_a0"].rearrange("e d (t p) -> (e d t) p", p=P)),
                     ("k_k", 4, A["rw_k_k"].rearrange("e (t p) -> (e t) p", p=P)),
                     ("k_a", 4, A["rw_k_a"].rearrange("e (t p) -> (e t) p", p=P)),
                     ("r_k", 4, A["rw_r_k"].rearrange("e (t a) n -> (e t) (a n)", a=2)),
                     ("gn_g", 4, A["rw_gn_g"].rearrange("e (t p) -> (e t) p", p=P)),
                     ("gn_b", 4, A["rw_gn_b"].rearrange("e (t p) -> (e t) p", p=P)),
                     ("gla_b", 8, A["gla_g_b"].rearrange("e d (t p) -> (e d t) p", p=P)),
                     ("norm_g", 2, A["gla_norm_g"].rearrange("e (t p) -> (e t) p", p=P)),
                     ("c", 8, A["c"].rearrange("e (t p) -> (e t) p", p=P)),
                     ("c_ctx", 8, A["c_ctx"].rearrange("(t p) -> t p", p=P))]
            for name, n, src in third:
                at = PAR[name] - 2 * P
                load("ld_par", stage[2][at:at + n, :], src)
            for b in range(4):
                src = A["ctx"] if b < 2 else A["x"]
                load("ld_tok", tok_in[:, b, :], src[0, (b % 2) * P:(b % 2 + 1) * P, :])
            load("ld_filt", zT, K["k_zT"])
            load("ld_filt", fw1, A["hy_f_w1"][0])
            load("ld_filt", fw2, A["hy_f_w2"][0])
            for i, name in enumerate(("hy_f_b1", "hy_f_freq1", "hy_f_b2", "hy_f_freq2")):
                load("ld_filt", hyp[0:HY_FO, i:i + 1], A[name].rearrange("e n -> n e"))
            load("ld_filt", w3, A["hy_f_w3"][0])
            load("ld_filt", big[:, 6656:7680], K["k_win"])
            load("ld_filt", skip_row, A["hy_skip"].rearrange("e o c -> e o c"))
            load("ld_filt", arena[:, 16384:17408], K["k_dft"])
            load("ld_filt", arena[:, 18432:18688], K["k_sin0"])
            load("ld_const", mean_w[:, :], K["k_mean"])
            load("ld_const", blk[:, :], K["k_blk"])
            load("ld_const", ones[:, :], K["k_ones"])
            load("ld_const", arena[:, 8192:8192 + NMASK * P], K["k_masks"])

            act.wait_ge(S("par_done"), 1)
            act.activation(sgc[:, :], par[:, PAR["c"]:PAR["c"] + 16], ACT.Silu).then_inc(S("silu_c"), 1)
            for k in range(KT):
                act.wait_ge(S("tok_turned"), k + 1)
                act.activation(hv[:, k], bank[(k + 1) % 8], ACT.Copy).then_inc(S("h_ready"), 1)

            def ada_out(g, c):
                act.wait_ge(S("ada_used"), 6 * g + c + 1)
                act.activation(ada_row(g)[:, 512 * c:512 * c + 512], bank[2 + c % 2][0:2], ACT.Copy)\
                   .then_inc(S("ada_row"), 1)

            act.wait_ge(S("sin_arg"), 1)
            act.activation(h1, pre, ACT.Sin).then_inc(S("sin_done"), 1)
            for c in range(2):
                ada_out(0, c)
            act.wait_ge(S("sin_arg"), 2)
            act.activation(h2, pre, ACT.Sin).then_inc(S("sin_done"), 1)
            for c in range(2, 6):
                ada_out(0, c)
            for o in range(2):
                act.wait_ge(S("filt_dft"), o + 1)
                for i, b in ((0, 0), (1, 1), (2, 3), (3, 4), (4, 0)):
                    act.activation(kf[:, o, i], bank[b], ACT.Copy).then_inc(S("kf_done"), 1)
                act.wait_ge(S("kf_done"), 6 * o + 5)
                act.activation(kf[0:1, o, 4], bank[5][0:1], ACT.Copy).then_inc(S("kf_done"), 1)

            def hi(phase, g, q, src):
                n, hq = first[phase, g] + q // 2, half0[phase, g] + q
                if phase == "odd_in" and q > 2:
                    n = first[phase, g] + (q + 1) // 2
                act.wait_ge(S(f"slot{n % R}"), arrival[n])
                if hq >= 2:
                    act.wait_ge(S("split_used"), hq - 1)
                if g == 0 and q < 2:
                    act.wait_ge(S("mods"), 1)
                act.activation(half_shape(split_hi(hq), src), src, ACT.Copy).then_inc(S("hi_done"), 1)

            def u_round(g):
                T0 = 0 if g < 5 else SEG
                for k in range(KT):
                    act.wait_ge(S("u_lat"), KT * g + k + 1)
                    if g < 5:
                        act.wait_ge(S("u_ctx"), KT * g + k + 1)
                    act.activation(uhv[:, k, T0:NT], uv[:, k, T0:NT], ACT.Copy).then_inc(S("u_hi"), 1)

            def ffn_silu(g):
                f = FFN.index(g)
                TN = NT if g < 5 else SEG

                def silu(t):
                    jf = t % 2
                    act.wait_ge(S("gu_ready"), FT * f + t + 1)
                    if FT * f + t >= 2:
                        act.wait_ge(S("hid"), FT * f + t - 1)
                    act.activation(tmp[:, jf * NT:jf * NT + TN], bank[2 * jf][:, 0:TN], ACT.Silu)\
                       .then_inc(S("silu"), 1)

                for up, down, t0, t1 in (("up_a", "down_a", 0, FA), ("up_b", "down_b", FA, FT)):
                    halves = [(up, q) for q in range(t1 - t0)]
                    halves += [(down, q) for q in range(2 * -(-(t1 - t0) // 4))]
                    for at, (phase, q) in enumerate(halves):
                        if at >= 2 and at - 2 < t1 - t0:
                            silu(t0 + at - 2)
                        hi(phase, g, q, half_src(phase, g, q, t1 - t0))

            def norm(g):
                T0, TN = (0, NT) if g < 4 else (SEG, SEG)

                for k in range(KT):
                    if k == 2 and g + 1 < SUBS:
                        ada_out(g + 1, 0)
                        ada_out(g + 1, 1)
                    act.wait_ge(S("centred"), KT * g + k + 1)
                    if KT * g + k - 1 > 0:
                        act.wait_ge(S("sq_used"), KT * g + k - 1)
                    act.activation(tmp[:, (k % 2) * NT:(k % 2) * NT + TN], hv[:, k, T0:NT], ACT.Square)\
                       .then_inc(S("sq"), 1)
                act.wait_ge(S("sq_used"), KT * (g + 1))
                act.activation(rs[:, 0:TN], bank[1][:, 0:TN], ACT.Sqrt, bias=eps[:, 0:1]).then_inc(S("std"), 1)
                for k in range(KT):
                    if k == 4 and g + 1 < SUBS:
                        ada_out(g + 1, 2)
                    act.wait_ge(S("normed"), KT * g + k + 1)
                    sg, sb_ = col("ln_g", 8 * g + k), col("ln_b", 8 * g + k)
                    if g == 2:
                        act.activation(hs[:, k, 0], us[:, k, 0], ACT.Identity, scale=sg, bias=sb_)
                        act.activation(hs[:, k, 1].rearrange("p (c r) -> p r c", r=ROWS),
                                       us[:, k, 1].rearrange("p (r c) -> p r c", r=ROWS),
                                       ACT.Identity, scale=sg, bias=sb_).then_inc(S("h_ready"), 1)
                    else:
                        act.activation(hv[:, k, T0:NT], uv[:, k, T0:NT], ACT.Identity, scale=sg, bias=sb_)\
                           .then_inc(S("h_ready"), 1)
                if g + 1 < SUBS:
                    for c in range(3, 6):
                        ada_out(g + 1, c)

            def out_hi(g, left, right, TN):
                for k in range(KT):
                    if g == 1 and k == 0:
                        act.wait_ge(S("state_new"), 16)
                    if k == 4:
                        act.wait_ge(S("mixed"), 1 if g == 1 else 2)
                    src = left[:, k] if k < 4 else right[:, k - 4]
                    act.activation(uhv[:, k, 0:TN], src[:, 0:TN], ACT.Copy).then_inc(S("u_hi"), 1)

            def even_mixer():
                for i in range(ZT):
                    if i == 0:
                        for q in range(2):
                            hi("even_in", 1, q, half_src("even_in", 1, q, 0))
                    elif i % 2 == 0 and i // 2 + 1 < 14:
                        hi("even_in", 1, i // 2 + 1, half_src("even_in", 1, i // 2 + 1, 0))
                    act.wait_ge(S("z_psum"), i + 1)
                    act.activation(bigt[:, i], bank[i % 8], ACT.Identity, scale=cfv[:, i, 1:2], bias=cfv[:, i, 3:4])\
                       .then_inc(S("z_main"), 1)
                act.wait_ge(S("z_done"), ZT)
                load("ld_dft", dft.rearrange("p a f -> p (a f)"), K["k_dft"])
                load("ld_dft", idft.rearrange("p f t -> p (f t)"), K["k_idft"])
                load("ld_lora", w_up, A["rw_w_up"].rearrange("e d l n -> (e d l) n"))
                load("ld_lora", a_up, A["rw_a_up"].rearrange("e d l n -> (e d l) n"))
                load("ld_lora", g_up, A["rw_g_up"][0])
                act.activation(bigt[:, 24], bigt[:, 24], ACT.Tanh).then_inc(S("lora_in"), 1)
                act.activation(bigt[:, 26], bigt[:, 26], ACT.Sigmoid).then_inc(S("lora_in"), 1)
                for b in range(4):
                    act.wait_ge(S("hy_turned"), 2 * b + 1)
                    act.activation(vtok[:, b], bank[2 * b], ACT.Copy).then_inc(S("vtok"), 1)
                    act.wait_ge(S("hy_turned"), 2 * b + 2)
                    act.activation(x1tok[:, b], bank[2 * b + 1], ACT.Copy).then_inc(S("vtok"), 1)
                act.wait_ge(S("hy_done"), 4)
                for q in range(20):
                    act.wait_ge(S("lora_psum"), q + 1)
                    if q < 8:
                        act.activation(sgw[q // 4][:, (q % 4) * NT:(q % 4 + 1) * NT], bank[q % 8], ACT.Sigmoid,
                                       bias=col("w0", q)).then_inc(S("lora_out"), 1)
                    elif q < 16:
                        e = q - 8
                        act.activation(aa[e // 4][:, (e % 4) * NT:(e % 4 + 1) * NT], bank[q % 8], ACT.Sigmoid,
                                       bias=col("a0", e)).then_inc(S("lora_out"), 1)
                    else:
                        e = q - 16
                        act.activation(gate[:, e * NT:(e + 1) * NT], bank[q % 8], ACT.Copy)\
                           .then_inc(S("lora_out"), 1)
                act.wait_ge(S("kk_raw"), 1)
                act.activation(prep, kk, ACT.Square).then_inc(S("kk_sq"), 1)
                for i in range(4):
                    act.wait_ge(S("kk_sum"), i + 1)
                    act.activation(prep2[:, i * NT:(i + 1) * NT], bank[i], ACT.Sqrt).then_inc(S("kk_norm"), 1)
                for b in range(4):
                    act.wait_ge(S("v_turned"), b + 1)
                    act.activation(vt[:, b], bank[4 + b], ACT.Copy).then_inc(S("vt"), 1)
                def decays_of(j):
                    for d in range(2):
                        if j:
                            act.wait_ge(S("slots"), 2 * j + d - 1)
                            act.wait_ge(S("slots_r"), 2 * j + d - 1)
                        ch = chunk_of(d, j)
                        cs = three(sgw[d])[:, :, ch * P:(ch + 1) * P]
                        hf_ = half[:, d, :, ch:ch + 1]
                        recv, read, key = decays[d]
                        if d == 0:
                            act.activation(recv[:, :, 1:P], cs[:, :, 0:P - 1], ACT.Exp, scale=-DECAY)
                            act.activation(recv[:, :, 0:1], hf_, ACT.Exp, scale=DECAY)
                            act.activation(read, cs, ACT.Exp, scale=-DECAY)
                            act.activation(key, cs, ACT.Exp, scale=DECAY).then_inc(S("exped"), 1)
                        else:
                            act.activation(recv, cs, ACT.Exp, scale=DECAY)
                            act.activation(read[:, :, 1:P], cs[:, :, 0:P - 1], ACT.Exp, scale=DECAY)
                            act.activation(read[:, :, 0:1], hf_, ACT.Exp, scale=-DECAY)
                            act.activation(key[:, :, 1:P], cs[:, :, 0:P - 1], ACT.Exp, scale=-DECAY)
                            act.activation(key[:, :, 0:1], hf_, ACT.Exp, scale=DECAY).then_inc(S("exped"), 1)

                act.wait_ge(S("sums"), 1)
                act.activation(small[:, 96:128], small[:, 64:96], ACT.Exp, scale=-DECAY).then_inc(S("edec"), 1)
                decays_of(0)
                for j in range(4):
                    for hf in range(2):
                        gi = 2 * j + hf
                        if hf == 0 and j < 3:
                            decays_of(j + 1)
                        for lv in range(1, LEVELS):
                            m = 1 << lv
                            for d in range(2):
                                act.wait_ge(S("z_mm"), 2 * (LEVELS * gi + lv) + d + 1)
                                act.activation(blocks(zs[:, d].rearrange("p h t -> p (h t)"), m, d),
                                               packed(bank[d][:, 0:2 * P], m), ACT.Copy).then_inc(S("zs"), 1)
                            if hf == 0 and lv in (2, 4):
                                d = lv // 2 - 1
                                for q in range(2):
                                    act.wait_ge(S("bk_turned"), 4 * j + 2 * d + q + 1)
                                    act.activation(bkt[:, d, q], bank[6 + q], ACT.Copy).then_inc(S("bkt"), 1)
                        for d in range(2):
                            act.wait_ge(S("x_mm"), 2 * gi + d + 1)
                            for q in range(2):
                                dst = xs[:, d, 0].rearrange("p (c q) v -> p q c v", q=2)[:, q]
                                ins = act.activation(dst, bank[2 * d + q][:, 0:128].rearrange("p (c v) -> p c v", c=2),
                                                     ACT.Copy)
                            ins.then_inc(S("xs"), 1)
                act.wait_ge(S("gn_centred"), 4)
                act.activation(prep, oacc, ACT.Square).then_inc(S("gn_sq"), 1)
                for i in range(4):
                    act.wait_ge(S("gn_var"), i + 1)
                    act.activation(prep2[:, i * NT:(i + 1) * NT], bank[4 + i], ACT.Sqrt, scale=1 / 64.0,
                                   bias=eps[:, 2:3]).then_inc(S("gn_std"), 1)
                out_hi(1, yhy, three(oacc), NT)
                for q in range(4):
                    hi("even_out", 1, q, half_src("even_out", 1, q, 0))

            def odd_mixer():
                act.wait_ge(S("gup_zero"), 1)
                load("ld_gla", gup[0:16, 0, :], A["gla_g_up"][0, 0])
                load("ld_gla", gup[16:32, 1, :], A["gla_g_up"][0, 1])
                load("ld_gla", greset, K["k_reset"])
                for q in range(2):
                    hi("odd_in", 4, q, half_src("odd_in", 4, q, 0))
                for i, (q, kind, j) in enumerate(OD_TILES):
                    if i and q > OD_TILES[i - 1][0] and q + 1 < OD_HALVES:
                        hi("odd_in", 4, q + 1, half_src("odd_in", 4, q + 1, 0))
                    act.wait_ge(S("z1_psum"), i + 1)
                    if kind == "k":
                        ins = act.activation(gk[:, j], bank[i % 8], ACT.Copy)
                    elif kind == "gd":
                        ins = act.activation(ggd, bank[i % 8][0:32], ACT.Copy)
                    elif kind == "q":
                        ins = act.activation(gq[:, j], bank[i % 8][:, 0:SEG], ACT.Copy)
                    elif kind == "v":
                        ins = act.activation(gvt[:, j % 4, (j // 4) * SEG:(j // 4 + 1) * SEG], bank[i % 8][:, 0:SEG],
                                             ACT.Copy)
                    else:
                        ins = act.activation(gog[:, j], bank[i % 8][:, 0:SEG], ACT.Silu)
                    ins.then_inc(S("z1_done"), 1)
                for q in range(8):
                    d, c = q // 4, q % 4
                    act.wait_ge(S("lg_psum"), q + 1)
                    act.activation(gcs[:, d, c], bank[q], ACT.Abs, bias=col("gla_b", q)).then_inc(S("lg_abs"), 1)
                act.wait_ge(S("lg_abs"), 8)
                act.activation(arena[:, 16384:20480], arena[:, 16384:20480], ACT.Exp, scale=-1.0).then_inc(S("lg_exp"), 1)
                act.wait_ge(S("lg_exp"), 1)
                act.activation(arena[:, 16384:20480], arena[:, 16384:20480], ACT.Ln, bias=eps[:, 3:4]).then_inc(S("lg_ln"), 1)
                act.wait_ge(S("ctx_arg"), 1)
                act.activation(kout.rearrange("p d c t -> p (d c t)"), kout.rearrange("p d c t -> p (d c t)"),
                               ACT.Exp, scale=1 / GLA_N).then_inc(S("ctx_exp"), 1)
                act.wait_ge(S("lat_arg"), 1)
                fl = lambda x: x.rearrange("p c t -> p (c t)")
                act.activation(gexp.rearrange("p d c n -> p (d c n)"), ghalf.rearrange("p d c n -> p (d c n)"),
                               ACT.Exp, scale=1 / GLA_N)
                act.activation(fl(qh[:, 0]), fl(sq2[:, 0:4]), ACT.Exp, scale=1 / GLA_N)
                act.activation(fl(kh[:, 0]), fl(sq2[:, 0:4]), ACT.Exp, scale=-1 / GLA_N)
                act.activation(fl(qh[:, 1]), fl(sq2[:, 4:8]), ACT.Exp, scale=-1 / GLA_N)
                act.activation(fl(kh[:, 1]), fl(sq2[:, 4:8]), ACT.Exp, scale=1 / GLA_N).then_inc(S("lat_exp"), 1)
                for q in range(4):
                    act.wait_ge(S("ko_turned"), q + 1)
                    act.activation(kot[:, q // 2, q % 2], bank[q], ACT.Copy).then_inc(S("kot"), 1)
                for q in range(4):
                    act.wait_ge(S("kh_turned"), q + 1)
                    act.activation(kht[:, q // 2, q % 2], bank[4 + q], ACT.Copy).then_inc(S("kht"), 1)
                act.wait_ge(S("go_done"), 4)
                act.activation(sq2.rearrange("p c t -> p (c t)"), go.rearrange("p c t -> p (c t)"), ACT.Square)\
                   .then_inc(S("go_sq"), 1)
                for i in range(2):
                    act.wait_ge(S("go_sum"), i + 1)
                    act.activation(grs[:, 2 * i:2 * i + 2].rearrange("p c t -> p (c t)"), bank[i], ACT.Sqrt,
                                   scale=1.0 / HV, bias=eps[:, 1:2]).then_inc(S("go_std"), 1)
                act.wait_ge(S("mixed"), 2)
                out_hi(4, go, go[:, 4:8], SEG)
                for q in range(4):
                    hi("odd_out", 4, q, half_src("odd_out", 4, q, 0))

            for g in range(SUBS):
                u_round(g)
                if g == 1:
                    even_mixer()
                elif g == 4:
                    odd_mixer()
                else:
                    ffn_silu(g)
                norm(g)
            for i in range(4):
                act.wait_ge(S("out_turned"), i + 1)
                act.activation(big[:, i * 512:(i + 1) * 512], bank[i], ACT.Copy).then_inc(S("rows_out"), 1)

        @block.tensor
        def _(pe):
            def mm(dst, w, x, first_, last):
                return pe.matmul(dst, w, x, start=first_, stop=last, skip_group_check=True)

            pe.wait_ge(S("ld_ident"), 16)
            pe.wait_ge(S("ld_par"), 16 * 18)
            for i, n in enumerate((120, 120, 125)):
                ins = pe.transpose(bank[0][:, i * P:i * P + n], stage[i][0:n, :], ident[0:n, 0:n])
            ins.then_inc(S("par_turned"), 1)
            pe.wait_ge(S("ld_tok"), 64)
            for k in range(KT):
                if k == KT - 1:
                    pe.wait_ge(S("par_done"), 1)
                for b in range(4):
                    ins = pe.transpose(bank[(k + 1) % 8][:, b * P:(b + 1) * P], tok_in[:, b, k * P:(k + 1) * P],
                                       ident[:, :])
                ins.then_inc(S("tok_turned"), 1)

            def mm3(dst, wh, wl, xh, xl, first_, last):
                mm(dst, wh, xh, first_, False)
                mm(dst, wh, xl, False, False)
                return mm(dst, wl, xh, False, last)

            def ada(g, part):
                for c in part:
                    n = first["ada", g] + c
                    pe.wait_ge(S(f"slot{n % R}"), arrival[n])
                    if c >= 2:
                        pe.wait_ge(S("ada_row"), 6 * g + c - 1)
                    w = slot(n).rearrange("p (k n) -> p k n", k=KT)
                    for k in range(KT):
                        ins = mm(bank[2 + c % 2][0:2], sc[:, 2 * k:2 * k + 2], w[:, k], k == 0, k == KT - 1)
                    ins.then_inc(S("ada_used"), 1)

            def ada_turn(g):
                pe.wait_ge(S("ada_row"), 6 * (g + 1))
                for t in range(24):
                    ins = pe.transpose(bank[4][:, 2 * t:2 * t + 2], ada_row(g)[:, t * P:(t + 1) * P], ident[0:2, 0:2])
                ins.then_inc(S("ada_turned"), 1)

            def taps_of(o):
                pe.wait_ge(S("taps_free"), o + 1)
                for dr in range(2):
                    for a in range(2):
                        ins = mm(bank[4 + 2 * dr + a], h2[:, a * P:(a + 1) * P],
                                 w3[:, (2 * o + dr) * HW:(2 * o + dr + 1) * HW], True, True)
                ins.then_inc(S("filt_taps"), 1)

            def response_of(o):
                pe.wait_ge(S("taps"), o + 1)
                if o:
                    pe.wait_ge(S("kf_done"), 6 * o)
                for a in range(2):
                    st, en = a == 0, a == 1
                    mm(bank[0], dft[:, a, 0:P], taps[:, 0, a], st, en)
                    mm(bank[1], dft[:, a, P:2 * P], taps[:, 0, a], st, en)
                    mm(bank[3], sin0[:, a], tap_m[:, a], st, en)
                    mm(bank[4], dft[:, a, 3 * P:4 * P], tap_m[:, a], st, en)
                    ins = mm(bank[5][0:1], dft[:, a, 2 * P:2 * P + 1], taps[:, 0, a], st, en)
                ins.then_inc(S("filt_dft"), 1)

            pe.wait_ge(S("h_ready"), KT)
            pe.wait_ge(S("ld_filt"), 16 * 12)
            mm(bank[6][0:HY_FO, 0:SEG], fw1, zT, True, True).then_inc(S("filt_mm"), 1)
            pe.wait_ge(S("sc_ready"), 1)
            ada(0, (0, 1))
            pe.wait_ge(S("sin_done"), 1)
            mm(bank[7][0:HY_FO, 0:SEG], fw2, h1, True, True).then_inc(S("filt_mm"), 1)
            ada(0, (2, 3))
            pe.wait_ge(S("sin_done"), 2)
            ada(0, (4, 5))
            ada_turn(0)
            pe.wait_ge(S("mods"), 1)
            taps_of(0)
            response_of(0)
            taps_of(1)
            response_of(1)
            pe.wait_ge(S("ld_const"), 64)

            def ffn(g):
                f = FFN.index(g)
                T0, TN = (0, NT) if g < 5 else (SEG, SEG)
                pe.wait_ge(S("u_lo"), U_BASE[g] + KT)

                def up_half(par, buf, hq1, ft1):
                    pe.wait_ge(S("lo_done"), hq1)
                    pe.wait_ge(S("pairs_free"), ft1)
                    wh = split_hi(buf).rearrange("p (a k f) -> p a k f", a=2, k=KT)
                    wl = split_lo(buf).rearrange("p (a k f) -> p a k f", a=2, k=KT)
                    for a in range(2):
                        for k in range(KT):
                            ins = mm3(bank[2 * par + a][:, 0:TN], wh[:, a, k], wl[:, a, k], uhv[:, k, T0:NT],
                                      ulv[:, k, T0:NT], k == 0, k == KT - 1)
                    ins.then_inc(S("gu_ready"), 1)
                    pe.wait_ge(S("gu_ready"), ft1)
                    pe.sem_inc(S("split_used"), 1)

                for up, down, t0, t1 in (("up_a", "down_a", 0, FA), ("up_b", "down_b", FA, FT)):
                    with pe.Fori(0, (t1 - t0) // 2) as it:
                        for par in range(2):
                            up_half(par, half0[up, g] + par, it * 2 + (half0[up, g] + par + 1), it * 2 + (FT * f + t0 + par + 1))
                    pe.wait_ge(S("hid"), FT * f + t1)
                    if t0:
                        pe.wait_ge(S("y_part"), KT * (f + 1))
                    kt = t0
                    for q in range(2 * -(-(t1 - t0) // 4)):
                        m = min(4, t1 - t0 - 4 * (q // 2)) // 2
                        hq = half0[down, g] + q
                        pe.wait_ge(S("lo_done"), hq + 1)
                        wh = split_hi(hq)[:, 0:m * D].rearrange("p (k d) -> p k d", k=m)
                        wl = split_lo(hq)[:, 0:m * D].rearrange("p (k d) -> p k d", k=m)
                        for j in range(m):
                            for t in range(KT):
                                ins = mm3(bank[t][:, 0:TN], wh[:, j, t * P:(t + 1) * P], wl[:, j, t * P:(t + 1) * P],
                                          hidh[:, kt - t0, 0:TN], hidl[:, kt - t0, 0:TN], kt == t0, kt == t1 - 1)
                                if kt == t1 - 1:
                                    ins.then_inc(S("y_done" if t0 else "y_half"), 1)
                            kt += 1
                        if kt == t1:
                            pe.wait_ge(S("y_done" if t0 else "y_half"), KT * (g + 1) if t0 else KT * (f + 1))
                            pe.sem_inc(S("split_used"), 1)
                        else:
                            ins.then_inc(S("split_used"), 1)
                    if t0 == 0:
                        pe.wait_ge(S("y_part"), KT * f + 4)

            def norm(g):
                T0, TN = (0, NT) if g < 4 else (SEG, SEG)
                for k in range(KT):
                    pe.wait_ge(S("resid"), resid_base[g] + len(segments(g)) * (k + 1))
                    ins = mm(bank[0][:, 0:TN], mean_w[:, :], hv[:, k, T0:NT], k == 0, k == KT - 1)
                ins.then_inc(S("mean"), 1)
                if g + 1 < SUBS:
                    ada(g + 1, range(2))
                for k in range(KT):
                    pe.wait_ge(S("sq"), KT * g + k + 1)
                    mm(bank[1][:, 0:TN], mean_w[:, :], tmp[:, (k % 2) * NT:(k % 2) * NT + TN], k == 0,
                       k == KT - 1).then_inc(S("sq_used"), 1)
                if g + 1 < SUBS:
                    ada(g + 1, range(2, 6))
                    ada_turn(g + 1)

            def project_out(g, phase, TN):
                for q in range(4):
                    hq = half0[phase, g] + q
                    pe.wait_ge(S("lo_done"), hq + 1)
                    wh = split_hi(hq).rearrange("p (k n) -> p k n", k=KT)
                    wl = split_lo(hq).rearrange("p (k n) -> p k n", k=KT)
                    for j in range(2):
                        for k in range(KT):
                            if q == 0 and j == 0:
                                pe.wait_ge(S("u_lo"), U_BASE[g] + KT + k + 1)
                            ins = mm3(bank[2 * q + j][:, 0:TN], wh[:, k, j * P:(j + 1) * P],
                                      wl[:, k, j * P:(j + 1) * P], uhv[:, k, 0:TN], ulv[:, k, 0:TN],
                                      k == 0, k == KT - 1)
                        ins.then_inc(S("y_done"), 1)
                    pe.wait_ge(S("y_done"), KT * g + 2 * (q + 1))
                    pe.sem_inc(S("split_used"), 1)

            def even_mixer():
                pe.wait_ge(S("u_lo"), U_BASE[1] + KT)
                for q in range(14):
                    hq = half0["even_in", 1] + q
                    pe.wait_ge(S("lo_done"), hq + 1)
                    m = min(2, ZT - 2 * q)
                    wh = split_hi(hq)[:, 0:KT * m * P].rearrange("p (k n) -> p k n", k=KT)
                    wl = split_lo(hq)[:, 0:KT * m * P].rearrange("p (k n) -> p k n", k=KT)
                    for i in range(2 * q, 2 * q + m):
                        at = (i % 2) * P
                        if i >= 8:
                            pe.wait_ge(S("z_done"), i - 7)
                        for k in range(KT):
                            ins = mm3(bank[i % 8], wh[:, k, at:at + P], wl[:, k, at:at + P], uhv[:, k], ulv[:, k],
                                      k == 0, k == KT - 1)
                        ins.then_inc(S("z_psum"), 1)
                    pe.wait_ge(S("z_psum"), i + 1)
                    pe.sem_inc(S("split_used"), 1)
                pe.wait_ge(S("z_done"), ZT)
                for b in range(4):
                    for q in range(2):
                        for c in range(CT):
                            ins = pe.transpose(bank[2 * b + q][:, c * P:(c + 1) * P],
                                               bigt[:, 4 * q + c, b * P:(b + 1) * P], ident[:, :])
                        ins.then_inc(S("hy_turned"), 1)
                pe.wait_ge(S("ld_dft"), 32)
                pe.wait_ge(S("vtok"), 8)
                for o in range(2):
                    for s in range(2):
                        if o:
                            pe.wait_ge(S("hy_y1"), 2 * s + 2)
                        for i in range(4):
                            for a in range(2):
                                ins = mm(bank[4 * s + i], dft[:, a, i * P:(i + 1) * P], vtok[:, 2 * s + a],
                                         a == 0, a == 1)
                        ins.then_inc(S("hy_f"), 1)
                    for s in range(2):
                        pe.wait_ge(S("hy_mul"), 2 * o + s + 1)
                        if o == 0:
                            for a in range(2):
                                for i in range(4):
                                    ins = mm(bank[4 * s + a], idft[:, i, a * P:(a + 1) * P], yf[:, s, i],
                                             i == 0, i == 3)
                        else:
                            for c in range(CT):
                                for i in range(4):
                                    ins = mm(bank[4 * s + c // 2][:, (c % 2) * SEG:(c % 2 + 1) * SEG],
                                             yf[:, s, i, c * P:(c + 1) * P], idft[:, i], i == 0, i == 3)
                        ins.then_inc(S("hy_i"), 1)
                pe.wait_ge(S("hy_done"), 4)
                pe.wait_ge(S("lora_in"), 2)
                pe.wait_ge(S("ld_lora"), 48)
                for q in range(20):
                    if q >= 8:
                        pe.wait_ge(S("lora_out"), q - 7)
                    d, c = q // 4, q % 4
                    lo = 64 * (d % 2)
                    if q < 16:
                        w = (w_up if q < 8 else a_up)[lo:lo + 64, c * P:(c + 1) * P]
                        x = bigt[lo:lo + 64, 24 if q < 8 else 25]
                    else:
                        w, x = g_up[:, c * P:(c + 1) * P], bigt[:, 26]
                    mm(bank[q % 8], w, x, True, True).then_inc(S("lora_psum"), 1)
                pe.wait_ge(S("lora_out"), 20)
                pe.wait_ge(S("kk_sq"), 1)
                for i in range(4):
                    mm(bank[i], blk[:, :], prep[:, i * NT:(i + 1) * NT], True, True).then_inc(S("kk_sum"), 1)
                for b in range(4):
                    for c in range(CT):
                        ins = pe.transpose(bank[4 + b][:, c * P:(c + 1) * P], zv[:, c * NT + b * P:c * NT + (b + 1) * P],
                                           ident[:, :])
                    ins.then_inc(S("v_turned"), 1)
                pe.wait_ge(S("bonus_in"), 1)
                for i in range(4):
                    mm(bank[i], blk[:, :], prep[:, i * NT:(i + 1) * NT], True, True).then_inc(S("bonus_sum"), 1)
                pe.wait_ge(S("vt"), 4)
                pe.wait_ge(S("prepared"), 1)
                pe.wait_ge(S("zeroed"), 1)
                for j in range(4):
                    for hf in range(2):
                        gi = 2 * j + hf
                        for d in range(2):
                            if hf == 0:
                                pe.wait_ge(S("slots"), 2 * j + d + 1)
                                pe.wait_ge(S("slots_r"), 2 * j + d + 1)
                            if d and gi:
                                pe.wait_ge(S("o_add"), 4 * gi)
                                pe.wait_ge(S("state_new"), 2 * gi)
                            for cc in range(2):
                                for q in range(2):
                                    mm(bank[n_bank(d, cc, q)], bk[:, d, 2 * hf + cc, q],
                                       ar[:, d, 2 * hf + cc].rearrange("p e a t -> p (e a t)"), True, True)\
                                        .then_inc(S("n_mm"), 1)
                        for lv in range(LEVELS):
                            m = 1 << lv
                            for d in range(2):
                                if lv == 0:
                                    pe.wait_ge(S("n_done"), 8 * gi + 8)
                                else:
                                    pe.wait_ge(S("tu"), (2 * (gi * LEVELS + lv - 1) + d + 1) * 2)
                                for hh in range(4):
                                    ins = mm(packed(bank[d][:, hh * 64:(hh + 1) * 64], m), nm[:, d, hh, 0],
                                             blocks(ident[:, :] if lv == 0 else tu[:, d, 0, hh], m, d), True, True)
                                ins.then_inc(S("z_mm"), 1)
                            if lv == 0:
                                continue
                            for d in range(2):
                                pe.wait_ge(S("zs"), 2 * (gi * (LEVELS - 1) + lv - 1) + d + 1)
                                if lv < LEVELS - 1:
                                    for hh in range(4):
                                        mm(packed(bank[2 + d][:, hh * 64:(hh + 1) * 64], m), tu[:, d, 1, hh],
                                           blocks(zs[:, d, hh], m, d), True, True)
                                for hh in range(4):
                                    ins = mm(packed(bank[4 + d][:, hh * 64:(hh + 1) * 64], m), zs[:, d, hh],
                                             blocks(tu[:, d, 1, hh], m, 1 - d), True, True)
                                ins.then_inc(S("d_mm"), 1)
                            if hf == 0 and lv in (1, 3):
                                d = lv // 2
                                if d:
                                    pe.wait_ge(S("bkt"), 4 * j + 2)
                                for q in range(2):
                                    for c in range(CT):
                                        ins = pe.transpose(bank[6 + q][:, c * P:(c + 1) * P], bk[:, d, c, q],
                                                           ident[:, :])
                                    ins.then_inc(S("bk_turned"), 1)
                        vcol = lambda hh: (4 * hf + hh) * 64
                        for d in range(2):
                            pe.wait_ge(S("tu"), 2 * LEVELS * 2 * (gi + 1))
                            ch = chunk_of(d, j)
                            if hf == 0 and d == 0:
                                pe.wait_ge(S("state_in"), 2 * (j + 1))
                            for hh in range(4):
                                c = 2 * hf + hh // 2
                                dst = bank[2 * d + hh % 2][:, (hh // 2) * 64:(hh // 2 + 1) * 64]
                                mm(dst, ar[:, d, c, hh % 2, 0], state[:, d, c], True, False)
                                ins = mm(dst, nm[:, d, hh, 2], vt[:, ch, vcol(hh):vcol(hh) + 64], False, True)
                            ins.then_inc(S("x_mm"), 1)
                        for d in range(2):
                            pe.wait_ge(S("xs"), 2 * gi + d + 1)
                            for hh in range(4):
                                ins = mm(bank[4 + d][:, hh * 64:(hh + 1) * 64], tu[:, d, 1, hh], xs[:, d, 0, hh],
                                         True, True)
                            ins.then_inc(S("sa_mm"), 1)
                        pe.wait_ge(S("bkt"), 4 * (j + 1))
                        for d in range(2):
                            pe.wait_ge(S("sa"), 2 * gi + d + 1)
                            ch = chunk_of(d, j)
                            for hh in range(4):
                                c, lo = 2 * hf + hh // 2, 64 * (hh % 2)
                                v = vt[:, ch, vcol(hh):vcol(hh) + 64]
                                dst = bank[6 + hh % 2][lo:lo + 64, (2 * d + hh // 2) * P:(2 * d + hh // 2 + 1) * P]
                                mm(dst, xs[:, d, 1, hh], nm[:, d, hh, 1], True, False)
                                mm(dst, v, nm[:, d, hh, 3], False, False)
                                mm(dst, state[:, d, c], ar[:, d, c, hh % 2, 1], False, True)
                                dst = bank[d][lo:lo + 64, (hh // 2) * 64:(hh // 2 + 1) * 64]
                                mm(dst, bkt[:, d, 0, vcol(hh):vcol(hh) + 64], xs[:, d, 1, hh], True, False)
                                ins = mm(dst, bkt[:, d, 1, vcol(hh):vcol(hh) + 64], v, False, True)
                            ins.then_inc(S("os_mm"), 1)
                pe.wait_ge(S("o_add"), 32)
                pe.wait_ge(S("state_new"), 16)
                for i in range(4):
                    mm(bank[i], blk[:, :], oacc[:, i * NT:(i + 1) * NT], True, True).then_inc(S("gn_mean"), 1)
                pe.wait_ge(S("gn_sq"), 1)
                for i in range(4):
                    mm(bank[4 + i], blk[:, :], prep[:, i * NT:(i + 1) * NT], True, True).then_inc(S("gn_var"), 1)
                pe.wait_ge(S("mixed"), 1)
                project_out(1, "even_out", NT)

            def odd_mixer():
                pe.wait_ge(S("u_lo"), U_BASE[4] + KT)
                for i, (q, kind, j) in enumerate(OD_TILES):
                    hq = half0["odd_in", 4] + q
                    new, last = i == 0 or OD_TILES[i - 1][0] < q, i + 1 == len(OD_TILES) or OD_TILES[i + 1][0] > q
                    if new:
                        pe.wait_ge(S("lo_done"), hq + 1)
                    if i >= 8:
                        pe.wait_ge(S("z1_done"), i - 7)
                    cols = P if kind == "gd" else 2 * P
                    wh = split_hi(hq)[:, 0:KT * cols].rearrange("p (k n) -> p k n", k=KT)
                    wl = split_lo(hq)[:, 0:KT * cols].rearrange("p (k n) -> p k n", k=KT)
                    for k in range(KT):
                        st, en = k == 0, k == KT - 1
                        at = 0 if kind == "gd" else (j % 2) * P
                        w2 = wh[:, k, at:at + P], wl[:, k, at:at + P]
                        if kind == "v":
                            tok = slice((j % 4) * P, (j % 4 + 1) * P)
                            ins = mm3(bank[i % 8][:, 0:SEG], uhv[:, k, tok], ulv[:, k, tok], wh[:, k], wl[:, k], st, en)
                        elif kind in ("k", "gd"):
                            ins = mm3(bank[i % 8], *w2, uhv[:, k], ulv[:, k], st, en)
                        else:
                            ins = mm3(bank[i % 8][:, 0:SEG], *w2, uhv[:, k, SEG:NT], ulv[:, k, SEG:NT], st, en)
                    ins.then_inc(S("z1_psum"), 1)
                    if last:
                        pe.wait_ge(S("z1_psum"), i + 1)
                        pe.sem_inc(S("split_used"), 1)
                pe.wait_ge(S("z1_done"), len(OD_TILES))
                pe.wait_ge(S("ld_gla"), 48)
                for q in range(8):
                    mm(bank[q], gup[:, q // 4, (q % 4) * P:(q % 4 + 1) * P], ggd, True, True)\
                        .then_inc(S("lg_psum"), 1)
                pe.wait_ge(S("kout"), 1)
                for q in range(4):
                    for c in range(4):
                        ins = pe.transpose(bank[q][:, c * P:(c + 1) * P], kout[:, q // 2, c, (q % 2) * P:(q % 2 + 1) * P],
                                           ident[:, :])
                    ins.then_inc(S("ko_turned"), 1)
                pe.wait_ge(S("lat_in"), 1)
                for q in range(4):
                    for c in range(4):
                        ins = pe.transpose(bank[4 + q][:, c * P:(c + 1) * P], kh[:, q // 2, c, (q % 2) * P:(q % 2 + 1) * P],
                                           ident[:, :])
                    ins.then_inc(S("kh_turned"), 1)
                pe.wait_ge(S("kot"), 4)
                for d in range(2):
                    for c in range(4):
                        for b in range(2):
                            ins = mm(bank[2 * d + c // 2][:, (c % 2) * HV:(c % 2 + 1) * HV],
                                     kot[:, d, b, c * P:(c + 1) * P], gvt[:, b, c * HV:(c + 1) * HV], b == 0, b == 1)
                ins.then_inc(S("gs_mm"), 1)
                pe.wait_ge(S("kht"), 4)
                for d in range(2):
                    for b in range(2):
                        for c in range(4):
                            ins = mm(bank[4 + 2 * d + b][:, c * P:(c + 1) * P], kh[:, d, c, b * P:(b + 1) * P],
                                     qh[:, d, c, b * P:(b + 1) * P], True, True)
                        ins.then_inc(S("sc_mm"), 1)
                pe.wait_ge(S("pm"), 4)
                for n in range(3):
                    pe.wait_ge(S("gst"), n + 1)
                    for d in range(2):
                        ch = XCHUNK(d, n)
                        lo = 64 * (ch % 2)
                        for c in range(4):
                            ins = mm(bank[4 * ((n + 1) % 2) + 2 * d + c // 2][:, (c % 2) * HV:(c % 2 + 1) * HV],
                                     kht[lo:lo + 64, d, ch // 2, c * P:(c + 1) * P],
                                     gvt[lo:lo + 64, 2 + ch // 2, c * HV:(c + 1) * HV], True, True)
                    ins.then_inc(S("gs_mm"), 1)
                pe.wait_ge(S("gst"), 4)
                for vt_ in range(8):
                    c, at = vt_ // 2, vt_ * P
                    for ch in range(4):
                        b = ch // 2
                        dst = bank[vt_ // 2][:, (vt_ % 2) * SEG + 64 * ch:(vt_ % 2) * SEG + 64 * ch + 64]
                        off = 64 * (ch % 2)
                        for d in range(2):
                            mm(dst, gvt[:, 2 + b, at:at + P], pm[:, d, b, c, off:off + 64], d == 0, False)
                            ins = mm(dst, gst[:, d, ch if d == 0 else 3 - ch, c, (vt_ % 2) * P:(vt_ % 2 + 1) * P],
                                     qh[:, d, c, 64 * ch:64 * ch + 64], False, d == 1)
                    if vt_ % 2:
                        ins.then_inc(S("go_mm"), 1)
                pe.wait_ge(S("go_sq"), 1)
                for c in range(4):
                    for i_ in range(2):
                        ins = mm(bank[c // 2][:, (c % 2) * SEG:(c % 2 + 1) * SEG], ones[:, :], sq2[:, 2 * c + i_],
                                 i_ == 0, i_ == 1)
                    if c % 2:
                        ins.then_inc(S("go_sum"), 1)
                pe.wait_ge(S("mixed"), 2)
                project_out(4, "odd_out", SEG)

            for g in range(SUBS):
                if g == 1:
                    even_mixer()
                elif g == 4:
                    odd_mixer()
                else:
                    ffn(g)
                norm(g)
            pe.wait_ge(S("h_ready"), KT * (SUBS + 1))
            for b in range(2):
                for q in range(2):
                    for c in range(4):
                        k = 4 * q + c
                        ins = pe.transpose(bank[2 * b + q][:, c * P:(c + 1) * P],
                                           hv[:, k, SEG + b * P:SEG + (b + 1) * P], ident[:, :])
                    ins.then_inc(S("out_turned"), 1)

        @block.vector
        def _(ve):
            v = Count()

            for i, val in enumerate((LN_EPS, GLA_EPS, GN_EPS, 1.0)):
                ve.memset(eps[:, i:i + 1], val).then_inc(S("ve_steps"), v.step())
            ve.wait_ge(S("ve_steps"), v.n)
            ve.wait_ge(S("par_turned"), 1)
            for i, n in enumerate((120, 120, 125)):
                ve.tensor_copy(par[:, i * P:i * P + n], bank[0][:, i * P:i * P + n]).then_inc(S("ve_steps"), v.step())
            ve.wait_ge(S("ve_steps"), v.n)
            ve.tensor_copy(cfv[:, 0:12, 0:3].rearrange("p i j -> p j i"),
                                 par[:, PAR["conv_w"]:PAR["conv_w"] + 36].rearrange("p (j i) -> p j i", j=3)).then_inc(S("ve_steps"), v.step())
            ve.tensor_copy(cfv[:, 0:12, 3], par[:, PAR["conv_b"]:PAR["conv_b"] + 12]).then_inc(S("ve_steps"), v.step())
            mu = par[:, PAR["mu"]:PAR["mu"] + 15]
            ve.tensor_scalar(cfv[:, 12:27, 0], mu, 0.5, None, ALU.mult).then_inc(S("ve_steps"), v.step())
            ve.tensor_scalar(cfv[:, 12:27, 2], mu, 0.5, None, ALU.mult).then_inc(S("ve_steps"), v.step())
            ve.tensor_scalar(cfv[:, 12:27, 1], mu, -1.0, 1.0, ALU.mult, ALU.add).then_inc(S("ve_steps"), v.step())
            ve.memset(cfv[:, 12:27, 3], 0.0).then_inc(S("ve_steps"), v.step())
            ve.wait_ge(S("ve_steps"), v.n)
            ve.sem_inc(S("par_done"), 1)
            ve.sem_inc(S("pairs_free"), 1)
            ve.sem_inc(S("pairs_free"), 1)
            ve.wait_ge(S("silu_c"), 1)
            sc2 = sc[:, :].rearrange("p (k s) -> p k s", s=2)
            ve.tensor_copy(sc2[:, :, 1], sgc[:, 0:8]).then_inc(S("ve_steps"), v.step())
            ve.tensor_copy(sc2[:, :, 0], sgc[:, 8:16]).then_inc(S("ve_steps"), v.step())
            ve.wait_ge(S("ve_steps"), v.n)
            ve.sem_inc(S("sc_ready"), 1)

            for i in range(2):
                ve.wait_ge(S("filt_mm"), i + 1)
                if i:
                    ve.wait_ge(S("sin_done"), 1)
                ve.tensor_scalar(pre, bank[6 + i][0:HY_FO, 0:SEG], hyp[0:HY_FO, 2 * i:2 * i + 1],
                                       hyp[0:HY_FO, 2 * i + 1:2 * i + 2], ALU.add, ALU.mult).then_inc(S("ve_steps"), v.step())
                ve.wait_ge(S("ve_steps"), v.n)
                ve.tensor_scalar(turns, pre, 1 / TWO_PI, MAGIC, ALU.mult, ALU.add).then_inc(S("ve_steps"), v.step())
                ve.wait_ge(S("ve_steps"), v.n)
                ve.tensor_scalar(turns, turns, MAGIC, None, ALU.subtract).then_inc(S("ve_steps"), v.step())
                ve.wait_ge(S("ve_steps"), v.n)
                for part in (PI_A, PI_B, PI_C):
                    ve.scalar_tensor_tensor(out=pre, in0=turns, scalar=-part, in1=pre, op0=ALU.mult,
                                                  op1=ALU.add).then_inc(S("ve_steps"), v.step())
                    ve.wait_ge(S("ve_steps"), v.n)
                ve.tensor_scalar(pre, pre, 3.1415925, -3.1415925, ALU.min, ALU.max).then_inc(S("sin_arg"), 1)
            def modulation(g):
                ve.wait_ge(S("ada_turned"), g + 1)
                m = modv[:, 24 * (g % 2):24 * (g % 2) + 24]
                at = PAR[f"ada_b{g // 3}"] + 24 * (g % 3)
                ve.tensor_tensor(m, bank[4][:, 0:48].rearrange("p (b s) -> p b s", s=2),
                                 par[:, at:at + 24].unsqueeze(2).to_broadcast([P, 24, 2]), ALU.add)\
                    .then_inc(S("ve_steps"), v.step())
                ve.wait_ge(S("ve_steps"), v.n)
                ve.tensor_scalar(m[:, 8:16], m[:, 8:16], 1.0, None, ALU.add).then_inc(S("ve_steps"), v.step())
                ve.wait_ge(S("ve_steps"), v.n)
                ve.tensor_scalar(m[:, 16:24], m[:, 16:24], 1.0 if g % 3 == 1 else 0.5, None, ALU.mult)\
                    .then_inc(S("mods"), 1)

            ve.wait_ge(S("ld_const"), 64)
            ve.tensor_copy(masks[:, :], arena[:, 8192:8192 + NMASK * P]).then_inc(S("ve_steps"), v.step())
            ve.wait_ge(S("ve_steps"), v.n)
            modulation(0)
            ve.sem_inc(S("taps_free"), 1)
            for o in range(2):
                ve.wait_ge(S("filt_taps"), o + 1)
                for dr in range(2):
                    for a in range(2):
                        ve.tensor_tensor(taps[:, dr, a], bank[4 + 2 * dr + a], win[:, a], ALU.mult).then_inc(S("ve_steps"), v.step())
                ve.wait_ge(S("ve_steps"), v.n)
                ve.memset(taps[0:1, 1, 0], 0.0).then_inc(S("ve_steps"), v.step())
                ve.tensor_tensor(taps[0:1, 0, 0], taps[0:1, 0, 0], skip_row[:, o], ALU.add).then_inc(S("ve_steps"), v.step())
                ve.wait_ge(S("ve_steps"), v.n)
                ve.tensor_tensor(tap_m, taps[:, 0], taps[:, 1], ALU.subtract).then_inc(S("ve_steps"), v.step())
                ve.wait_ge(S("ve_steps"), v.n)
                ve.tensor_tensor(taps[:, 0], taps[:, 0], taps[:, 1], ALU.add).then_inc(S("taps"), 1)
                ve.wait_ge(S("filt_dft"), o + 1)
                if o == 0:
                    ve.wait_ge(S("kf_done"), 6)
                    ve.sem_inc(S("taps_free"), 1)

            def u_lat(g):
                ve.wait_ge(S("mods"), g + 1)
                for k in range(KT):
                    ve.wait_ge(S("h_ready"), KT * g + k + 1)
                    ve.tensor_scalar(us[:, k, 1], hs[:, k, 1], modv[:, 24 * (g % 2) + 8 + k, 1:2],
                                     modv[:, 24 * (g % 2) + k, 1:2], ALU.mult, ALU.add).then_inc(S("u_lat"), 1)
                T0 = 0 if g < 5 else SEG
                for k in range(KT):
                    ve.wait_ge(S("u_hi"), U_BASE[g] + k + 1)
                    ve.tensor_tensor(ulv[:, k, T0:NT], uv[:, k, T0:NT], uhf[:, k, T0:NT], ALU.subtract)\
                        .then_inc(S("u_lo"), 1)
                ve.tensor_scalar(hs[:, :, 1], hs[:, :, 1], ALPHA, None, ALU.mult).then_inc(S("ve_steps"), v.step())

            def out_lo(g, left, right, TN):
                for k in range(KT):
                    ve.wait_ge(S("u_hi"), U_BASE[g] + KT + k + 1)
                    src = left[:, k] if k < 4 else right[:, k - 4]
                    ve.tensor_tensor(ulv[:, k, 0:TN], src[:, 0:TN], uhf[:, k, 0:TN], ALU.subtract)\
                        .then_inc(S("u_lo"), 1)

            def ffn_gate(g):
                f = FFN.index(g)
                TN = NT if g < 5 else SEG
                ve.wait_ge(S("u_lo"), U_BASE[g] + KT)
                for t0, t1 in ((0, FA), (FA, FT)):
                    with ve.Fori(0, (t1 - t0) // 2) as c:
                        for jf in range(2):
                            done = FT * f + t0 + jf + 1
                            prod = tmp[:, jf * NT:jf * NT + TN]
                            at = bass.ds(c * (2 * NT) + jf * NT, TN)
                            ve.wait_ge(S("silu"), c * 2 + done)
                            ve.tensor_tensor(prod, bank[2 * jf + 1][:, 0:TN], prod, ALU.mult).then_inc(S("pairs_free"), 1)
                            ve.wait_ge(S("pairs_free"), c * 2 + (done + 2))
                            ve.tensor_copy(hid_hi[:, at], prod).then_inc(S("hid_rounded"), 1)
                            ve.wait_ge(S("hid_rounded"), c * 2 + done)
                            ve.tensor_tensor(hid_lo[:, at], prod, hid_hi[:, at].bitcast(F32), ALU.subtract)\
                                .then_inc(S("hid"), 1)
                    if t0 == 0:
                        ve.wait_ge(S("ve_steps"), v.n)
                        if g < 4:
                            ve.wait_ge(S("scaled_ctx"), g + 1)
                        for k in range(KT):
                            ve.wait_ge(S("y_half"), KT * f + k + 1)
                            for s_ in segments(g):
                                lo = s_ * SEG if g < 4 else 0
                                ins = ve.scalar_tensor_tensor(out=hs[:, k, s_], in0=bank[k][:, lo:lo + SEG],
                                                              scalar=modv[:, 24 * (g % 2) + 16 + k, s_:s_ + 1],
                                                              in1=hs[:, k, s_], op0=ALU.mult, op1=ALU.add)
                            ins.then_inc(S("y_part"), 1)

            def norm(g):
                T0, TN = (0, NT) if g < 4 else (SEG, SEG)
                ve.wait_ge(S("ve_steps"), v.n)
                if g in FFN:
                    ve.wait_ge(S("y_part"), KT * (FFN.index(g) + 1))
                elif g < 4:
                    ve.wait_ge(S("scaled_ctx"), g + 1)
                for k in range(KT):
                    ve.wait_ge(S("y_done"), KT * g + k + 1)
                    for s in segments(g):
                        lo = s * SEG if g < 4 else 0
                        ve.scalar_tensor_tensor(out=hs[:, k, s], in0=bank[k][:, lo:lo + SEG],
                                                scalar=modv[:, 24 * (g % 2) + 16 + k, s:s + 1], in1=hs[:, k, s],
                                                op0=ALU.mult, op1=ALU.add).then_inc(S("resid"), 1)
                ve.wait_ge(S("resid"), resid_base[g + 1])
                ve.wait_ge(S("mean"), g + 1)
                for k in range(KT):
                    ve.tensor_tensor(hv[:, k, T0:NT], hv[:, k, T0:NT], bank[0][:, 0:TN], ALU.subtract)\
                        .then_inc(S("centred"), 1)
                ve.wait_ge(S("centred"), KT * (g + 1))
                ve.wait_ge(S("std"), g + 1)
                ve.reciprocal(rs[:, 0:TN], rs[:, 0:TN]).then_inc(S("ve_steps"), v.step())
                ve.wait_ge(S("ve_steps"), v.n)
                for k in range(KT):
                    ve.tensor_tensor(uv[:, k, T0:NT], hv[:, k, T0:NT], rs[:, 0:TN], ALU.mult)\
                        .then_inc(S("normed"), 1)
                if g + 1 < SUBS:
                    modulation(g + 1)

            def even_mixer():
                for i in range(ZT):
                    ve.wait_ge(S("z_main"), i + 1)
                    z = bank[i % 8].rearrange("p (s t) -> p s t", s=2)
                    o = bigt[:, i].rearrange("p (s t) -> p s t", s=2)
                    ve.scalar_tensor_tensor(out=o[:, :, 1:SEG], in0=z[:, :, 0:SEG - 1], scalar=cfv[:, i, 0:1],
                                                  in1=o[:, :, 1:SEG], op0=ALU.mult, op1=ALU.add).then_inc(S("ve_steps"), v.step())
                    ve.wait_ge(S("ve_steps"), v.n)
                    ve.scalar_tensor_tensor(out=o[:, :, 0:SEG - 1], in0=z[:, :, 1:SEG], scalar=cfv[:, i, 2:3],
                                            in1=o[:, :, 0:SEG - 1], op0=ALU.mult, op1=ALU.add)\
                        .then_inc(S("z_done"), 1)
                for o in range(2):
                    for s in range(2):
                        ve.wait_ge(S("hy_f"), 2 * o + s + 1)
                        if o == 0 and s == 0:
                            ve.wait_ge(S("vtok"), 8)
                        else:
                            ve.wait_ge(S("hy_mul"), 2 * o + s)
                        for i in range(2):
                            re, im = bank[4 * s + i], bank[4 * s + 2 + i]
                            kre, kim, kre2 = kf[:, o, i], kf[:, o, 2 + i], kf[:, o, 4 if i == 0 else i]
                            ve.tensor_tensor(ft[0], re, kre, ALU.mult).then_inc(S("ve_steps"), v.step())
                            ve.tensor_tensor(ft[1], im, kim, ALU.mult).then_inc(S("ve_steps"), v.step())
                            ve.wait_ge(S("ve_steps"), v.n)
                            ve.tensor_tensor(yf[:, s, i], ft[0], ft[1], ALU.subtract).then_inc(S("ve_steps"), v.step())
                            ve.wait_ge(S("ve_steps"), v.n)
                            ve.tensor_tensor(ft[0], re, kim, ALU.mult).then_inc(S("ve_steps"), v.step())
                            ve.tensor_tensor(ft[1], im, kre2, ALU.mult).then_inc(S("ve_steps"), v.step())
                            ve.wait_ge(S("ve_steps"), v.n)
                            ins = ve.tensor_tensor(yf[:, s, 2 + i], ft[0], ft[1], ALU.add)
                            if i == 0:
                                ins.then_inc(S("ve_steps"), v.step())
                                ve.wait_ge(S("ve_steps"), v.n)
                        ins.then_inc(S("hy_mul"), 1)
                    for s in range(2):
                        ve.wait_ge(S("hy_i"), 2 * o + s + 1)
                        for a in range(2):
                            if o == 0:
                                ve.tensor_tensor(vtok[:, 2 * s + a], bank[4 * s + a], x1tok[:, 2 * s + a], ALU.mult)\
                                    .then_inc(S("hy_y1"), 1)
                            else:
                                ve.tensor_tensor(yhy[:, 2 * a:2 * a + 2, s * SEG:(s + 1) * SEG],
                                                 bank[4 * s + a].rearrange("p (c t) -> p c t", c=2),
                                                 bigt[:, 8 + 2 * a:10 + 2 * a, s * SEG:(s + 1) * SEG], ALU.mult)\
                                    .then_inc(S("hy_done"), 1)
                tile_of = lambda ap, c: ap[:, c * NT:(c + 1) * NT]
                ve.wait_ge(S("hy_done"), 4)
                for c in range(CT):
                    ve.tensor_scalar(tile_of(kk, c), tile_of(zk, c), col("k_k", c), None, ALU.mult).then_inc(S("ve_steps"), v.step())
                ve.wait_ge(S("ve_steps"), v.n)
                ve.sem_inc(S("kk_raw"), 1)
                for d in range(2):
                    for c in range(CT):
                        ve.wait_ge(S("lora_out"), CT * d + c + 1)
                        for n in range(4):
                            at = slice(c * NT + n * P, c * NT + (n + 1) * P)
                            ve.tensor_tensor_scan(sgw[d][:, at], ones[:, :], sgw[d][:, at], 0.0, ALU.mult, ALU.add)\
                                .then_inc(S("ve_steps"), v.step())
                ve.wait_ge(S("ve_steps"), v.n)
                for d in range(2):
                    ve.tensor_scalar(half[:, d], sgw[d].rearrange("p (c n t) -> p c n t", c=CT, n=4)[:, :, :, P - 1],
                                     0.5, None, ALU.mult).then_inc(S("ve_steps"), v.step())
                ve.wait_ge(S("ve_steps"), v.n)
                for d in range(2):
                    chunks = sgw[d].rearrange("p (g t) -> p g t", t=P)
                    hb = small[:, 64 + 16 * d:80 + 16 * d].unsqueeze(2).to_broadcast([P, 16, P])
                    ve.tensor_tensor(chunks, chunks, hb, ALU.subtract).then_inc(S("ve_steps"), v.step())
                ve.wait_ge(S("ve_steps"), v.n)
                ve.sem_inc(S("sums"), 1)
                ve.wait_ge(S("kk_norm"), 4)
                ve.tensor_scalar(prep2, prep2, 1e-12, None, ALU.max).then_inc(S("ve_steps"), v.step())
                ve.wait_ge(S("ve_steps"), v.n)
                ve.reciprocal(prep2, prep2).then_inc(S("ve_steps"), v.step())
                ve.wait_ge(S("ve_steps"), v.n)
                ve.tensor_tensor(kk, kk, prep2, ALU.mult).then_inc(S("ve_steps"), v.step())
                ve.wait_ge(S("ve_steps"), v.n)
                ve.wait_ge(S("lora_out"), 20)
                ve.tensor_tensor(prep, aa[0], aa[1], ALU.add).then_inc(S("ve_steps"), v.step())
                ve.tensor_scalar(small[:, 20:24], par[:, PAR["k_a"]:PAR["k_a"] + 4], -1.0, 1.0, ALU.mult, ALU.add).then_inc(S("ve_steps"), v.step())
                ve.wait_ge(S("ve_steps"), v.n)
                ve.tensor_scalar(small[:, 24:28], small[:, 20:24], 2.0, None, ALU.mult).then_inc(S("ve_steps"), v.step())
                ve.wait_ge(S("ve_steps"), v.n)
                for c in range(CT):
                    ve.tensor_scalar(tile_of(prep, c), tile_of(prep, c), col("k_a", c), small[:, 24 + c:25 + c],
                                           ALU.mult, ALU.add).then_inc(S("ve_steps"), v.step())
                ve.wait_ge(S("ve_steps"), v.n)
                ve.tensor_tensor(prep, prep, zk, ALU.mult).then_inc(S("ve_steps"), v.step())
                ve.wait_ge(S("ve_steps"), v.n)
                for c in range(CT):
                    ve.scalar_tensor_tensor(out=tile_of(prep, c), in0=tile_of(prep, c), scalar=col("r_k", c),
                                                  in1=tile_of(zr, c), op0=ALU.mult, op1=ALU.mult).then_inc(S("ve_steps"), v.step())
                ve.wait_ge(S("ve_steps"), v.n)
                ve.sem_inc(S("bonus_in"), 1)
                for d in range(2):
                    for c in range(CT):
                        dst = tile_of(kd[0] if d == 0 else prep2, c)
                        ve.tensor_scalar(dst, tile_of(aa[d], c), col("k_a", c), small[:, 20 + c:21 + c],
                                               ALU.mult, ALU.add).then_inc(S("ve_steps"), v.step())
                ve.wait_ge(S("ve_steps"), v.n)
                ve.tensor_tensor(kd[0], kd[0], zk, ALU.mult).then_inc(S("ve_steps"), v.step())
                ve.wait_ge(S("ve_steps"), v.n)
                ve.tensor_tensor(zk, zk, prep2, ALU.mult).then_inc(S("ve_steps"), v.step())
                ve.tensor_tensor(aa[0], aa[0], kk, ALU.mult).then_inc(S("ve_steps"), v.step())
                ve.tensor_tensor(aa[1], aa[1], kk, ALU.mult).then_inc(S("ve_steps"), v.step())
                ve.wait_ge(S("v_turned"), 4)
                for c in range(CT):
                    ve.wait_ge(S("bonus_sum"), c + 1)
                    ve.tensor_tensor(tile_of(zv, c), bank[c], tile_of(zv, c), ALU.mult).then_inc(S("ve_steps"), v.step())
                ve.memset(arena[:, 42496:43008], 0.0).then_inc(S("ve_steps"), v.step())
                ve.wait_ge(S("ve_steps"), v.n)
                ve.sem_inc(S("prepared"), 1)
                chunk = lambda ap, ch: three(ap)[:, :, ch * P:(ch + 1) * P]

                def slots_of(j, d):
                    ch = chunk_of(d, j)
                    ve.wait_ge(S("exped"), 2 * j + d + 1)
                    recv, read, key = decays[d]
                    for e in range(2):
                        hp = slice(64 * e, 64 * e + 64)
                        ve.scalar_tensor_tensor(out=ar[hp, d, :, e, 0], in0=chunk(kk, ch)[hp], scalar=-1.0,
                                                in1=recv[hp], op0=ALU.mult, op1=ALU.mult)\
                            .then_inc(S("ve_steps"), v.step())
                    ve.tensor_tensor(bk[:, d, :, 1], chunk(kd[d], ch), key, ALU.mult).then_inc(S("ve_steps"), v.step())
                    ve.tensor_tensor(bk[:, d, :, 0], chunk(aa[d], ch), key, ALU.mult).then_inc(S("ve_steps"), v.step())
                    ve.wait_ge(S("ve_steps"), v.n)
                    ve.sem_inc(S("slots"), 1)

                def scale_state(j, d):
                    ed = edec[:, d, :, chunk_of(d, j)].unsqueeze(2).to_broadcast([P, CT, 64])
                    ve.tensor_tensor(state[:, d], state[:, d], ed, ALU.mult).then_inc(S("state_in"), 1)

                ve.wait_ge(S("edec"), 1)
                for d in range(2):
                    slots_of(0, d)
                    scale_state(0, d)
                ve.wait_ge(S("zeroed"), 1)
                for j in range(4):
                    for hf in range(2):
                        gi = 2 * j + hf
                        for d in range(2):
                            mk = maskv[:, M_STRICT + 2 * d:M_STRICT + 2 * d + 2].rearrange("p m t -> p (m t)")\
                                .unsqueeze(1).to_broadcast([P, 2, 2 * P])
                            for cc in range(2):
                                for q in range(2):
                                    ve.wait_ge(S("n_mm"), 8 * gi + 4 * d + 2 * cc + q + 1)
                                    ve.copy_predicated(nm[:, d, 2 * cc:2 * cc + 2, 2 * q:2 * q + 2]
                                                       .rearrange("p h a t -> p h (a t)"), mk,
                                                       bank[n_bank(d, cc, q)].rearrange("p (b t) -> p b t", b=2))\
                                        .then_inc(S("n_done"), 1)
                        for lv in range(LEVELS):
                            m = 1 << lv
                            for d in range(2):
                                um, tm = (M_UP, M_LO) if d == 0 else (M_LO, M_UP)
                                mask = lambda k, which: blocks(maskv[:, k + lv], m, which).unsqueeze(1)\
                                    .to_broadcast([P, 4, 64 // m, m])
                                wide = lambda ap: ap[:, 0:2 * P].rearrange("p (h g m) -> p h g m", h=4, m=m)
                                if lv == 0:
                                    ve.wait_ge(S("z_mm"), 2 * LEVELS * gi + d + 1)
                                    ve.wait_ge(S("tu_reset"), 2 * gi + d + 1)
                                    if d == 0:
                                        ve.wait_ge(S("n_done"), 8 * (gi + 1))
                                    tsrc = wide(bank[d])
                                    usrc = blocks(nm[:, d, :, 0], m, 1 - d)
                                else:
                                    ve.wait_ge(S("d_mm"), 2 * (gi * (LEVELS - 1) + lv - 1) + d + 1)
                                    tsrc = wide(bank[2 + d])
                                    usrc = wide(bank[4 + d])
                                if lv < LEVELS - 1:
                                    ve.copy_predicated(blocks(tu[:, d, 0], m, d), mask(tm, d), tsrc)\
                                        .then_inc(S("tu"), 1)
                                    ve.copy_predicated(blocks(tu[:, d, 1], m, 1 - d), mask(um, 1 - d), usrc)\
                                        .then_inc(S("tu"), 1)
                                else:
                                    ve.copy_predicated(blocks(tu[:, d, 1], m, 1 - d), mask(um, 1 - d), usrc)\
                                        .then_inc(S("tu"), 2)
                        if hf == 0:
                            ve.wait_ge(S("state_in"), 2 * (j + 1))
                        for d in range(2):
                            ve.wait_ge(S("sa_mm"), 2 * gi + d + 1)
                            ve.tensor_copy(xs[:, d, 1].rearrange("p h v -> p (h v)"), bank[4 + d][:, 0:256])\
                                .then_inc(S("sa"), 1)
                        ve.wait_ge(S("os_mm"), 2 * gi + 2)
                        for d in range(2):
                            st = state[:, d, 2 * hf:2 * hf + 2]
                            ve.tensor_tensor(st, st, bank[d][:, 0:128].rearrange("p (c v) -> p c v", c=2), ALU.add)\
                                .then_inc(S("ve_steps"), v.step())
                        ve.wait_ge(S("ve_steps"), v.n)
                        for d in range(2):
                            st = state[:, d, 2 * hf:2 * hf + 2]
                            ed = edec[:, d, 2 * hf:2 * hf + 2, chunk_of(d, j)].unsqueeze(2).to_broadcast([P, 2, 64])
                            ve.tensor_tensor(st, st, ed, ALU.mult).then_inc(S("state_new"), 1)
                        if hf and j < 3:
                            slots_of(j + 1, 0)
                        for d in range(2):
                            ch = chunk_of(d, j)
                            for q in range(2):
                                lo = 64 * q
                                dst = three(oacc)[lo:lo + 64, 2 * hf:2 * hf + 2, ch * P:(ch + 1) * P]
                                src = bank[6 + q][lo:lo + 64, 2 * d * P:2 * (d + 1) * P]\
                                    .rearrange("p (c t) -> p c t", c=2)
                                if j % 2 == 0:
                                    ve.tensor_copy(dst, src).then_inc(S("o_add"), 1)
                                else:
                                    ve.tensor_tensor(dst, dst, src, ALU.add).then_inc(S("o_add"), 1)
                        if hf and j < 3:
                            slots_of(j + 1, 1)
                            ve.wait_ge(S("state_new"), 4 * (j + 1))
                            for d in range(2):
                                scale_state(j + 1, d)
                ve.wait_ge(S("o_add"), 32)
                for c in range(CT):
                    ve.wait_ge(S("gn_mean"), c + 1)
                    o = tile_of(oacc, c)
                    ve.scalar_tensor_tensor(out=o, in0=bank[c], scalar=-1 / 64.0, in1=o, op0=ALU.mult, op1=ALU.add)\
                        .then_inc(S("gn_centred"), 1)
                ve.wait_ge(S("gn_centred"), 4)
                ve.wait_ge(S("gn_std"), 4)
                ve.reciprocal(prep2, prep2).then_inc(S("ve_steps"), v.step())
                ve.wait_ge(S("ve_steps"), v.n)
                ve.tensor_tensor(oacc, oacc, prep2, ALU.mult).then_inc(S("ve_steps"), v.step())
                ve.wait_ge(S("ve_steps"), v.n)
                for c in range(CT):
                    ve.tensor_scalar(tile_of(oacc, c), tile_of(oacc, c), col("gn_g", c), col("gn_b", c),
                                           ALU.mult, ALU.add).then_inc(S("ve_steps"), v.step())
                ve.wait_ge(S("ve_steps"), v.n)
                ve.tensor_tensor(oacc, oacc, zv, ALU.add).then_inc(S("ve_steps"), v.step())
                ve.wait_ge(S("ve_steps"), v.n)
                ve.tensor_tensor(oacc, oacc, gate, ALU.mult).then_inc(S("ve_steps"), v.step())
                ve.wait_ge(S("ve_steps"), v.n)
                ve.sem_inc(S("mixed"), 1)
                ve.sem_inc(S("scratch_free"), 1)
                out_lo(1, yhy, three(oacc), NT)

            def odd_mixer():
                ve.wait_ge(S("z1_done"), len(OD_TILES))
                for q in range(8):
                    ve.wait_ge(S("lg_abs"), q + 1)
                    ve.tensor_scalar(gg[:, q // 4, q % 4], bank[q], col("gla_b", q), 0.0, ALU.add, ALU.min).then_inc(S("ve_steps"), v.step())
                ve.wait_ge(S("ve_steps"), v.n)
                ve.wait_ge(S("lg_ln"), 1)
                ggf = arena[:, 8192:12288]
                ve.tensor_tensor(ggf, ggf, arena[:, 16384:20480], ALU.subtract).then_inc(S("ve_steps"), v.step())
                ve.wait_ge(S("ve_steps"), v.n)
                ve.wait_ge(S("ld_gla"), 48)
                for q in range(8):
                    ve.tensor_tensor_scan(gcs[:, q // 4, q % 4], greset, gg[:, q // 4, q % 4], 0.0, ALU.mult,
                                                ALU.add).then_inc(S("ve_steps"), v.step())
                ve.wait_ge(S("ve_steps"), v.n)
                tot = gcs[:, 0, :, SEG - 1].unsqueeze(2).to_broadcast([P, 4, SEG])
                ve.tensor_tensor(kout[:, 0], tot, gcs[:, 0, :, 0:SEG], ALU.subtract).then_inc(S("ve_steps"), v.step())
                ve.tensor_tensor(kout[:, 1], gcs[:, 1, :, 0:SEG], gg[:, 1, :, 0:SEG], ALU.subtract).then_inc(S("ve_steps"), v.step())
                ve.wait_ge(S("ve_steps"), v.n)
                ve.sem_inc(S("ctx_arg"), 1)
                for d in range(2):
                    ve.tensor_scalar(ghalf[:, d], gcs[:, d, :, SEG + 63:NT:64], 0.5, None, ALU.mult).then_inc(S("ve_steps"), v.step())
                ve.wait_ge(S("ve_steps"), v.n)
                for c in range(4):
                    hb = lambda d: ghalf[:, d, c].unsqueeze(2).to_broadcast([P, 4, 64])
                    cv = lambda ap: ap.rearrange("p (n t) -> p n t", n=4)
                    ve.tensor_tensor(cv(sq2[:, c]), cv(gcs[:, 0, c, SEG:NT]), hb(0), ALU.subtract).then_inc(S("ve_steps"), v.step())
                    ve.tensor_tensor(sq2[:, 4 + c], gcs[:, 1, c, SEG:NT], gg[:, 1, c, SEG:NT], ALU.subtract).then_inc(S("ve_steps"), v.step())
                    ve.wait_ge(S("ve_steps"), v.n)
                    ve.tensor_tensor(cv(sq2[:, 4 + c]), cv(sq2[:, 4 + c]), hb(1), ALU.subtract).then_inc(S("ve_steps"), v.step())
                ve.wait_ge(S("ve_steps"), v.n)
                ve.wait_ge(S("ctx_exp"), 1)
                ve.sem_inc(S("lat_arg"), 1)
                for d in range(2):
                    ve.tensor_tensor(kout[:, d], kout[:, d], gk[:, :, 0:SEG], ALU.mult).then_inc(S("ve_steps"), v.step())
                ve.wait_ge(S("ve_steps"), v.n)
                ve.sem_inc(S("kout"), 1)
                ve.wait_ge(S("lat_exp"), 1)
                for d in range(2):
                    ve.scalar_tensor_tensor(out=qh[:, d], in0=gq, scalar=HK ** -0.5, in1=qh[:, d],
                                                  op0=ALU.mult, op1=ALU.mult).then_inc(S("ve_steps"), v.step())
                    ve.tensor_tensor(kh[:, d], gk[:, :, SEG:NT], kh[:, d], ALU.mult).then_inc(S("ve_steps"), v.step())
                ve.wait_ge(S("ve_steps"), v.n)
                ve.sem_inc(S("lat_in"), 1)
                ve.wait_ge(S("pm_zero"), 1)
                eb = lambda d, n: gexp[:, d, :, XCHUNK(d, n)].unsqueeze(2).to_broadcast([P, 4, HV])
                ve.wait_ge(S("gs_mm"), 1)
                for d in range(2):
                    ins = ve.tensor_tensor(gst[:, d, 0], psum[:, 2 * d:2 * d + 2, :].rearrange("p b (c v) -> p (b c) v", c=2),
                                           eb(d, 0), ALU.mult)
                    if d == 0:
                        ins.then_inc(S("ve_steps"), v.step())
                ins.then_inc(S("gst"), 1)
                for d in range(2):
                    for b in range(2):
                        ve.wait_ge(S("sc_mm"), 2 * d + b + 1)
                        ve.copy_predicated(pm[:, d, b], maskv[:, M_GLA + d].unsqueeze(1).to_broadcast([P, 4, P]),
                                           bank[4 + 2 * d + b].rearrange("p (c t) -> p c t", c=4))\
                            .then_inc(S("pm"), 1)
                for n in range(3):
                    ve.wait_ge(S("gs_mm"), n + 2)
                    ve.wait_ge(S("gst"), n + 1)
                    b0 = 4 * ((n + 1) % 2)
                    for d in range(2):
                        nxt = gst[:, d, n + 1]
                        ve.tensor_tensor(nxt, psum[:, b0 + 2 * d:b0 + 2 * d + 2, :]
                                               .rearrange("p b (c v) -> p (b c) v", c=2), gst[:, d, n], ALU.add).then_inc(S("ve_steps"), v.step())
                        ve.wait_ge(S("ve_steps"), v.n)
                        ve.tensor_tensor(nxt, nxt, eb(d, n), ALU.mult).then_inc(S("ve_steps"), v.step())
                        ve.wait_ge(S("ve_steps"), v.n)
                        ins = ve.tensor_tensor(nxt, nxt, eb(d, n + 1), ALU.mult)
                        if d == 0:
                            ins.then_inc(S("ve_steps"), v.step())
                    ve.wait_ge(S("ve_steps"), v.n)
                    ins.then_inc(S("gst"), 1)
                for b in range(4):
                    ve.wait_ge(S("go_mm"), b + 1)
                    ve.tensor_copy(go[:, 2 * b:2 * b + 2].rearrange("p c t -> p (c t)"), bank[b])\
                        .then_inc(S("go_done"), 1)
                ve.wait_ge(S("go_done"), 4)
                ve.wait_ge(S("go_std"), 2)
                ve.reciprocal(grs.rearrange("p c t -> p (c t)"), grs.rearrange("p c t -> p (c t)")).then_inc(S("ve_steps"), v.step())
                ve.wait_ge(S("ve_steps"), v.n)
                g2 = go.rearrange("p (c a) t -> p c a t", a=2)
                for a in range(2):
                    ve.scalar_tensor_tensor(out=g2[:, :, a], in0=g2[:, :, a], scalar=col("norm_g", a),
                                                  in1=grs, op0=ALU.mult, op1=ALU.mult).then_inc(S("ve_steps"), v.step())
                ve.wait_ge(S("ve_steps"), v.n)
                ve.tensor_tensor(go, go, gog, ALU.mult).then_inc(S("ve_steps"), v.step())
                ve.wait_ge(S("ve_steps"), v.n)
                ve.sem_inc(S("mixed"), 1)
                ve.sem_inc(S("scratch_free"), 1)
                out_lo(4, go, go[:, 4:8], SEG)

            for g in range(SUBS):
                u_lat(g)
                if g == 1:
                    even_mixer()
                elif g == 4:
                    odd_mixer()
                else:
                    ffn_gate(g)
                norm(g)

        @block.gpsimd
        def _(pool):
            def remainders(phase, g, sizes, tiles=0):
                q = 0
                for halves in sizes:
                    for _ in range(halves):
                        hq = half0[phase, g] + q
                        src = half_src(phase, g, q, tiles)
                        pool.wait_ge(S("hi_done"), hq + 1)
                        pool.tensor_tensor(half_shape(split_lo(hq), src), src,
                                           half_shape(split_hi(hq).bitcast(F32), src), ALU.subtract)\
                            .then_inc(S("lo_done"), 1)
                        q += 1
                    pool.wait_ge(S("lo_done"), hq + 1)
                    pool.sem_inc(S("chunk_split"), 1)

            def u_ctx(g):
                pool.wait_ge(S("mods"), g + 1)
                for k in range(KT):
                    pool.wait_ge(S("h_ready"), KT * g + k + 1)
                    pool.tensor_scalar(us[:, k, 0], hs[:, k, 0], modv[:, 24 * (g % 2) + 8 + k, 0:1],
                                       modv[:, 24 * (g % 2) + k, 0:1], ALU.mult, ALU.add).then_inc(S("u_ctx"), 1)
                if g < 4:
                    pool.wait_ge(S("u_ctx"), KT * (g + 1))
                    pool.tensor_scalar(hs[:, :, 0], hs[:, :, 0], ALPHA, None, ALU.mult).then_inc(S("scaled_ctx"), 1)

            def recurrence_resets():
                pool.wait_ge(S("hy_done"), 4)
                pool.wait_ge(S("lora_psum"), 20)
                pool.memset(arena[:, 6144:10240], 0.0).then_inc(S("nm_zero"), 1)
                pool.memset(arena[:, 12288:13312], 0.0).then_inc(S("nm_zero"), 1)
                pool.wait_ge(S("prepared"), 1)
                for e in range(2):
                    pool.wait_ge(S("nm_zero"), 2 + e)
                    zero = ar[64 - 64 * e:128 - 64 * e, :, :, e].rearrange("p d c a t -> p (d c) (a t)")
                    pool.memset(zero, 0.0).then_inc(S("nm_zero"), 1)
                pool.wait_ge(S("nm_zero"), 4)
                pool.sem_inc(S("zeroed"), 1)
                for gi in range(8):
                    j = gi // 2
                    if gi % 2 == 0:
                        for d in range(2):
                            pool.wait_ge(S("exped"), 2 * j + d + 1)
                            if j:
                                pool.wait_ge(S("os_mm"), 4 * j)
                            ch = chunk_of(d, j)
                            for e in range(2):
                                hp = slice(64 * e, 64 * e + 64)
                                if j:
                                    pool.wait_ge(S("tu_reset"), 4 * j)
                                if j or d or e:
                                    pool.wait_ge(S("readers"), 4 * j + 2 * d + e)
                                pool.tensor_tensor(ar[hp, d, :, e, 1], three(zr)[hp, :, ch * P:(ch + 1) * P],
                                                   decays[d][1][hp], ALU.mult).then_inc(S("readers"), 1)
                            pool.wait_ge(S("readers"), 4 * j + 2 * d + 2)
                            pool.sem_inc(S("slots_r"), 1)
                    if gi:
                        pool.wait_ge(S("sa_mm"), 2 * gi)
                    for d in range(2):
                        pool.tensor_copy(tu[:, d].rearrange("p a h t -> p (a h) t"),
                                         ident[:, :].unsqueeze(1).to_broadcast([P, 8, P])).then_inc(S("tu_reset"), 1)

            pool.wait_ge(S("ld_ident"), 16)
            for g in range(SUBS):
                if g < 5:
                    u_ctx(g)
                if g == 1:
                    remainders("even_in", g, [2] * 7)
                    recurrence_resets()
                    remainders("even_out", g, [2, 2])
                elif g == 4:
                    pool.memset(arena[0:32, 40448:41472], 0.0).then_inc(S("gup_zero"), 1)
                    remainders("odd_in", g, [2, 1, 2, 2, 2, 2, 2])
                    pool.wait_ge(S("z1_done"), len(OD_TILES))
                    pool.memset(big[:, 11776:13824], 0.0).then_inc(S("pm_zero"), 1)
                    remainders("odd_out", g, [2, 2])
                else:
                    remainders("up_a", g, [2] * (FA // 2))
                    remainders("down_a", g, [2] * (FA // 4), FA)
                    remainders("up_b", g, [2] * ((FT - FA) // 2))
                    remainders("down_b", g, [2, 2, 2], FT - FA)


OD_TILES = ([(j // 2, "k", j) for j in range(4)] + [(2, "gd", 0)] + [(3 + j // 2, "q", j) for j in range(4)]
            + [(5 + j // 4, "v", j) for j in range(16)] + [(9 + j // 2, "og", j) for j in range(8)])
OD_HALVES = 13


def kernel(**inputs):
    import concourse.bacc as bacc
    from concourse.bass_utils import run_bass_kernel_spmd as run

    nc = bacc.Bacc("TRN2", target_bir_lowering=False, num_devices=1)
    arrays, A, K = {}, {}, {}
    for name, value in inputs.items():
        arr = np.ascontiguousarray(value)
        arrays["in_" + name] = arr
        A[name] = nc.dram_tensor("in_" + name, arr.shape, mybir.dt.from_np(arr.dtype), kind="ExternalInput").ap()
    for name, arr in constants().items():
        arrays[name] = arr
        K[name] = nc.dram_tensor(name, arr.shape, mybir.dt.from_np(arr.dtype), kind="ExternalInput").ap()
    out = nc.dram_tensor("out", (1, SEG, D), F32, kind="ExternalOutput").ap()
    program(nc, A, K, out)
    r = run(nc, [arrays], core_ids=[0])
    return r.results[0]["out"]
```

```python
import math
from contextlib import ExitStack

import numpy as np
import concourse.bass as bass
from concourse import mybir

F32 = mybir.dt.float32
F32R = mybir.dt.float32r
U8 = mybir.dt.uint8
ALU = mybir.AluOpType
ACT = mybir.ActivationFunctionType

P = 128
D = 1024
KT = D // P
SEG = 256
NT = 2 * SEG
DEPTH = 2
F = 2816
FT = F // P
GRID_W = 64
ROWS = SEG // GRID_W
ALPHA = (2 * DEPTH) ** 0.25
LN_EPS = 1e-6
HW = 512
CT = HW // P
ZT = 27
HY_EMB, HY_FO = 33, 64
GN_EPS = 64e-5
GLA_EPS = 1e-5
GLA_N = 16.0
HK, HV = 128, 256
DECAY = math.exp(-0.5)

R = 2
HALF = 2048
FA = 12
SLOT = 4096
SUBS = 3 * DEPTH
ARENA = 45568
LEVELS = 7

PAR = {}


def _columns():
    at = 0
    for name, n in (("ada_b0", 72), ("ln_g", 48)):
        PAR[name] = at
        at += n
    at = P
    for name, n in (("ada_b1", 72), ("ln_b", 48)):
        PAR[name] = at
        at += n
    at = 2 * P
    for name, n in (("conv_w", 36), ("conv_b", 12), ("mu", 15), ("w0", 8), ("a0", 8), ("k_k", 4), ("k_a", 4),
                    ("r_k", 4), ("gn_g", 4), ("gn_b", 4), ("gla_b", 8), ("norm_g", 2), ("c", 8), ("c_ctx", 8)):
        PAR[name] = at
        at += n


_columns()

M_UP, M_LO, M_STRICT, M_GLA = 0, LEVELS, 2 * LEVELS, 2 * LEVELS + 4


def constants():
    i = np.arange(P)
    row, col = i[:, None], i[None, :]
    masks = []
    for lv in range(LEVELS):
        m = 1 << lv
        masks.append((row // (2 * m) == col // (2 * m)) & (row // m % 2 == 0) & (col // m % 2 == 1))
    masks += [m.T for m in masks]
    masks += [row < col, row <= col, row > col, row >= col]
    same = row // 64 == col // 64
    masks += [same & (row <= col), same & (row >= col)]
    t = np.arange(SEG)
    f = np.arange(SEG)
    w = 2 * np.pi * np.outer(t, f) / (2 * SEG)
    fwd = np.concatenate([np.cos(w), -np.sin(w)], 1)
    fwd[:, SEG] = np.cos(np.pi * t)
    s0 = -np.sin(w[:, :P])
    inv = np.concatenate([2 * np.cos(w.T), -2 * np.sin(w.T)], 0) / (2 * SEG)
    inv[0] = 1 / (2 * SEG)
    inv[SEG] = np.cos(np.pi * t) / (2 * SEG)
    tt = np.linspace(0.0, 1.0, SEG)[:, None]
    bands = (HY_EMB - 1) // 2
    fr = np.linspace(1e-4, bands - 1, bands)[None, :]
    ww = 2 * np.pi * t[:, None] / SEG
    z = np.concatenate([tt, np.cos(fr * ww), -np.sin(fr * ww)], 1)
    deltas = np.linspace(math.log(1e-2) / 1.5, math.log(1e-2) / 0.3, HW)
    win = np.exp(-tt * np.abs(deltas))
    reset = np.ones((P, NT))
    reset[:, [0, 256, 320, 384, 448]] = 0
    tile = lambda a, n: a.reshape(n, P, -1).transpose(1, 0, 2).reshape(P, -1)
    blk = np.kron(np.eye(2), np.ones((64, 64)))
    f32 = lambda a: np.ascontiguousarray(a, dtype=np.float32)
    return {
        "k_ident": f32(np.eye(P)), "k_mean": f32(np.full((P, P), 1 / D)), "k_blk": f32(blk),
        "k_ones": f32(np.ones((P, P))),
        "k_masks": f32(np.stack(masks, 1).reshape(P, -1)),
        "k_dft": f32(tile(fwd, 2)), "k_sin0": f32(tile(s0, 2)), "k_idft": f32(tile(inv, 4)),
        "k_zT": f32(z.T), "k_win": f32(tile(win, 2)), "k_reset": f32(reset),
    }


NMASK = 2 * LEVELS + 6


def _round_bits(x, bits):
    e = math.floor(math.log2(abs(x)))
    s = 2.0 ** (bits - 1 - e)
    return math.floor(x * s) / s


TWO_PI = 2 * math.pi
PI_A = _round_bits(TWO_PI, 10)
PI_B = _round_bits(TWO_PI - PI_A, 11)
PI_C = TWO_PI - PI_A - PI_B
MAGIC = 1.5 * 2.0 ** 23


def plan():
    items = []
    items += [(("ada", 0), 0, 16)] * 6
    for g in range(SUBS):
        if g % 3 != 1:
            phases = [(("up_a", g), [2] * (FA // 2), 32), (("down_a", g), [2] * (FA // 4), 16),
                      (("up_b", g), [2] * ((FT - FA) // 2), 32), (("down_b", g), [2, 2, 2], 16)]
        elif g == 1:
            phases = [(("even_in", g), [2] * 7, 16), (("even_out", g), [2, 2], 16)]
        else:
            phases = [(("odd_in", g), [2, 1, 2, 2, 2, 2, 2], 16), (("odd_out", g), [2, 2], 16)]
        mine = [(phase, n, each) for phase, halves, each in phases for n in halves]
        items.append(mine[0])
        if g + 1 < SUBS:
            items += [(("ada", g + 1), 0, 16)] * 6
        items += mine[1:]
    chunks, half0, arrival, holder, slot_total = {}, {}, [], [], [0] * R
    ada = split = halves = 0
    done = []
    for n, (phase, hn, each) in enumerate(items):
        chunks.setdefault(phase, []).append(n)
        half0.setdefault(phase, halves)
        halves += hn
        slot_total[n % R] += each
        arrival.append(slot_total[n % R])
        if hn:
            split += 1
            done.append(("chunk_split", split))
        else:
            ada += 1
            done.append(("ada_used", ada))
        holder.append(done[n - R] if n >= R else None)
    return chunks, half0, arrival, holder


def program(nc, A, K, out):
    chunks, half0, arrival, holder = plan()
    with ExitStack() as ctx:
        def sb(name, n, dt=F32, parts=P):
            return ctx.enter_context(nc.sbuf_tensor(name, [parts, n], dt))

        h = sb("h", KT * NT)
        tmp = sb("tmp", 2 * NT)
        rs = sb("rs", NT)
        par = sb("par", 3 * P)
        masks = sb("masks", NMASK * P, U8)
        ident = sb("ident", P)
        mean_w = sb("mean_w", P)
        blk = sb("blk", P)
        ones = sb("ones", P)
        sc = sb("sc", 2 * KT)
        sgc = sb("sgc", 2 * KT)
        mods = sb("mods", 2 * 48)
        cf = sb("cf", ZT * 4)
        hyp = sb("hyp", 4)
        eps = sb("eps", 4)
        small = sb("small", 128)
        arena = sb("arena", ARENA)
        base = nc.sbuf_base - 4 * ARENA

        def rounded(name, at, n):
            return nc.alloc_sbuf_tensor_at(name, [P, n], F32R, offset=base + 4 * at)

        w_hi = rounded("w_hi", 8192, 2 * HALF)
        w_lo = rounded("w_lo", 12288, 2 * HALF)
        u_hi = rounded("u_hi", 16384, KT * NT)
        u_lo = rounded("u_lo", 20480, KT * NT)
        hid_hi = rounded("hid_hi", 24576, FA * NT)
        hid_lo = rounded("hid_lo", 30720, FA * NT)
        big = arena[:, 26624:40448]
        u = arena[:, 24576:28672]
        psum = ctx.enter_context(nc.psum_tensor("psum", [P, 8, 512], F32))

        hv = h[:, :].rearrange("p (k t) -> p k t", k=KT)
        uv = u.rearrange("p (k t) -> p k t", k=KT)
        uhv = u_hi[:, :].rearrange("p (k t) -> p k t", k=KT)
        ulv = u_lo[:, :].rearrange("p (k t) -> p k t", k=KT)
        uhf = u_hi[:, :].bitcast(F32).rearrange("p (k t) -> p k t", k=KT)
        hidh = hid_hi[:, :].rearrange("p (k t) -> p k t", t=NT)
        hidl = hid_lo[:, :].rearrange("p (k t) -> p k t", t=NT)
        hs = h[:, :].rearrange("p (k s t) -> p k s t", k=KT, s=2)
        us = u.rearrange("p (k s t) -> p k s t", k=KT, s=2)
        modv = mods[:, :].rearrange("p (b s) -> p b s", s=2)
        bank = [psum[:, b, :] for b in range(8)]
        bigt = big.rearrange("p (i t) -> p i t", t=NT)
        maskv = masks[:, :].rearrange("p (m t) -> p m t", t=P)
        cfv = cf[:, :].rearrange("p (i j) -> p i j", j=4)

        sems = {}

        def S(name):
            if name not in sems:
                sems[name] = ctx.enter_context(nc.semaphore(name))
            return sems[name]

        def col(name, i=0):
            return par[:, PAR[name] + i:PAR[name] + i + 1]

        def slot(n):
            return arena[:, (n % R) * SLOT:(n % R + 1) * SLOT]

        def split_hi(q):
            return w_hi[:, (q % 2) * HALF:(q % 2 + 1) * HALF]

        def split_lo(q):
            return w_lo[:, (q % 2) * HALF:(q % 2 + 1) * HALF]

        def ada_row(g, c):
            if g == 1:
                return arena[0:2, 28672 + 512 * c:29184 + 512 * c] if c < 4 else tmp[0:2, 512 * (c - 4):512 * (c - 3)]
            at = (11264 if g == 0 else 34816) + 512 * c
            return arena[0:2, at:at + 512]

        def row_bank(g, c):
            return bank[2 if g == 1 else 2 + c % 2]

        class Count:
            n = 0

            def step(self):
                self.n += 1
                return 1

        tok_in = big[:, 0:4096].rearrange("p (b d) -> p b d", b=4)
        stage = [big[:, 4096 + i * P:4096 + (i + 1) * P] for i in range(3)]
        w3 = big[0:HY_FO, 4608:6656]
        win = big[:, 6656:7680].rearrange("p (a c) -> p a c", a=2)
        taps = big[:, 7680:9728].rearrange("p (d a c) -> p d a c", d=2, a=2)
        tap_m = big[:, 9728:10752].rearrange("p (a c) -> p a c", a=2)
        zT = big[0:HY_EMB, 10752:11008]
        fw1 = big[0:HY_EMB, 11008:11072]
        fw2 = big[0:HY_FO, 11072:11136]
        pre = big[0:HY_FO, 11136:11392]
        turns = big[0:HY_FO, 11392:11648]
        h1 = big[0:HY_FO, 11648:11904]
        h2 = big[0:HY_FO, 11904:12160]
        skip_row = big[0:1, 12160:13184].rearrange("p (o c) -> p o c", o=2)
        yhy = arena[:, 24576:26624].rearrange("p (c t) -> p c t", t=NT)
        kf = arena[:, 40448:45568].rearrange("p (o i c) -> p o i c", o=2, i=5)
        dft = arena[:, 16384:17408].rearrange("p (a f) -> p a f", a=2)
        sin0 = arena[:, 18432:18688].rearrange("p (a f) -> p a f", a=2)
        idft = arena[:, 17408:18432].rearrange("p (f t) -> p f t", f=4)
        vtok = arena[:, 0:2048].rearrange("p (b c) -> p b c", b=4)
        x1tok = arena[:, 2048:4096].rearrange("p (b c) -> p b c", b=4)
        yf = arena[:, 4096:8192].rearrange("p (s i c) -> p s i c", s=2, i=4)
        ft = [arena[:, 8192 + i * 512:8704 + i * 512] for i in range(2)]
        w_up = arena[:, 9216:9728]
        a_up = arena[:, 9728:10240]
        g_up = arena[:, 10240:10752]
        prep = arena[:, 0:2048]
        prep2 = arena[:, 2048:4096]
        bonus = arena[:, 4096:6144]
        gn_sq, gn_rstd = big[:, 0:2048], big[:, 2048:4096]
        kd1_factor = arena[:, 18432:20480]
        three = lambda ap: ap.rearrange("p (c t) -> p c t", t=NT)
        zr, zk, zv = big[:, 12 * NT:16 * NT], big[:, 16 * NT:20 * NT], big[:, 20 * NT:24 * NT]
        sgw = [big[:, 0:2048], big[:, 2048:4096]]
        aa = [big[:, 4096:6144], arena[:, 20480:22528]]
        kd = [arena[:, 22528:24576], zk]
        oacc = arena[:, 40448:42496]
        state = arena[:, 42496:43008].rearrange("p (d c v) -> p d c v", d=2, c=CT)
        gate, kk = arena[:, 43008:45056], arena[:, 16384:18432]
        ar = arena[:, 0:4096].rearrange("p (d c e a t) -> p d c e a t", d=2, c=CT, e=2, a=2)
        bk = arena[:, 18432:20480].rearrange("p (d c a t) -> p d c a t", d=2, c=CT, a=2)
        bkt = arena[:, 4096:6144].rearrange("p (d a c) -> p d a c", d=2, a=2)
        nm = arena[:, 6144:10240].rearrange("p (d h a t) -> p d h a t", d=2, h=4, a=4)
        tu = arena[:, 10240:12288].rearrange("p (d a h t) -> p d a h t", d=2, a=2, h=4)
        zs = arena[:, 12288:13312].rearrange("p (d h t) -> p d h t", d=2, h=4)
        xs = arena[:, 13312:14336].rearrange("p (d a h v) -> p d a h v", d=2, a=2, h=4)
        vt = arena[:, 14336:16384].rearrange("p (b c) -> p b c", b=4)
        decays = [[arena[:, 38912 + 512 * i:39424 + 512 * i].rearrange("p (c t) -> p c t", c=CT) for i in range(3)],
                  [at.rearrange("p (c t) -> p c t", c=CT) for at in (tmp[:, 0:512], tmp[:, 512:1024],
                                                                      arena[:, 45056:45568])]]
        half = small[:, 64:96].rearrange("p (d c n) -> p d c n", d=2, c=CT)
        edec = small[:, 96:128].rearrange("p (d c n) -> p d c n", d=2, c=CT)

        def blocks(ap, m, which):
            lead = " ".join("abc"[:len(ap.shape) - 2])
            return ap.rearrange(f"p {lead} (g s m) -> p {lead} g s m", s=2, m=m)[(slice(None),) * (len(ap.shape)) + (which,)]

        def packed(ap, m):
            return ap.rearrange("p (g m) -> p g m", m=m)

        gq = big[:, 0:1024].rearrange("p (c t) -> p c t", c=4)
        gk = big[:, 1024:3072].rearrange("p (c t) -> p c t", c=4)
        gvt = big[:, 3072:7168].rearrange("p (b c) -> p b c", b=4)
        gog = big[:, 7168:9216].rearrange("p (c t) -> p c t", c=8)
        ggd = big[0:32, 9216:9728]
        kout = big[:, 9728:11776].rearrange("p (d c t) -> p d c t", d=2, c=4)
        go = big[:, 9728:11776].rearrange("p (c t) -> p c t", c=8)
        pm = big[:, 11776:13824].rearrange("p (d b h t) -> p d b h t", d=2, b=2, h=4)
        gcs = arena[:, 16384:20480].rearrange("p (d c t) -> p d c t", d=2, c=4)
        gup = arena[0:32, 40448:41472].rearrange("p (d c) -> p d c", d=2)
        greset = arena[:, 41472:41984]
        grs = arena[:, 41984:43008].rearrange("p (c t) -> p c t", c=4)
        sq2 = arena[:, 43008:45056].rearrange("p (c t) -> p c t", c=8)
        gg = arena[:, 8192:12288].rearrange("p (d c t) -> p d c t", d=2, c=4)
        gst = arena[:, 0:8192].rearrange("p (d n c v) -> p d n c v", d=2, n=4, c=4)
        qh = arena[:, 8192:10240].rearrange("p (d c t) -> p d c t", d=2, c=4)
        kh = arena[:, 10240:12288].rearrange("p (d c t) -> p d c t", d=2, c=4)
        kht = arena[:, 12288:14336].rearrange("p (d b c) -> p d b c", d=2, b=2)
        kot = arena[:, 14336:16384].rearrange("p (d b c) -> p d b c", d=2, b=2)
        ghalf = small[:, 0:32].rearrange("p (d c n) -> p d c n", d=2, c=4)
        gpair = small[:, 64:96].rearrange("p (d c n) -> p d c n", d=2, c=4)
        gexp = small[:, 32:64].rearrange("p (d c n) -> p d c n", d=2, c=4)

        def half_src(phase, g, q, tiles):
            if phase == "odd_in" and q == 2:
                return slot(chunks[phase, g][1])[:, 0:KT * P]
            qq = q + 1 if phase == "odd_in" and q > 2 else q
            s_ = slot(chunks[phase, g][qq // 2])
            if phase.startswith("up"):
                return s_.rearrange("p (a k f) -> p a k f", a=2, k=KT)[:, :, :, (qq % 2) * P:(qq % 2 + 1) * P]
            if phase.startswith("down"):
                m = min(4, tiles - 4 * (qq // 2)) // 2
                return s_[:, (qq % 2) * m * D:(qq % 2 + 1) * m * D]
            cols = 384 if phase == "even_in" and qq >= 12 else 512
            v_ = s_[:, 0:KT * cols].rearrange("p (k n) -> p k n", k=KT)
            return v_[:, :, (qq % 2) * 256:min(cols, (qq % 2 + 1) * 256)]

        def half_shape(buf, src):
            if len(src.shape) == 2:
                return buf[:, 0:src.shape[1]]
            if len(src.shape) == 3:
                k, n = src.shape[1:]
                return buf[:, 0:k * n].rearrange("p (k n) -> p k n", k=k)
            a_, k, n = src.shape[1:]
            return buf[:, 0:a_ * k * n].rearrange("p (a k n) -> p a k n", a=a_, k=k)

        def chunk_of(d, j):
            return j if d == 0 else j ^ 1

        def n_bank(d, cc, q):
            return (2, 3, 4, 5)[2 * cc + q] if d == 0 else (0, 1, 6, 7)[2 * cc + q]

        XCHUNK = lambda d, n: n if d == 0 else 3 - n

        def segments(g):
            return (0, 1) if g < 4 else (1,)

        resid_base = [0]
        for g in range(SUBS):
            resid_base.append(resid_base[-1] + KT * len(segments(g)))

        U_BASE = [KT * (g + (g > 1) + (g > 4)) for g in range(SUBS)]
        FFN = (0, 2, 3, 5)

        block = ctx.enter_context(nc.Block())

        @block.sync
        def _(sp):
            def free(n):
                if holder[n]:
                    sp.wait_ge(S(holder[n][0]), holder[n][1])

            def load_ada(g):
                w = A["ada_w"][g // 3].rearrange("(k p) n -> p k n", p=P)
                for c in range(6):
                    n = chunks["ada", g][c]
                    free(n)
                    at = 3 * D * (g % 3) + 512 * c
                    sp.dma_start(slot(n).rearrange("p (k n) -> p k n", k=KT),
                                 w[:, :, at:at + 512]).then_inc(S(f"slot{n % R}"), 16)

            def load_up(phase, g, c0, count, start=0):
                l, i = g // 3, (g % 3) // 2
                wg = A["ffn_wg"][l, i].rearrange("(k p) f -> p k f", p=P)
                wu = A["ffn_wu"][l, i].rearrange("(k p) f -> p k f", p=P)
                n0 = chunks[phase, g]

                def pair(n, c, gone, value):
                    dst = slot(n).rearrange("p (a k f) -> p a k f", a=2, k=KT)
                    sp.wait_ge(S(gone), value)
                    sp.dma_start(dst[:, 0], wg[:, :, bass.ds(c * 256, 256)]).then_inc(S(f"slot{n % R}"), 16)
                    sp.dma_start(dst[:, 1], wu[:, :, bass.ds(c * 256, 256)]).then_inc(S(f"slot{n % R}"), 16)

                for c in range(start, R + 1):
                    pair(n0[c], c0 + c, *holder[n0[c]])
                loops = (count - R - 1) // R
                if loops:
                    with sp.Fori(0, loops) as it:
                        for r in range(R + 1, 2 * R + 1):
                            pair(n0[r], it * R + (c0 + r), "chunk_split", it * R + holder[n0[r]][1])
                for c in range(R + 1 + loops * R, count):
                    pair(n0[c], c0 + c, *holder[n0[c]])

            def load_down(phase, g, k0, k1):
                wd = A["ffn_wd"][g // 3, (g % 3) // 2].rearrange("(k p) d -> p k d", p=P)
                for c, k in enumerate(range(k0, k1, 4)):
                    n = chunks[phase, g][c]
                    m = min(4, k1 - k)
                    free(n)
                    sp.dma_start(slot(n)[:, 0:m * D].rearrange("p (k d) -> p k d", k=m),
                                 wd[:, k:k + m, :]).then_inc(S(f"slot{n % R}"), 16)

            def load_cols(phase, g, w, blocks_, c0=0):
                v = w.rearrange("(k p) n -> p k n", p=P)
                for c, (at, m) in enumerate(blocks_, c0):
                    n = chunks[phase, g][c]
                    free(n)
                    sp.dma_start(slot(n)[:, 0:KT * m].rearrange("p (k n) -> p k n", k=KT),
                                 v[:, :, at:at + m]).then_inc(S(f"slot{n % R}"), 16)

            load_ada(0)
            EVEN = [(512 * c, min(512, ZT * P - 512 * c)) for c in range(7)]
            ODD = [(512, 512), (2048, 128), (0, 512), (1024, 512), (1536, 512), (2080, 512), (2592, 512)]
            for g in range(SUBS):
                if g == 1:
                    load_cols("even_in", g, A["ev_w_in"][0], EVEN[:1])
                elif g == 4:
                    load_cols("odd_in", g, A["od_w_in"][0], ODD[:1])
                else:
                    n, l, i = chunks["up_a", g][0], g // 3, (g % 3) // 2
                    free(n)
                    for a_, w in enumerate((A["ffn_wg"], A["ffn_wu"])):
                        sp.dma_start(slot(n).rearrange("p (a k f) -> p a k f", a=2, k=KT)[:, a_],
                                     w[l, i].rearrange("(k p) f -> p k f", p=P)[:, :, 0:2 * P])\
                            .then_inc(S(f"slot{n % R}"), 16)
                if g + 1 < SUBS:
                    load_ada(g + 1)
                if g == 1:
                    load_cols("even_in", g, A["ev_w_in"][0], EVEN[1:], 1)
                    sp.wait_ge(S("os_mm"), 16)
                    load_cols("even_out", g, A["ev_w_out"][0], [(0, 512), (512, 512)])
                elif g == 4:
                    load_cols("odd_in", g, A["od_w_in"][0], ODD[1:], 1)
                    sp.wait_ge(S("go_mm"), 4)
                    load_cols("odd_out", g, A["od_w_out"][0], [(0, 512), (512, 512)])
                else:
                    load_up("up_a", g, 0, FA // 2, 1)
                    load_down("down_a", g, 0, FA)
                    load_up("up_b", g, FA // 2, (FT - FA) // 2)
                    load_down("down_b", g, FA, FT)
            sp.wait_ge(S("rows_out"), 4)
            rows = out[0].rearrange("(r c) d -> r c d", r=ROWS)
            o_sb = big[:, 0:2048].rearrange("p (b d) -> p b d", b=2)
            for b in range(2):
                for r in range(ROWS):
                    sp.dma_start(rows[r, 32 * b:32 * b + 32, :], o_sb[r:P:ROWS, b, :]).then_inc(S("stored"), 16)
            sp.wait_ge(S("stored"), 16 * 8)

        @block.scalar
        def _(act):
            def load(name, dst, src):
                act.dma_start(dst, src).then_inc(S(name), 16)

            load("ld_ident", ident[:, :], K["k_ident"])
            l0 = [("ada_b", 0, 72, A["ada_b"][0:1].rearrange("l (t p) -> (l t) p", p=P), 0),
                  ("ln_g", 72, 48, A["ln_g"].rearrange("l i (t p) -> (l i t) p", p=P), 0),
                  ("ada_b", 0, 72, A["ada_b"][1:2].rearrange("l (t p) -> (l t) p", p=P), 1),
                  ("ln_b", 72, 48, A["ln_b"].rearrange("l i (t p) -> (l i t) p", p=P), 1)]
            for _, at, n, src, s in l0:
                load("ld_par", stage[s][at:at + n, :], src)
            third = [("conv_w", 36, A["hy_conv_w"].rearrange("e j (t p) -> (e j t) p", p=P)),
                     ("conv_b", 12, A["hy_conv_b"].rearrange("e (t p) -> (e t) p", p=P)),
                     ("mu", 15, A["rw_mu"].rearrange("e (t p) -> (e t) p", p=P)),
                     ("w0", 8, A["rw_w0"].rearrange("e d (t p) -> (e d t) p", p=P)),
                     ("a0", 8, A["rw_a0"].rearrange("e d (t p) -> (e d t) p", p=P)),
                     ("k_k", 4, A["rw_k_k"].rearrange("e (t p) -> (e t) p", p=P)),
                     ("k_a", 4, A["rw_k_a"].rearrange("e (t p) -> (e t) p", p=P)),
                     ("r_k", 4, A["rw_r_k"].rearrange("e (t a) n -> (e t) (a n)", a=2)),
                     ("gn_g", 4, A["rw_gn_g"].rearrange("e (t p) -> (e t) p", p=P)),
                     ("gn_b", 4, A["rw_gn_b"].rearrange("e (t p) -> (e t) p", p=P)),
                     ("gla_b", 8, A["gla_g_b"].rearrange("e d (t p) -> (e d t) p", p=P)),
                     ("norm_g", 2, A["gla_norm_g"].rearrange("e (t p) -> (e t) p", p=P)),
                     ("c", 8, A["c"].rearrange("e (t p) -> (e t) p", p=P)),
                     ("c_ctx", 8, A["c_ctx"].rearrange("(t p) -> t p", p=P))]
            for name, n, src in third:
                at = PAR[name] - 2 * P
                load("ld_par", stage[2][at:at + n, :], src)
            for b in range(4):
                src = A["ctx"] if b < 2 else A["x"]
                load("ld_tok", tok_in[:, b, :], src[0, (b % 2) * P:(b % 2 + 1) * P, :])
            load("ld_filt", zT, K["k_zT"])
            load("ld_filt", fw1, A["hy_f_w1"][0])
            load("ld_filt", fw2, A["hy_f_w2"][0])
            for i, name in enumerate(("hy_f_b1", "hy_f_freq1", "hy_f_b2", "hy_f_freq2")):
                load("ld_filt", hyp[0:HY_FO, i:i + 1], A[name].rearrange("e n -> n e"))
            load("ld_filt", w3, A["hy_f_w3"][0])
            load("ld_filt", big[:, 6656:7680], K["k_win"])
            load("ld_filt", skip_row, A["hy_skip"].rearrange("e o c -> e o c"))
            load("ld_filt", arena[:, 16384:17408], K["k_dft"])
            load("ld_filt", arena[:, 18432:18688], K["k_sin0"])
            load("ld_const", mean_w[:, :], K["k_mean"])
            load("ld_const", blk[:, :], K["k_blk"])
            load("ld_const", ones[:, :], K["k_ones"])
            load("ld_const", arena[:, 8192:8192 + NMASK * P], K["k_masks"])

            act.wait_ge(S("par_done"), 1)
            act.activation(sgc[:, :], par[:, PAR["c"]:PAR["c"] + 16], ACT.Silu).then_inc(S("silu_c"), 1)
            for k in range(KT):
                act.wait_ge(S("tok_turned"), k + 1)
                act.activation(hv[:, k], bank[(k + 1) % 8], ACT.Copy).then_inc(S("h_ready"), 1)

            def ada_out(g, c):
                act.wait_ge(S("ada_used"), 6 * g + c + 1)
                act.activation(ada_row(g, c), row_bank(g, c)[0:2], ACT.Copy).then_inc(S("ada_row"), 1)

            def hi(phase, g, q, src):
                n, hq = chunks[phase, g][q // 2], half0[phase, g] + q
                if phase == "odd_in" and q > 1:
                    n = chunks[phase, g][1 if q == 2 else (q + 1) // 2]
                act.wait_ge(S(f"slot{n % R}"), arrival[n])
                if hq >= 2:
                    act.wait_ge(S("split_used"), hq - 1)
                if g == 0 and q < 2:
                    act.wait_ge(S("mods"), 1)
                act.activation(half_shape(split_hi(hq), src), src, ACT.Copy).then_inc(S("hi_done"), 1)

            def first_halves(g):
                phase = "even_in" if g == 1 else "odd_in" if g == 4 else "up_a"
                for q in range(2):
                    hi(phase, g, q, half_src(phase, g, q, FA))

            act.wait_ge(S("sin_arg"), 1)
            act.activation(h1, pre, ACT.Sin).then_inc(S("sin_done"), 1)
            for c in range(2):
                ada_out(0, c)
            act.wait_ge(S("sin_arg"), 2)
            act.activation(h2, pre, ACT.Sin).then_inc(S("sin_done"), 1)
            for c in range(2, 6):
                ada_out(0, c)
            first_halves(0)
            ada_out(1, 0)
            for o in range(2):
                act.wait_ge(S("filt_dft"), o + 1)
                for i, b in ((0, 0), (1, 1), (2, 3), (3, 4), (4, 0)):
                    act.activation(kf[:, o, i], bank[b], ACT.Copy).then_inc(S("kf_done"), 1)
                act.wait_ge(S("kf_done"), 6 * o + 5)
                act.activation(kf[0:1, o, 4], bank[5][0:1], ACT.Copy).then_inc(S("kf_done"), 1)
                for c in ((1, 2, 3), (4, 5))[o]:
                    ada_out(1, c)

            def u_round(g):
                T0 = 0 if g < 5 else SEG
                for k in range(KT):
                    act.wait_ge(S("u_lat"), KT * g + k + 1)
                    if g < 5:
                        act.wait_ge(S("u_ctx"), KT * g + k + 1)
                    act.activation(uhv[:, k, T0:NT], uv[:, k, T0:NT], ACT.Copy).then_inc(S("u_hi"), 1)

            def ffn_silu(g):
                f = FFN.index(g)
                TN = NT if g < 5 else SEG

                def silu(t):
                    jf = t % 2
                    act.wait_ge(S("gu_ready"), FT * f + t + 1)
                    if FT * f + t >= 2:
                        act.wait_ge(S("hid"), FT * f + t - 1)
                    act.activation(tmp[:, jf * NT:jf * NT + TN], bank[2 * jf][:, 0:TN], ACT.Silu)\
                       .then_inc(S("silu"), 1)

                for up, down, t0, t1 in (("up_a", "down_a", 0, FA), ("up_b", "down_b", FA, FT)):
                    halves = [(up, q) for q in range(t1 - t0)]
                    halves += [(down, q) for q in range(2 * -(-(t1 - t0) // 4))]
                    for at, (phase, q) in enumerate(halves):
                        if at >= 2 and at - 2 < t1 - t0:
                            silu(t0 + at - 2)
                        if t0 or at >= 2:
                            hi(phase, g, q, half_src(phase, g, q, t1 - t0))

            def norm(g):
                T0, TN = (0, NT) if g < 4 else (SEG, SEG)
                if g + 1 < SUBS:
                    first_halves(g + 1)
                for k in range(KT):
                    act.wait_ge(S("centred"), KT * g + k + 1)
                    if KT * g + k - 1 > 0:
                        act.wait_ge(S("sq_used"), KT * g + k - 1)
                    act.activation(tmp[:, (k % 2) * NT:(k % 2) * NT + TN], hv[:, k, T0:NT], ACT.Square)\
                       .then_inc(S("sq"), 1)
                act.wait_ge(S("sq_used"), KT * (g + 1))
                act.activation(rs[:, 0:TN], bank[1][:, 0:TN], ACT.Sqrt, bias=eps[:, 0:1]).then_inc(S("std"), 1)
                for k in range(KT):
                    act.wait_ge(S("normed"), KT * g + k + 1)
                    sg, sb_ = col("ln_g", 8 * g + k), col("ln_b", 8 * g + k)
                    if g == 2:
                        act.activation(hs[:, k, 0], us[:, k, 0], ACT.Identity, scale=sg, bias=sb_)
                        act.activation(hs[:, k, 1].rearrange("p (c r) -> p r c", r=ROWS),
                                       us[:, k, 1].rearrange("p (r c) -> p r c", r=ROWS),
                                       ACT.Identity, scale=sg, bias=sb_).then_inc(S("h_ready"), 1)
                    else:
                        act.activation(hv[:, k, T0:NT], uv[:, k, T0:NT], ACT.Identity, scale=sg, bias=sb_)\
                           .then_inc(S("h_ready"), 1)
                if g + 2 < SUBS:
                    ada_out(g + 2, 0)

            def out_hi(g, src, k, TN):
                act.activation(uhv[:, k, 0:TN], src[:, 0:TN], ACT.Copy).then_inc(S("u_hi"), 1)

            def even_mixer():
                for i in range(ZT):
                    if i and i % 2 == 0 and i // 2 + 1 < 14:
                        hi("even_in", 1, i // 2 + 1, half_src("even_in", 1, i // 2 + 1, 0))
                    act.wait_ge(S("z_psum"), i + 1)
                    act.activation(bigt[:, i], bank[i % 8], ACT.Identity, scale=cfv[:, i, 1:2], bias=cfv[:, i, 3:4])\
                       .then_inc(S("z_main"), 1)
                act.wait_ge(S("z_done"), ZT)
                load("ld_dft", dft.rearrange("p a f -> p (a f)"), K["k_dft"])
                load("ld_dft", idft.rearrange("p f t -> p (f t)"), K["k_idft"])
                load("ld_lora", w_up, A["rw_w_up"].rearrange("e d l n -> (e d l) n"))
                load("ld_lora", a_up, A["rw_a_up"].rearrange("e d l n -> (e d l) n"))
                load("ld_lora", g_up, A["rw_g_up"][0])
                act.activation(bigt[:, 24], bigt[:, 24], ACT.Tanh).then_inc(S("lora_in"), 1)
                act.activation(bigt[:, 26], bigt[:, 26], ACT.Sigmoid).then_inc(S("lora_in"), 1)
                for b in range(4):
                    act.wait_ge(S("hy_turned"), 2 * b + 1)
                    act.activation(vtok[:, b], bank[2 * b], ACT.Copy).then_inc(S("vtok"), 1)
                    act.wait_ge(S("hy_turned"), 2 * b + 2)
                    act.activation(x1tok[:, b], bank[2 * b + 1], ACT.Copy).then_inc(S("vtok"), 1)
                act.wait_ge(S("hy_done"), 4)
                for q in range(20):
                    act.wait_ge(S("lora_psum"), q + 1)
                    if q < 8:
                        act.activation(sgw[q // 4][:, (q % 4) * NT:(q % 4 + 1) * NT], bank[q % 8], ACT.Sigmoid,
                                       bias=col("w0", q)).then_inc(S("lora_out"), 1)
                    elif q < 16:
                        e = q - 8
                        act.activation(aa[e // 4][:, (e % 4) * NT:(e % 4 + 1) * NT], bank[q % 8], ACT.Sigmoid,
                                       bias=col("a0", e)).then_inc(S("lora_out"), 1)
                    else:
                        e = q - 16
                        act.activation(gate[:, e * NT:(e + 1) * NT], bank[q % 8], ACT.Copy)\
                           .then_inc(S("lora_out"), 1)
                act.wait_ge(S("kk_raw"), 1)
                act.activation(prep, kk, ACT.Square).then_inc(S("kk_sq"), 1)
                for i in range(4):
                    act.wait_ge(S("kk_sum"), i + 1)
                    act.activation(prep2[:, i * NT:(i + 1) * NT], bank[i], ACT.Sqrt).then_inc(S("kk_norm"), 1)
                for b in range(4):
                    act.wait_ge(S("v_turned"), b + 1)
                    act.activation(vt[:, b], bank[4 + b], ACT.Copy).then_inc(S("vt"), 1)
                def decays_of(j):
                    for d in range(2):
                        if j:
                            act.wait_ge(S("slots"), 2 * j + d - 1)
                            act.wait_ge(S("slots_r"), 2 * j + d - 1)
                        ch = chunk_of(d, j)
                        cs = three(sgw[d])[:, :, ch * P:(ch + 1) * P]
                        hf_ = half[:, d, :, ch:ch + 1]
                        recv, read, key = decays[d]
                        if d == 0:
                            act.activation(recv[:, :, 1:P], cs[:, :, 0:P - 1], ACT.Exp, scale=-DECAY)
                            act.activation(recv[:, :, 0:1], hf_, ACT.Exp, scale=DECAY)
                            act.activation(read, cs, ACT.Exp, scale=-DECAY)
                            act.activation(key, cs, ACT.Exp, scale=DECAY).then_inc(S("exped"), 1)
                        else:
                            act.activation(recv, cs, ACT.Exp, scale=DECAY)
                            act.activation(read[:, :, 1:P], cs[:, :, 0:P - 1], ACT.Exp, scale=DECAY)
                            act.activation(read[:, :, 0:1], hf_, ACT.Exp, scale=-DECAY)
                            act.activation(key[:, :, 1:P], cs[:, :, 0:P - 1], ACT.Exp, scale=-DECAY)
                            act.activation(key[:, :, 0:1], hf_, ACT.Exp, scale=DECAY).then_inc(S("exped"), 1)

                act.wait_ge(S("sums"), 1)
                act.activation(small[:, 96:128], small[:, 64:96], ACT.Exp, scale=-DECAY).then_inc(S("edec"), 1)
                decays_of(0)
                for j in range(4):
                    for hf in range(2):
                        gi = 2 * j + hf
                        if hf == 0 and j < 3:
                            decays_of(j + 1)
                        for lv in range(1, LEVELS):
                            m = 1 << lv
                            for d in range(2):
                                act.wait_ge(S("z_mm"), 2 * (LEVELS * gi + lv) + d + 1)
                                act.activation(blocks(zs[:, d].rearrange("p h t -> p (h t)"), m, d),
                                               packed(bank[d][:, 0:2 * P], m), ACT.Copy).then_inc(S("zs"), 1)
                            if hf == 0 and lv in (2, 4):
                                d = lv // 2 - 1
                                for q in range(2):
                                    act.wait_ge(S("bk_turned"), 4 * j + 2 * d + q + 1)
                                    act.activation(bkt[:, d, q], bank[6 + q], ACT.Copy).then_inc(S("bkt"), 1)
                        for d in range(2):
                            act.wait_ge(S("x_mm"), 2 * gi + d + 1)
                            for q in range(2):
                                dst = xs[:, d, 0].rearrange("p (c q) v -> p q c v", q=2)[:, q]
                                ins = act.activation(dst, bank[2 * d + q][:, 0:128].rearrange("p (c v) -> p c v", c=2),
                                                     ACT.Copy)
                            ins.then_inc(S("xs"), 1)
                act.wait_ge(S("state_new"), 16)
                for k in range(CT):
                    out_hi(1, yhy[:, k], k, NT)
                for i in range(4):
                    at = slice(i * NT, (i + 1) * NT)
                    act.wait_ge(S("gn_centred"), i + 1)
                    act.activation(gn_sq[:, at], oacc[:, at], ACT.Square).then_inc(S("gn_sq"), 1)
                for i in range(4):
                    act.wait_ge(S("gn_var"), i + 1)
                    act.activation(gn_rstd[:, i * NT:(i + 1) * NT], bank[4 + i], ACT.Ln, scale=1 / 64.0,
                                   bias=eps[:, 2:3]).then_inc(S("gn_ln"), 1)
                for i in range(4):
                    at = slice(i * NT, (i + 1) * NT)
                    act.wait_ge(S("gn_ln"), i + 1)
                    act.activation(gn_rstd[:, at], gn_rstd[:, at], ACT.Exp, scale=-0.5).then_inc(S("gn_rstd"), 1)
                for q in range(2):
                    hi("even_out", 1, q, half_src("even_out", 1, q, 0))
                for k in range(CT, KT):
                    act.wait_ge(S("mixed"), k - CT + 1)
                    out_hi(1, three(oacc)[:, k - CT], k, NT)
                for q in range(2, 4):
                    hi("even_out", 1, q, half_src("even_out", 1, q, 0))

            def odd_mixer():
                act.wait_ge(S("gup_zero"), 1)
                load("ld_gla", gup[0:16, 0, :], A["gla_g_up"][0, 0])
                load("ld_gla", gup[16:32, 1, :], A["gla_g_up"][0, 1])
                load("ld_gla", greset, K["k_reset"])
                for i, (q, kind, j) in enumerate(OD_TILES):
                    if i and q > OD_TILES[i - 1][0] and q + 1 < OD_HALVES:
                        hi("odd_in", 4, q + 1, half_src("odd_in", 4, q + 1, 0))
                    act.wait_ge(S("z1_psum"), i + 1)
                    if kind == "k":
                        ins = act.activation(gk[:, j], bank[i % 8], ACT.Copy)
                    elif kind == "gd":
                        ins = act.activation(ggd, bank[i % 8][0:32], ACT.Copy)
                    elif kind == "q":
                        ins = act.activation(gq[:, j], bank[i % 8][:, 0:SEG], ACT.Copy)
                    elif kind == "v":
                        ins = act.activation(gvt[:, j % 4, (j // 4) * SEG:(j // 4 + 1) * SEG], bank[i % 8][:, 0:SEG],
                                             ACT.Copy)
                    else:
                        ins = act.activation(gog[:, j], bank[i % 8][:, 0:SEG], ACT.Silu)
                    ins.then_inc(S("z1_done"), 1)
                for q in range(8):
                    d, c = q // 4, q % 4
                    act.wait_ge(S("lg_psum"), q + 1)
                    act.activation(gcs[:, d, c], bank[q], ACT.Abs, bias=col("gla_b", q)).then_inc(S("lg_abs"), 1)
                act.wait_ge(S("lg_abs"), 8)
                act.activation(arena[:, 16384:20480], arena[:, 16384:20480], ACT.Exp, scale=-1.0).then_inc(S("lg_exp"), 1)
                act.wait_ge(S("lg_exp"), 1)
                act.activation(arena[:, 16384:20480], arena[:, 16384:20480], ACT.Ln, bias=eps[:, 3:4]).then_inc(S("lg_ln"), 1)
                act.wait_ge(S("ctx_arg"), 1)
                act.activation(kout.rearrange("p d c t -> p (d c t)"), kout.rearrange("p d c t -> p (d c t)"),
                               ACT.Exp, scale=1 / GLA_N).then_inc(S("ctx_exp"), 1)
                act.wait_ge(S("lat_arg"), 1)
                fl = lambda x: x.rearrange("p c t -> p (c t)")
                act.activation(gexp.rearrange("p d c n -> p (d c n)"), ghalf.rearrange("p d c n -> p (d c n)"),
                               ACT.Exp, scale=1 / GLA_N)
                act.activation(fl(qh[:, 0]), fl(sq2[:, 0:4]), ACT.Exp, scale=1 / GLA_N)
                act.activation(fl(kh[:, 0]), fl(sq2[:, 0:4]), ACT.Exp, scale=-1 / GLA_N)
                act.activation(fl(qh[:, 1]), fl(sq2[:, 4:8]), ACT.Exp, scale=-1 / GLA_N)
                act.activation(fl(kh[:, 1]), fl(sq2[:, 4:8]), ACT.Exp, scale=1 / GLA_N).then_inc(S("lat_exp"), 1)
                for q in range(4):
                    act.wait_ge(S("ko_turned"), q + 1)
                    act.activation(kot[:, q // 2, q % 2], bank[q], ACT.Copy).then_inc(S("kot"), 1)
                for q in range(4):
                    act.wait_ge(S("kh_turned"), q + 1)
                    act.activation(kht[:, q // 2, q % 2], bank[4 + q], ACT.Copy).then_inc(S("kht"), 1)
                for b in range(2):
                    act.wait_ge(S("go_done"), 2 * b + 2)
                    act.activation(sq2[:, 4 * b:4 * b + 4].rearrange("p c t -> p (c t)"),
                                   go[:, 4 * b:4 * b + 4].rearrange("p c t -> p (c t)"), ACT.Square)\
                       .then_inc(S("go_sq"), 1)
                for i in range(2):
                    act.wait_ge(S("go_sum"), i + 1)
                    act.activation(grs[:, 2 * i:2 * i + 2].rearrange("p c t -> p (c t)"), bank[i], ACT.Ln,
                                   scale=1.0 / HV, bias=eps[:, 1:2]).then_inc(S("go_ln"), 1)
                for i in range(2):
                    act.wait_ge(S("go_ln"), i + 1)
                    r_ = grs[:, 2 * i:2 * i + 2].rearrange("p c t -> p (c t)")
                    act.activation(r_, r_, ACT.Exp, scale=-0.5).then_inc(S("go_rstd"), 1)
                for q in range(2):
                    hi("odd_out", 4, q, half_src("odd_out", 4, q, 0))
                for k in range(KT):
                    act.wait_ge(S("mixed"), CT + 1 + k // 4)
                    out_hi(4, go[:, k], k, SEG)
                for q in range(2, 4):
                    hi("odd_out", 4, q, half_src("odd_out", 4, q, 0))

            for g in range(SUBS):
                u_round(g)
                if 1 <= g < SUBS - 1:
                    for c in range(1, 6):
                        ada_out(g + 1, c)
                if g == 1:
                    even_mixer()
                elif g == 4:
                    odd_mixer()
                else:
                    ffn_silu(g)
                norm(g)
            for i in range(4):
                act.wait_ge(S("out_turned"), i + 1)
                act.activation(big[:, i * 512:(i + 1) * 512], bank[i], ACT.Copy).then_inc(S("rows_out"), 1)

        @block.tensor
        def _(pe):
            def mm(dst, w, x, first_, last):
                return pe.matmul(dst, w, x, start=first_, stop=last, skip_group_check=True)

            pe.wait_ge(S("ld_ident"), 16)
            pe.wait_ge(S("ld_par"), 16 * 18)
            for i, n in enumerate((120, 120, 125)):
                ins = pe.transpose(bank[0][:, i * P:i * P + n], stage[i][0:n, :], ident[0:n, 0:n])
            ins.then_inc(S("par_turned"), 1)
            pe.wait_ge(S("ld_tok"), 64)
            for k in range(KT):
                if k == KT - 1:
                    pe.wait_ge(S("par_done"), 1)
                for b in range(4):
                    ins = pe.transpose(bank[(k + 1) % 8][:, b * P:(b + 1) * P], tok_in[:, b, k * P:(k + 1) * P],
                                       ident[:, :])
                ins.then_inc(S("tok_turned"), 1)

            def mm3(dst, wh, wl, xh, xl, first_, last):
                mm(dst, wh, xh, first_, False)
                mm(dst, wh, xl, False, False)
                return mm(dst, wl, xh, False, last)

            def ada(g, part):
                for c in part:
                    n = chunks["ada", g][c]
                    pe.wait_ge(S(f"slot{n % R}"), arrival[n])
                    if c >= 2 or (g == 1 and c):
                        pe.wait_ge(S("ada_row"), 6 * g + c - (g != 1))
                    w = slot(n).rearrange("p (k n) -> p k n", k=KT)
                    for k in range(KT):
                        ins = mm(row_bank(g, c)[0:2], sc[:, 2 * k:2 * k + 2], w[:, k], k == 0, k == KT - 1)
                    ins.then_inc(S("ada_used"), 1)

            def ada_turn(g):
                pe.wait_ge(S("ada_row"), 6 * (g + 1))
                for t in range(24):
                    ins = pe.transpose(bank[4][:, 2 * t:2 * t + 2], ada_row(g, t // 4)[:, t % 4 * P:(t % 4 + 1) * P],
                                       ident[0:2, 0:2])
                ins.then_inc(S("ada_turned"), 1)

            def taps_of(o):
                pe.wait_ge(S("taps_free"), o + 1)
                for dr in range(2):
                    for a in range(2):
                        ins = mm(bank[4 + 2 * dr + a], h2[:, a * P:(a + 1) * P],
                                 w3[:, (2 * o + dr) * HW:(2 * o + dr + 1) * HW], True, True)
                ins.then_inc(S("filt_taps"), 1)

            def response_of(o):
                pe.wait_ge(S("taps"), o + 1)
                if o:
                    pe.wait_ge(S("kf_done"), 6 * o)
                for a in range(2):
                    st, en = a == 0, a == 1
                    mm(bank[0], dft[:, a, 0:P], taps[:, 0, a], st, en)
                    mm(bank[1], dft[:, a, P:2 * P], taps[:, 0, a], st, en)
                    mm(bank[3], sin0[:, a], tap_m[:, a], st, en)
                    mm(bank[4], dft[:, a, 3 * P:4 * P], tap_m[:, a], st, en)
                    ins = mm(bank[5][0:1], dft[:, a, 2 * P:2 * P + 1], taps[:, 0, a], st, en)
                ins.then_inc(S("filt_dft"), 1)

            pe.wait_ge(S("h_ready"), KT)
            pe.wait_ge(S("ld_filt"), 16 * 12)
            mm(bank[6][0:HY_FO, 0:SEG], fw1, zT, True, True).then_inc(S("filt_mm"), 1)
            pe.wait_ge(S("sc_ready"), 1)
            ada(0, (0, 1))
            pe.wait_ge(S("sin_done"), 1)
            mm(bank[7][0:HY_FO, 0:SEG], fw2, h1, True, True).then_inc(S("filt_mm"), 1)
            ada(0, (2, 3))
            pe.wait_ge(S("sin_done"), 2)
            ada(0, (4, 5))
            ada_turn(0)
            pe.wait_ge(S("mods"), 1)
            taps_of(0)
            ada(1, (0,))
            response_of(0)
            ada(1, (1, 2))
            taps_of(1)
            ada(1, (3,))
            response_of(1)
            ada(1, (4, 5))
            pe.wait_ge(S("kf_done"), 12)
            ada_turn(1)
            pe.wait_ge(S("ld_const"), 64)

            def ffn(g):
                f = FFN.index(g)
                T0, TN = (0, NT) if g < 5 else (SEG, SEG)
                pe.wait_ge(S("u_lo"), U_BASE[g] + KT)

                def up_half(par, buf, hq1, ft1):
                    pe.wait_ge(S("lo_done"), hq1)
                    pe.wait_ge(S("pairs_free"), ft1)
                    wh = split_hi(buf).rearrange("p (a k f) -> p a k f", a=2, k=KT)
                    wl = split_lo(buf).rearrange("p (a k f) -> p a k f", a=2, k=KT)
                    for a in range(2):
                        for k in range(KT):
                            ins = mm3(bank[2 * par + a][:, 0:TN], wh[:, a, k], wl[:, a, k], uhv[:, k, T0:NT],
                                      ulv[:, k, T0:NT], k == 0, k == KT - 1)
                    ins.then_inc(S("gu_ready"), 1)
                    pe.wait_ge(S("gu_ready"), ft1)
                    pe.sem_inc(S("split_used"), 1)

                for up, down, t0, t1 in (("up_a", "down_a", 0, FA), ("up_b", "down_b", FA, FT)):
                    with pe.Fori(0, (t1 - t0) // 2) as it:
                        for par in range(2):
                            up_half(par, half0[up, g] + par, it * 2 + (half0[up, g] + par + 1), it * 2 + (FT * f + t0 + par + 1))
                    pe.wait_ge(S("hid"), FT * f + t1)
                    if t0 == 0 and g + 1 < SUBS:
                        pe.wait_ge(S("mods"), g + 2)
                    if t0:
                        pe.wait_ge(S("y_part"), KT * (f + 1))
                    kt = t0
                    for q in range(2 * -(-(t1 - t0) // 4)):
                        m = min(4, t1 - t0 - 4 * (q // 2)) // 2
                        hq = half0[down, g] + q
                        pe.wait_ge(S("lo_done"), hq + 1)
                        wh = split_hi(hq)[:, 0:m * D].rearrange("p (k d) -> p k d", k=m)
                        wl = split_lo(hq)[:, 0:m * D].rearrange("p (k d) -> p k d", k=m)
                        for j in range(m):
                            for t in range(KT):
                                ins = mm3(bank[t][:, 0:TN], wh[:, j, t * P:(t + 1) * P], wl[:, j, t * P:(t + 1) * P],
                                          hidh[:, kt - t0, 0:TN], hidl[:, kt - t0, 0:TN], kt == t0, kt == t1 - 1)
                                if kt == t1 - 1:
                                    ins.then_inc(S("y_done" if t0 else "y_half"), 1)
                            kt += 1
                        if kt == t1:
                            pe.wait_ge(S("y_done" if t0 else "y_half"), KT * (g + 1) if t0 else KT * (f + 1))
                            pe.sem_inc(S("split_used"), 1)
                        else:
                            ins.then_inc(S("split_used"), 1)
                    if t0 == 0:
                        pe.wait_ge(S("y_part"), KT * f + 4)

            def norm(g):
                T0, TN = (0, NT) if g < 4 else (SEG, SEG)
                for k in range(KT):
                    pe.wait_ge(S("resid"), resid_base[g] + len(segments(g)) * (k + 1))
                    ins = mm(bank[0][:, 0:TN], mean_w[:, :], hv[:, k, T0:NT], k == 0, k == KT - 1)
                ins.then_inc(S("mean"), 1)
                for k in range(KT):
                    pe.wait_ge(S("sq"), KT * g + k + 1)
                    mm(bank[1][:, 0:TN], mean_w[:, :], tmp[:, (k % 2) * NT:(k % 2) * NT + TN], k == 0,
                       k == KT - 1).then_inc(S("sq_used"), 1)
                if g + 2 < SUBS:
                    ada(g + 2, range(6))
                    ada_turn(g + 2)

            def project_out(g, phase, TN):
                for q in range(4):
                    hq = half0[phase, g] + q
                    pe.wait_ge(S("lo_done"), hq + 1)
                    wh = split_hi(hq).rearrange("p (k n) -> p k n", k=KT)
                    wl = split_lo(hq).rearrange("p (k n) -> p k n", k=KT)
                    for j in range(2):
                        for k in range(KT):
                            if q == 0 and j == 0:
                                pe.wait_ge(S("u_lo"), U_BASE[g] + KT + k + 1)
                            ins = mm3(bank[2 * q + j][:, 0:TN], wh[:, k, j * P:(j + 1) * P],
                                      wl[:, k, j * P:(j + 1) * P], uhv[:, k, 0:TN], ulv[:, k, 0:TN],
                                      k == 0, k == KT - 1)
                        ins.then_inc(S("y_done"), 1)
                    pe.wait_ge(S("y_done"), KT * g + 2 * (q + 1))
                    pe.sem_inc(S("split_used"), 1)

            def even_mixer():
                pe.wait_ge(S("u_lo"), U_BASE[1] + KT)
                for q in range(14):
                    hq = half0["even_in", 1] + q
                    if q == 2:
                        pe.wait_ge(S("mods"), 3)
                    pe.wait_ge(S("lo_done"), hq + 1)
                    m = min(2, ZT - 2 * q)
                    wh = split_hi(hq)[:, 0:KT * m * P].rearrange("p (k n) -> p k n", k=KT)
                    wl = split_lo(hq)[:, 0:KT * m * P].rearrange("p (k n) -> p k n", k=KT)
                    for i in range(2 * q, 2 * q + m):
                        at = (i % 2) * P
                        if i >= 8:
                            pe.wait_ge(S("z_done"), i - 7)
                        for k in range(KT):
                            ins = mm3(bank[i % 8], wh[:, k, at:at + P], wl[:, k, at:at + P], uhv[:, k], ulv[:, k],
                                      k == 0, k == KT - 1)
                        ins.then_inc(S("z_psum"), 1)
                    pe.wait_ge(S("z_psum"), i + 1)
                    pe.sem_inc(S("split_used"), 1)
                pe.wait_ge(S("z_done"), ZT)
                for b in range(4):
                    for q in range(2):
                        for c in range(CT):
                            ins = pe.transpose(bank[2 * b + q][:, c * P:(c + 1) * P],
                                               bigt[:, 4 * q + c, b * P:(b + 1) * P], ident[:, :])
                        ins.then_inc(S("hy_turned"), 1)
                pe.wait_ge(S("ld_dft"), 32)
                pe.wait_ge(S("vtok"), 8)
                for o in range(2):
                    for s in range(2):
                        if o:
                            pe.wait_ge(S("hy_y1"), 2 * s + 2)
                        for i in range(4):
                            for a in range(2):
                                ins = mm(bank[4 * s + i], dft[:, a, i * P:(i + 1) * P], vtok[:, 2 * s + a],
                                         a == 0, a == 1)
                        ins.then_inc(S("hy_f"), 1)
                    for s in range(2):
                        pe.wait_ge(S("hy_mul"), 2 * o + s + 1)
                        if o == 0:
                            for a in range(2):
                                for i in range(4):
                                    ins = mm(bank[4 * s + a], idft[:, i, a * P:(a + 1) * P], yf[:, s, i],
                                             i == 0, i == 3)
                        else:
                            for c in range(CT):
                                for i in range(4):
                                    ins = mm(bank[4 * s + c // 2][:, (c % 2) * SEG:(c % 2 + 1) * SEG],
                                             yf[:, s, i, c * P:(c + 1) * P], idft[:, i], i == 0, i == 3)
                        ins.then_inc(S("hy_i"), 1)
                pe.wait_ge(S("hy_done"), 4)
                pe.wait_ge(S("lora_in"), 2)
                pe.wait_ge(S("ld_lora"), 48)
                for q in range(20):
                    if q >= 8:
                        pe.wait_ge(S("lora_out"), q - 7)
                    d, c = q // 4, q % 4
                    lo = 64 * (d % 2)
                    if q < 16:
                        w = (w_up if q < 8 else a_up)[lo:lo + 64, c * P:(c + 1) * P]
                        x = bigt[lo:lo + 64, 24 if q < 8 else 25]
                    else:
                        w, x = g_up[:, c * P:(c + 1) * P], bigt[:, 26]
                    mm(bank[q % 8], w, x, True, True).then_inc(S("lora_psum"), 1)
                pe.wait_ge(S("lora_out"), 20)
                pe.wait_ge(S("kk_sq"), 1)
                for i in range(4):
                    mm(bank[i], blk[:, :], prep[:, i * NT:(i + 1) * NT], True, True).then_inc(S("kk_sum"), 1)
                for b in range(4):
                    for c in range(CT):
                        ins = pe.transpose(bank[4 + b][:, c * P:(c + 1) * P], zv[:, c * NT + b * P:c * NT + (b + 1) * P],
                                           ident[:, :])
                    ins.then_inc(S("v_turned"), 1)
                pe.wait_ge(S("bonus_in"), 1)
                pe.wait_ge(S("kk_norm"), 4)
                for i in range(4):
                    mm(bank[i], blk[:, :], bonus[:, i * NT:(i + 1) * NT], True, True).then_inc(S("bonus_sum"), 1)
                pe.wait_ge(S("vt"), 4)
                pe.wait_ge(S("prepared"), 1)
                pe.wait_ge(S("zeroed"), 1)
                for j in range(4):
                    for hf in range(2):
                        gi = 2 * j + hf
                        for d in range(2):
                            if hf == 0:
                                pe.wait_ge(S("slots"), 2 * j + d + 1)
                                pe.wait_ge(S("slots_r"), 2 * j + d + 1)
                            if d and gi:
                                pe.wait_ge(S("o_add"), 4 * gi)
                                pe.wait_ge(S("state_new"), 2 * gi)
                            for cc in range(2):
                                for q in range(2):
                                    mm(bank[n_bank(d, cc, q)], bk[:, d, 2 * hf + cc, q],
                                       ar[:, d, 2 * hf + cc].rearrange("p e a t -> p (e a t)"), True, True)\
                                        .then_inc(S("n_mm"), 1)
                        for lv in range(LEVELS):
                            m = 1 << lv
                            for d in range(2):
                                if lv == 0:
                                    pe.wait_ge(S("n_done"), 8 * gi + 8)
                                else:
                                    pe.wait_ge(S("tu"), (2 * (gi * LEVELS + lv - 1) + d + 1) * 2)
                                for hh in range(4):
                                    ins = mm(packed(bank[d][:, hh * 64:(hh + 1) * 64], m), nm[:, d, hh, 0],
                                             blocks(ident[:, :] if lv == 0 else tu[:, d, 0, hh], m, d), True, True)
                                ins.then_inc(S("z_mm"), 1)
                            if lv == 0:
                                continue
                            for d in range(2):
                                pe.wait_ge(S("zs"), 2 * (gi * (LEVELS - 1) + lv - 1) + d + 1)
                                if lv < LEVELS - 1:
                                    for hh in range(4):
                                        mm(packed(bank[2 + d][:, hh * 64:(hh + 1) * 64], m), tu[:, d, 1, hh],
                                           blocks(zs[:, d, hh], m, d), True, True)
                                for hh in range(4):
                                    ins = mm(packed(bank[4 + d][:, hh * 64:(hh + 1) * 64], m), zs[:, d, hh],
                                             blocks(tu[:, d, 1, hh], m, 1 - d), True, True)
                                ins.then_inc(S("d_mm"), 1)
                            if hf == 0 and lv in (1, 3):
                                d = lv // 2
                                if d:
                                    pe.wait_ge(S("bkt"), 4 * j + 2)
                                for q in range(2):
                                    for c in range(CT):
                                        ins = pe.transpose(bank[6 + q][:, c * P:(c + 1) * P], bk[:, d, c, q],
                                                           ident[:, :])
                                    ins.then_inc(S("bk_turned"), 1)
                        vcol = lambda hh: (4 * hf + hh) * 64
                        for d in range(2):
                            pe.wait_ge(S("tu"), 2 * LEVELS * 2 * (gi + 1))
                            ch = chunk_of(d, j)
                            if hf == 0 and d == 0:
                                pe.wait_ge(S("state_in"), 2 * (j + 1))
                            for hh in range(4):
                                c = 2 * hf + hh // 2
                                dst = bank[2 * d + hh % 2][:, (hh // 2) * 64:(hh // 2 + 1) * 64]
                                mm(dst, ar[:, d, c, hh % 2, 0], state[:, d, c], True, False)
                                ins = mm(dst, nm[:, d, hh, 2], vt[:, ch, vcol(hh):vcol(hh) + 64], False, True)
                            ins.then_inc(S("x_mm"), 1)
                        for d in range(2):
                            pe.wait_ge(S("xs"), 2 * gi + d + 1)
                            for hh in range(4):
                                ins = mm(bank[4 + d][:, hh * 64:(hh + 1) * 64], tu[:, d, 1, hh], xs[:, d, 0, hh],
                                         True, True)
                            ins.then_inc(S("sa_mm"), 1)
                        pe.wait_ge(S("bkt"), 4 * (j + 1))
                        for d in range(2):
                            pe.wait_ge(S("sa"), 2 * gi + d + 1)
                            ch = chunk_of(d, j)
                            for hh in range(4):
                                c, lo = 2 * hf + hh // 2, 64 * (hh % 2)
                                v = vt[:, ch, vcol(hh):vcol(hh) + 64]
                                dst = bank[6 + hh % 2][lo:lo + 64, (2 * d + hh // 2) * P:(2 * d + hh // 2 + 1) * P]
                                mm(dst, xs[:, d, 1, hh], nm[:, d, hh, 1], True, False)
                                mm(dst, v, nm[:, d, hh, 3], False, False)
                                mm(dst, state[:, d, c], ar[:, d, c, hh % 2, 1], False, True)
                                dst = bank[d][lo:lo + 64, (hh // 2) * 64:(hh // 2 + 1) * 64]
                                mm(dst, bkt[:, d, 0, vcol(hh):vcol(hh) + 64], xs[:, d, 1, hh], True, False)
                                ins = mm(dst, bkt[:, d, 1, vcol(hh):vcol(hh) + 64], v, False, True)
                            ins.then_inc(S("os_mm"), 1)
                pe.wait_ge(S("o_add"), 32)
                pe.wait_ge(S("state_new"), 16)
                for i in range(4):
                    mm(bank[i], blk[:, :], oacc[:, i * NT:(i + 1) * NT], True, True).then_inc(S("gn_mean"), 1)
                for i in range(4):
                    pe.wait_ge(S("gn_sq"), i + 1)
                    mm(bank[4 + i], blk[:, :], gn_sq[:, i * NT:(i + 1) * NT], True, True).then_inc(S("gn_var"), 1)
                project_out(1, "even_out", NT)

            def odd_mixer():
                pe.wait_ge(S("u_lo"), U_BASE[4] + KT)
                for i, (q, kind, j) in enumerate(OD_TILES):
                    hq = half0["odd_in", 4] + q
                    new, last = i == 0 or OD_TILES[i - 1][0] < q, i + 1 == len(OD_TILES) or OD_TILES[i + 1][0] > q
                    if new:
                        pe.wait_ge(S("lo_done"), hq + 1)
                    if i == 4:
                        pe.wait_ge(S("mods"), 6)
                    if i >= 8:
                        pe.wait_ge(S("z1_done"), i - 7)
                    cols = P if kind == "gd" else 2 * P
                    wh = split_hi(hq)[:, 0:KT * cols].rearrange("p (k n) -> p k n", k=KT)
                    wl = split_lo(hq)[:, 0:KT * cols].rearrange("p (k n) -> p k n", k=KT)
                    for k in range(KT):
                        st, en = k == 0, k == KT - 1
                        at = 0 if kind == "gd" else (j % 2) * P
                        w2 = wh[:, k, at:at + P], wl[:, k, at:at + P]
                        if kind == "v":
                            tok = slice((j % 4) * P, (j % 4 + 1) * P)
                            ins = mm3(bank[i % 8][:, 0:SEG], uhv[:, k, tok], ulv[:, k, tok], wh[:, k], wl[:, k], st, en)
                        elif kind in ("k", "gd"):
                            ins = mm3(bank[i % 8], *w2, uhv[:, k], ulv[:, k], st, en)
                        else:
                            ins = mm3(bank[i % 8][:, 0:SEG], *w2, uhv[:, k, SEG:NT], ulv[:, k, SEG:NT], st, en)
                    ins.then_inc(S("z1_psum"), 1)
                    if last:
                        pe.wait_ge(S("z1_psum"), i + 1)
                        pe.sem_inc(S("split_used"), 1)
                pe.wait_ge(S("z1_done"), len(OD_TILES))
                pe.wait_ge(S("ld_gla"), 48)
                for q in range(8):
                    mm(bank[q], gup[:, q // 4, (q % 4) * P:(q % 4 + 1) * P], ggd, True, True)\
                        .then_inc(S("lg_psum"), 1)
                pe.wait_ge(S("kout"), 1)
                for q in range(4):
                    for c in range(4):
                        ins = pe.transpose(bank[q][:, c * P:(c + 1) * P], kout[:, q // 2, c, (q % 2) * P:(q % 2 + 1) * P],
                                           ident[:, :])
                    ins.then_inc(S("ko_turned"), 1)
                pe.wait_ge(S("lat_in"), 1)
                for q in range(4):
                    for c in range(4):
                        ins = pe.transpose(bank[4 + q][:, c * P:(c + 1) * P], kh[:, q // 2, c, (q % 2) * P:(q % 2 + 1) * P],
                                           ident[:, :])
                    ins.then_inc(S("kh_turned"), 1)
                pe.wait_ge(S("kot"), 4)
                for d in range(2):
                    for c in range(4):
                        for b in range(2):
                            ins = mm(bank[2 * d + c // 2][:, (c % 2) * HV:(c % 2 + 1) * HV],
                                     kot[:, d, b, c * P:(c + 1) * P], gvt[:, b, c * HV:(c + 1) * HV], b == 0, b == 1)
                ins.then_inc(S("gs_mm"), 1)
                pe.wait_ge(S("kht"), 4)
                for d in range(2):
                    for b in range(2):
                        for c in range(4):
                            ins = mm(bank[4 + 2 * d + b][:, c * P:(c + 1) * P], kh[:, d, c, b * P:(b + 1) * P],
                                     qh[:, d, c, b * P:(b + 1) * P], True, True)
                        ins.then_inc(S("sc_mm"), 1)
                pe.wait_ge(S("pm"), 4)
                for n in range(3):
                    pe.wait_ge(S("gst"), n + 1)
                    for d in range(2):
                        ch = XCHUNK(d, n)
                        lo = 64 * (ch % 2)
                        for c in range(4):
                            ins = mm(bank[4 * ((n + 1) % 2) + 2 * d + c // 2][:, (c % 2) * HV:(c % 2 + 1) * HV],
                                     kht[lo:lo + 64, d, ch // 2, c * P:(c + 1) * P],
                                     gvt[lo:lo + 64, 2 + ch // 2, c * HV:(c + 1) * HV], True, True)
                    ins.then_inc(S("gs_mm"), 1)
                pe.wait_ge(S("gst"), 4)
                pe.wait_ge(S("pm"), 5)
                for vt_ in range(8):
                    c, at = vt_ // 2, vt_ * P
                    dst = bank[vt_ // 2][:, (vt_ % 2) * SEG:(vt_ % 2 + 1) * SEG]
                    for b in range(2):
                        mm(dst[:, b * P:(b + 1) * P], gvt[:, 2 + b, at:at + P], pm[:, 0, b, c], True, False)
                        for ch in (2 * b, 2 * b + 1):
                            for d in range(2):
                                ins = mm(dst[:, 64 * ch:64 * ch + 64],
                                         gst[:, d, ch if d == 0 else 3 - ch, c, (vt_ % 2) * P:(vt_ % 2 + 1) * P],
                                         qh[:, d, c, 64 * ch:64 * ch + 64], False, ch % 2 == 1 and d == 1)
                    if vt_ % 2:
                        ins.then_inc(S("go_mm"), 1)
                for c in range(4):
                    pe.wait_ge(S("go_sq"), c // 2 + 1)
                    for i_ in range(2):
                        ins = mm(bank[c // 2][:, (c % 2) * SEG:(c % 2 + 1) * SEG], ones[:, :], sq2[:, 2 * c + i_],
                                 i_ == 0, i_ == 1)
                    if c % 2:
                        ins.then_inc(S("go_sum"), 1)
                project_out(4, "odd_out", SEG)

            for g in range(SUBS):
                if g == 1:
                    even_mixer()
                elif g == 4:
                    odd_mixer()
                else:
                    ffn(g)
                norm(g)
            pe.wait_ge(S("h_ready"), KT * (SUBS + 1))
            for b in range(2):
                for q in range(2):
                    for c in range(4):
                        k = 4 * q + c
                        ins = pe.transpose(bank[2 * b + q][:, c * P:(c + 1) * P],
                                           hv[:, k, SEG + b * P:SEG + (b + 1) * P], ident[:, :])
                    ins.then_inc(S("out_turned"), 1)

        @block.vector
        def _(ve):
            v = Count()

            for i, val in enumerate((LN_EPS, GLA_EPS, GN_EPS, 1.0)):
                ve.memset(eps[:, i:i + 1], val).then_inc(S("ve_steps"), v.step())
            ve.wait_ge(S("ve_steps"), v.n)
            ve.wait_ge(S("par_turned"), 1)
            for i, n in enumerate((120, 120, 125)):
                ve.tensor_copy(par[:, i * P:i * P + n], bank[0][:, i * P:i * P + n]).then_inc(S("ve_steps"), v.step())
            ve.wait_ge(S("ve_steps"), v.n)
            ve.tensor_copy(cfv[:, 0:12, 0:3].rearrange("p i j -> p j i"),
                                 par[:, PAR["conv_w"]:PAR["conv_w"] + 36].rearrange("p (j i) -> p j i", j=3)).then_inc(S("ve_steps"), v.step())
            ve.tensor_copy(cfv[:, 0:12, 3], par[:, PAR["conv_b"]:PAR["conv_b"] + 12]).then_inc(S("ve_steps"), v.step())
            mu = par[:, PAR["mu"]:PAR["mu"] + 15]
            ve.tensor_scalar(cfv[:, 12:27, 0], mu, 0.5, None, ALU.mult).then_inc(S("ve_steps"), v.step())
            ve.tensor_scalar(cfv[:, 12:27, 2], mu, 0.5, None, ALU.mult).then_inc(S("ve_steps"), v.step())
            ve.tensor_scalar(cfv[:, 12:27, 1], mu, -1.0, 1.0, ALU.mult, ALU.add).then_inc(S("ve_steps"), v.step())
            ve.memset(cfv[:, 12:27, 3], 0.0).then_inc(S("ve_steps"), v.step())
            ve.wait_ge(S("ve_steps"), v.n)
            ve.sem_inc(S("par_done"), 1)
            ve.sem_inc(S("pairs_free"), 1)
            ve.sem_inc(S("pairs_free"), 1)
            ve.wait_ge(S("silu_c"), 1)
            sc2 = sc[:, :].rearrange("p (k s) -> p k s", s=2)
            ve.tensor_copy(sc2[:, :, 1], sgc[:, 0:8]).then_inc(S("ve_steps"), v.step())
            ve.tensor_copy(sc2[:, :, 0], sgc[:, 8:16]).then_inc(S("ve_steps"), v.step())
            ve.wait_ge(S("ve_steps"), v.n)
            ve.sem_inc(S("sc_ready"), 1)

            for i in range(2):
                ve.wait_ge(S("filt_mm"), i + 1)
                if i:
                    ve.wait_ge(S("sin_done"), 1)
                ve.tensor_scalar(pre, bank[6 + i][0:HY_FO, 0:SEG], hyp[0:HY_FO, 2 * i:2 * i + 1],
                                       hyp[0:HY_FO, 2 * i + 1:2 * i + 2], ALU.add, ALU.mult).then_inc(S("ve_steps"), v.step())
                ve.wait_ge(S("ve_steps"), v.n)
                ve.tensor_scalar(turns, pre, 1 / TWO_PI, MAGIC, ALU.mult, ALU.add).then_inc(S("ve_steps"), v.step())
                ve.wait_ge(S("ve_steps"), v.n)
                ve.tensor_scalar(turns, turns, MAGIC, None, ALU.subtract).then_inc(S("ve_steps"), v.step())
                ve.wait_ge(S("ve_steps"), v.n)
                for part in (PI_A, PI_B, PI_C):
                    ve.scalar_tensor_tensor(out=pre, in0=turns, scalar=-part, in1=pre, op0=ALU.mult,
                                                  op1=ALU.add).then_inc(S("ve_steps"), v.step())
                    ve.wait_ge(S("ve_steps"), v.n)
                ve.tensor_scalar(pre, pre, 3.1415925, -3.1415925, ALU.min, ALU.max).then_inc(S("sin_arg"), 1)
            def modulation(g):
                ve.wait_ge(S("ada_turned"), g + 1)
                m = modv[:, 24 * (g % 2):24 * (g % 2) + 24]
                at = PAR[f"ada_b{g // 3}"] + 24 * (g % 3)
                ve.tensor_tensor(m, bank[4][:, 0:48].rearrange("p (b s) -> p b s", s=2),
                                 par[:, at:at + 24].unsqueeze(2).to_broadcast([P, 24, 2]), ALU.add)\
                    .then_inc(S("ve_steps"), v.step())
                ve.wait_ge(S("ve_steps"), v.n)
                ve.tensor_scalar(m[:, 8:16], m[:, 8:16], 1.0, None, ALU.add).then_inc(S("ve_steps"), v.step())
                ve.wait_ge(S("ve_steps"), v.n)
                ve.tensor_scalar(m[:, 16:24], m[:, 16:24], 1.0 if g % 3 == 1 else 0.5, None, ALU.mult)\
                    .then_inc(S("mods"), 1)

            ve.wait_ge(S("ld_const"), 64)
            ve.tensor_copy(masks[:, :], arena[:, 8192:8192 + NMASK * P]).then_inc(S("ve_steps"), v.step())
            ve.wait_ge(S("ve_steps"), v.n)
            modulation(0)
            ve.sem_inc(S("taps_free"), 1)
            for o in range(2):
                ve.wait_ge(S("filt_taps"), o + 1)
                for dr in range(2):
                    for a in range(2):
                        ve.tensor_tensor(taps[:, dr, a], bank[4 + 2 * dr + a], win[:, a], ALU.mult).then_inc(S("ve_steps"), v.step())
                ve.wait_ge(S("ve_steps"), v.n)
                ve.memset(taps[0:1, 1, 0], 0.0).then_inc(S("ve_steps"), v.step())
                ve.tensor_tensor(taps[0:1, 0, 0], taps[0:1, 0, 0], skip_row[:, o], ALU.add).then_inc(S("ve_steps"), v.step())
                ve.wait_ge(S("ve_steps"), v.n)
                ve.tensor_tensor(tap_m, taps[:, 0], taps[:, 1], ALU.subtract).then_inc(S("ve_steps"), v.step())
                ve.wait_ge(S("ve_steps"), v.n)
                ve.tensor_tensor(taps[:, 0], taps[:, 0], taps[:, 1], ALU.add).then_inc(S("taps"), 1)
                ve.wait_ge(S("filt_dft"), o + 1)
                if o == 0:
                    ve.wait_ge(S("kf_done"), 6)
                    ve.sem_inc(S("taps_free"), 1)

            def u_lat(g):
                ve.wait_ge(S("mods"), g + 1)
                for k in range(KT):
                    ve.wait_ge(S("h_ready"), KT * g + k + 1)
                    ve.tensor_scalar(us[:, k, 1], hs[:, k, 1], modv[:, 24 * (g % 2) + 8 + k, 1:2],
                                     modv[:, 24 * (g % 2) + k, 1:2], ALU.mult, ALU.add).then_inc(S("u_lat"), 1)
                T0 = 0 if g < 5 else SEG
                for k in range(KT):
                    ve.wait_ge(S("u_hi"), U_BASE[g] + k + 1)
                    ve.tensor_tensor(ulv[:, k, T0:NT], uv[:, k, T0:NT], uhf[:, k, T0:NT], ALU.subtract)\
                        .then_inc(S("u_lo"), 1)
                ve.tensor_scalar(hs[:, :, 1], hs[:, :, 1], ALPHA, None, ALU.mult).then_inc(S("ve_steps"), v.step())

            def out_lo(g, src, k, TN):
                ve.wait_ge(S("u_hi"), U_BASE[g] + KT + k + 1)
                ve.tensor_tensor(ulv[:, k, 0:TN], src[:, 0:TN], uhf[:, k, 0:TN], ALU.subtract).then_inc(S("u_lo"), 1)

            def ffn_gate(g):
                f = FFN.index(g)
                TN = NT if g < 5 else SEG
                ve.wait_ge(S("u_lo"), U_BASE[g] + KT)
                for t0, t1 in ((0, FA), (FA, FT)):
                    with ve.Fori(0, (t1 - t0) // 2) as c:
                        for jf in range(2):
                            done = FT * f + t0 + jf + 1
                            prod = tmp[:, jf * NT:jf * NT + TN]
                            at = bass.ds(c * (2 * NT) + jf * NT, TN)
                            ve.wait_ge(S("silu"), c * 2 + done)
                            ve.tensor_tensor(prod, bank[2 * jf + 1][:, 0:TN], prod, ALU.mult).then_inc(S("pairs_free"), 1)
                            ve.wait_ge(S("pairs_free"), c * 2 + (done + 2))
                            ve.tensor_copy(hid_hi[:, at], prod).then_inc(S("hid_rounded"), 1)
                            ve.wait_ge(S("hid_rounded"), c * 2 + done)
                            ve.tensor_tensor(hid_lo[:, at], prod, hid_hi[:, at].bitcast(F32), ALU.subtract)\
                                .then_inc(S("hid"), 1)
                    if t0 == 0:
                        ve.wait_ge(S("ve_steps"), v.n)
                        if g < 4:
                            ve.wait_ge(S("scaled_ctx"), g + 1)
                        for k in range(KT):
                            ve.wait_ge(S("y_half"), KT * f + k + 1)
                            for s_ in segments(g):
                                lo = s_ * SEG if g < 4 else 0
                                ins = ve.scalar_tensor_tensor(out=hs[:, k, s_], in0=bank[k][:, lo:lo + SEG],
                                                              scalar=modv[:, 24 * (g % 2) + 16 + k, s_:s_ + 1],
                                                              in1=hs[:, k, s_], op0=ALU.mult, op1=ALU.add)
                            ins.then_inc(S("y_part"), 1)

            def norm(g):
                T0, TN = (0, NT) if g < 4 else (SEG, SEG)
                ve.wait_ge(S("ve_steps"), v.n)
                if g in FFN:
                    ve.wait_ge(S("y_part"), KT * (FFN.index(g) + 1))
                elif g < 4:
                    ve.wait_ge(S("scaled_ctx"), g + 1)
                for k in range(KT):
                    ve.wait_ge(S("y_done"), KT * g + k + 1)
                    for s in segments(g):
                        lo = s * SEG if g < 4 else 0
                        ve.scalar_tensor_tensor(out=hs[:, k, s], in0=bank[k][:, lo:lo + SEG],
                                                scalar=modv[:, 24 * (g % 2) + 16 + k, s:s + 1], in1=hs[:, k, s],
                                                op0=ALU.mult, op1=ALU.add).then_inc(S("resid"), 1)
                ve.wait_ge(S("resid"), resid_base[g + 1])
                ve.wait_ge(S("mean"), g + 1)
                for k in range(KT):
                    ve.tensor_tensor(hv[:, k, T0:NT], hv[:, k, T0:NT], bank[0][:, 0:TN], ALU.subtract)\
                        .then_inc(S("centred"), 1)
                ve.wait_ge(S("centred"), KT * (g + 1))
                ve.wait_ge(S("std"), g + 1)
                ve.reciprocal(rs[:, 0:TN], rs[:, 0:TN]).then_inc(S("ve_steps"), v.step())
                ve.wait_ge(S("ve_steps"), v.n)
                for k in range(KT):
                    ve.tensor_tensor(uv[:, k, T0:NT], hv[:, k, T0:NT], rs[:, 0:TN], ALU.mult)\
                        .then_inc(S("normed"), 1)

            def even_mixer():
                for i in range(ZT):
                    ve.wait_ge(S("z_main"), i + 1)
                    z = bank[i % 8].rearrange("p (s t) -> p s t", s=2)
                    o = bigt[:, i].rearrange("p (s t) -> p s t", s=2)
                    ve.scalar_tensor_tensor(out=o[:, :, 1:SEG], in0=z[:, :, 0:SEG - 1], scalar=cfv[:, i, 0:1],
                                                  in1=o[:, :, 1:SEG], op0=ALU.mult, op1=ALU.add).then_inc(S("ve_steps"), v.step())
                    ve.wait_ge(S("ve_steps"), v.n)
                    ve.scalar_tensor_tensor(out=o[:, :, 0:SEG - 1], in0=z[:, :, 1:SEG], scalar=cfv[:, i, 2:3],
                                            in1=o[:, :, 0:SEG - 1], op0=ALU.mult, op1=ALU.add)\
                        .then_inc(S("z_done"), 1)
                for o in range(2):
                    for s in range(2):
                        ve.wait_ge(S("hy_f"), 2 * o + s + 1)
                        if o == 0 and s == 0:
                            ve.wait_ge(S("vtok"), 8)
                        else:
                            ve.wait_ge(S("hy_mul"), 2 * o + s)
                        for i in range(2):
                            re, im = bank[4 * s + i], bank[4 * s + 2 + i]
                            kre, kim, kre2 = kf[:, o, i], kf[:, o, 2 + i], kf[:, o, 4 if i == 0 else i]
                            ve.tensor_tensor(ft[0], re, kre, ALU.mult).then_inc(S("ve_steps"), v.step())
                            ve.tensor_tensor(ft[1], im, kim, ALU.mult).then_inc(S("ve_steps"), v.step())
                            ve.wait_ge(S("ve_steps"), v.n)
                            ve.tensor_tensor(yf[:, s, i], ft[0], ft[1], ALU.subtract).then_inc(S("ve_steps"), v.step())
                            ve.wait_ge(S("ve_steps"), v.n)
                            ve.tensor_tensor(ft[0], re, kim, ALU.mult).then_inc(S("ve_steps"), v.step())
                            ve.tensor_tensor(ft[1], im, kre2, ALU.mult).then_inc(S("ve_steps"), v.step())
                            ve.wait_ge(S("ve_steps"), v.n)
                            ins = ve.tensor_tensor(yf[:, s, 2 + i], ft[0], ft[1], ALU.add)
                            if i == 0:
                                ins.then_inc(S("ve_steps"), v.step())
                                ve.wait_ge(S("ve_steps"), v.n)
                        ins.then_inc(S("hy_mul"), 1)
                    for s in range(2):
                        ve.wait_ge(S("hy_i"), 2 * o + s + 1)
                        for a in range(2):
                            if o == 0:
                                ve.tensor_tensor(vtok[:, 2 * s + a], bank[4 * s + a], x1tok[:, 2 * s + a], ALU.mult)\
                                    .then_inc(S("hy_y1"), 1)
                            else:
                                ve.tensor_tensor(yhy[:, 2 * a:2 * a + 2, s * SEG:(s + 1) * SEG],
                                                 bank[4 * s + a].rearrange("p (c t) -> p c t", c=2),
                                                 bigt[:, 8 + 2 * a:10 + 2 * a, s * SEG:(s + 1) * SEG], ALU.mult)\
                                    .then_inc(S("hy_done"), 1)
                tile_of = lambda ap, c: ap[:, c * NT:(c + 1) * NT]
                ve.wait_ge(S("hy_done"), 4)
                for c in range(CT):
                    ve.tensor_scalar(tile_of(kk, c), tile_of(zk, c), col("k_k", c), None, ALU.mult).then_inc(S("ve_steps"), v.step())
                ve.wait_ge(S("ve_steps"), v.n)
                ve.sem_inc(S("kk_raw"), 1)
                for d in range(2):
                    for c in range(CT):
                        ve.wait_ge(S("lora_out"), CT * d + c + 1)
                        for n in range(4):
                            at = slice(c * NT + n * P, c * NT + (n + 1) * P)
                            ve.tensor_tensor_scan(sgw[d][:, at], ones[:, :], sgw[d][:, at], 0.0, ALU.mult, ALU.add)\
                                .then_inc(S("ve_steps"), v.step())
                ve.wait_ge(S("ve_steps"), v.n)
                for d in range(2):
                    ve.tensor_scalar(half[:, d], sgw[d].rearrange("p (c n t) -> p c n t", c=CT, n=4)[:, :, :, P - 1],
                                     0.5, None, ALU.mult).then_inc(S("ve_steps"), v.step())
                ve.wait_ge(S("ve_steps"), v.n)
                for d in range(2):
                    chunks = sgw[d].rearrange("p (g t) -> p g t", t=P)
                    hb = small[:, 64 + 16 * d:80 + 16 * d].unsqueeze(2).to_broadcast([P, 16, P])
                    ve.tensor_tensor(chunks, chunks, hb, ALU.subtract).then_inc(S("ve_steps"), v.step())
                ve.wait_ge(S("ve_steps"), v.n)
                ve.sem_inc(S("sums"), 1)
                ve.tensor_scalar(small[:, 20:24], par[:, PAR["k_a"]:PAR["k_a"] + 4], -1.0, 1.0, ALU.mult, ALU.add)\
                    .then_inc(S("ve_steps"), v.step())
                ve.wait_ge(S("ve_steps"), v.n)
                ve.tensor_scalar(small[:, 24:28], small[:, 20:24], 2.0, None, ALU.mult).then_inc(S("bonus_coef"), 1)
                ve.wait_ge(S("lora_out"), 16)
                for d in range(2):
                    for c in range(CT):
                        dst = tile_of(kd[0] if d == 0 else kd1_factor, c)
                        ve.tensor_scalar(dst, tile_of(aa[d], c), col("k_a", c), small[:, 20 + c:21 + c],
                                         ALU.mult, ALU.add).then_inc(S("ve_steps"), v.step())
                ve.wait_ge(S("ve_steps"), v.n)
                ve.tensor_tensor(kd[0], kd[0], zk, ALU.mult).then_inc(S("ve_steps"), v.step())
                ve.wait_ge(S("ve_steps"), v.n)
                ve.wait_ge(S("bonus_k"), 1)
                ve.tensor_tensor(zk, zk, kd1_factor, ALU.mult).then_inc(S("ve_steps"), v.step())
                ve.wait_ge(S("kk_norm"), 4)
                ve.tensor_scalar(prep2, prep2, 1e-12, None, ALU.max).then_inc(S("ve_steps"), v.step())
                ve.wait_ge(S("ve_steps"), v.n)
                ve.reciprocal(prep2, prep2).then_inc(S("ve_steps"), v.step())
                ve.wait_ge(S("ve_steps"), v.n)
                ve.tensor_tensor(kk, kk, prep2, ALU.mult).then_inc(S("ve_steps"), v.step())
                ve.wait_ge(S("ve_steps"), v.n)
                ve.tensor_tensor(aa[0], aa[0], kk, ALU.mult).then_inc(S("ve_steps"), v.step())
                ve.tensor_tensor(aa[1], aa[1], kk, ALU.mult).then_inc(S("ve_steps"), v.step())
                ve.wait_ge(S("v_turned"), 4)
                for c in range(CT):
                    ve.wait_ge(S("bonus_sum"), c + 1)
                    ve.tensor_tensor(tile_of(zv, c), bank[c], tile_of(zv, c), ALU.mult).then_inc(S("ve_steps"), v.step())
                ve.memset(arena[:, 42496:43008], 0.0).then_inc(S("ve_steps"), v.step())
                ve.wait_ge(S("ve_steps"), v.n)
                ve.sem_inc(S("prepared"), 1)
                chunk = lambda ap, ch: three(ap)[:, :, ch * P:(ch + 1) * P]

                def slots_of(j, d):
                    ch = chunk_of(d, j)
                    ve.wait_ge(S("exped"), 2 * j + d + 1)
                    recv, read, key = decays[d]
                    for e in range(2):
                        hp = slice(64 * e, 64 * e + 64)
                        ve.scalar_tensor_tensor(out=ar[hp, d, :, e, 0], in0=chunk(kk, ch)[hp], scalar=-1.0,
                                                in1=recv[hp], op0=ALU.mult, op1=ALU.mult)\
                            .then_inc(S("ve_steps"), v.step())
                    ve.tensor_tensor(bk[:, d, :, 1], chunk(kd[d], ch), key, ALU.mult).then_inc(S("ve_steps"), v.step())
                    ve.tensor_tensor(bk[:, d, :, 0], chunk(aa[d], ch), key, ALU.mult).then_inc(S("ve_steps"), v.step())
                    ve.wait_ge(S("ve_steps"), v.n)
                    ve.sem_inc(S("slots"), 1)

                def scale_state(j, d):
                    ed = edec[:, d, :, chunk_of(d, j)].unsqueeze(2).to_broadcast([P, CT, 64])
                    ve.tensor_tensor(state[:, d], state[:, d], ed, ALU.mult).then_inc(S("state_in"), 1)

                ve.wait_ge(S("edec"), 1)
                for d in range(2):
                    slots_of(0, d)
                    scale_state(0, d)
                ve.wait_ge(S("zeroed"), 1)
                for j in range(4):
                    for hf in range(2):
                        gi = 2 * j + hf
                        for d in range(2):
                            mk = maskv[:, M_STRICT + 2 * d:M_STRICT + 2 * d + 2].rearrange("p m t -> p (m t)")\
                                .unsqueeze(1).to_broadcast([P, 2, 2 * P])
                            for cc in range(2):
                                for q in range(2):
                                    ve.wait_ge(S("n_mm"), 8 * gi + 4 * d + 2 * cc + q + 1)
                                    ve.copy_predicated(nm[:, d, 2 * cc:2 * cc + 2, 2 * q:2 * q + 2]
                                                       .rearrange("p h a t -> p h (a t)"), mk,
                                                       bank[n_bank(d, cc, q)].rearrange("p (b t) -> p b t", b=2))\
                                        .then_inc(S("n_done"), 1)
                        for lv in range(LEVELS):
                            m = 1 << lv
                            for d in range(2):
                                um, tm = (M_UP, M_LO) if d == 0 else (M_LO, M_UP)
                                mask = lambda k, which: blocks(maskv[:, k + lv], m, which).unsqueeze(1)\
                                    .to_broadcast([P, 4, 64 // m, m])
                                wide = lambda ap: ap[:, 0:2 * P].rearrange("p (h g m) -> p h g m", h=4, m=m)
                                if lv == 0:
                                    ve.wait_ge(S("z_mm"), 2 * LEVELS * gi + d + 1)
                                    ve.wait_ge(S("tu_reset"), 2 * gi + d + 1)
                                    if d == 0:
                                        ve.wait_ge(S("n_done"), 8 * (gi + 1))
                                    tsrc = wide(bank[d])
                                    usrc = blocks(nm[:, d, :, 0], m, 1 - d)
                                else:
                                    ve.wait_ge(S("d_mm"), 2 * (gi * (LEVELS - 1) + lv - 1) + d + 1)
                                    tsrc = wide(bank[2 + d])
                                    usrc = wide(bank[4 + d])
                                if lv < LEVELS - 1:
                                    ve.copy_predicated(blocks(tu[:, d, 0], m, d), mask(tm, d), tsrc)\
                                        .then_inc(S("tu"), 1)
                                    ve.copy_predicated(blocks(tu[:, d, 1], m, 1 - d), mask(um, 1 - d), usrc)\
                                        .then_inc(S("tu"), 1)
                                else:
                                    ve.copy_predicated(blocks(tu[:, d, 1], m, 1 - d), mask(um, 1 - d), usrc)\
                                        .then_inc(S("tu"), 2)
                        if hf == 0:
                            ve.wait_ge(S("state_in"), 2 * (j + 1))
                        for d in range(2):
                            ve.wait_ge(S("sa_mm"), 2 * gi + d + 1)
                            ve.tensor_copy(xs[:, d, 1].rearrange("p h v -> p (h v)"), bank[4 + d][:, 0:256])\
                                .then_inc(S("sa"), 1)
                        ve.wait_ge(S("os_mm"), 2 * gi + 2)
                        for d in range(2):
                            st = state[:, d, 2 * hf:2 * hf + 2]
                            ve.tensor_tensor(st, st, bank[d][:, 0:128].rearrange("p (c v) -> p c v", c=2), ALU.add)\
                                .then_inc(S("ve_steps"), v.step())
                        ve.wait_ge(S("ve_steps"), v.n)
                        for d in range(2):
                            st = state[:, d, 2 * hf:2 * hf + 2]
                            ed = edec[:, d, 2 * hf:2 * hf + 2, chunk_of(d, j)].unsqueeze(2).to_broadcast([P, 2, 64])
                            ve.tensor_tensor(st, st, ed, ALU.mult).then_inc(S("state_new"), 1)
                        if hf and j < 3:
                            slots_of(j + 1, 0)
                        for d in range(2):
                            ch = chunk_of(d, j)
                            for q in range(2):
                                lo = 64 * q
                                dst = three(oacc)[lo:lo + 64, 2 * hf:2 * hf + 2, ch * P:(ch + 1) * P]
                                src = bank[6 + q][lo:lo + 64, 2 * d * P:2 * (d + 1) * P]\
                                    .rearrange("p (c t) -> p c t", c=2)
                                if j % 2 == 0:
                                    ve.tensor_copy(dst, src).then_inc(S("o_add"), 1)
                                else:
                                    ve.tensor_tensor(dst, dst, src, ALU.add).then_inc(S("o_add"), 1)
                        if hf and j < 3:
                            slots_of(j + 1, 1)
                            ve.wait_ge(S("state_new"), 4 * (j + 1))
                            for d in range(2):
                                scale_state(j + 1, d)
                ve.wait_ge(S("o_add"), 32)
                for c in range(CT):
                    ve.wait_ge(S("gn_mean"), c + 1)
                    o = tile_of(oacc, c)
                    ve.scalar_tensor_tensor(out=o, in0=bank[c], scalar=-1 / 64.0, in1=o, op0=ALU.mult, op1=ALU.add)\
                        .then_inc(S("gn_centred"), 1)
                for k in range(CT):
                    out_lo(1, yhy[:, k], k, NT)
                ve.wait_ge(S("gn_centred"), 4)
                for c in range(CT):
                    o = tile_of(oacc, c)
                    ve.wait_ge(S("gn_rstd"), c + 1)
                    ve.scalar_tensor_tensor(out=o, in0=o, scalar=col("gn_g", c), in1=tile_of(gn_rstd, c),
                                            op0=ALU.mult, op1=ALU.mult).then_inc(S("ve_steps"), v.step())
                    ve.wait_ge(S("ve_steps"), v.n)
                    ve.scalar_tensor_tensor(out=o, in0=o, scalar=col("gn_b", c), in1=tile_of(zv, c),
                                            op0=ALU.add, op1=ALU.add).then_inc(S("ve_steps"), v.step())
                    ve.wait_ge(S("ve_steps"), v.n)
                    ve.tensor_tensor(o, o, tile_of(gate, c), ALU.mult).then_inc(S("mixed"), 1)
                ve.wait_ge(S("mixed"), CT)
                for k in range(CT, KT):
                    out_lo(1, three(oacc)[:, k - CT], k, NT)

            def odd_mixer():
                ve.wait_ge(S("z1_done"), len(OD_TILES))
                for q in range(8):
                    ve.wait_ge(S("lg_abs"), q + 1)
                    ve.tensor_scalar(gg[:, q // 4, q % 4], bank[q], col("gla_b", q), 0.0, ALU.add, ALU.min).then_inc(S("ve_steps"), v.step())
                ve.wait_ge(S("ve_steps"), v.n)
                ve.wait_ge(S("lg_ln"), 1)
                ggf = arena[:, 8192:12288]
                ve.tensor_tensor(ggf, ggf, arena[:, 16384:20480], ALU.subtract).then_inc(S("ve_steps"), v.step())
                ve.wait_ge(S("ve_steps"), v.n)
                ve.wait_ge(S("ld_gla"), 48)
                for q in range(8):
                    ve.tensor_tensor_scan(gcs[:, q // 4, q % 4], greset, gg[:, q // 4, q % 4], 0.0, ALU.mult,
                                                ALU.add).then_inc(S("ve_steps"), v.step())
                ve.wait_ge(S("ve_steps"), v.n)
                tot = gcs[:, 0, :, SEG - 1].unsqueeze(2).to_broadcast([P, 4, SEG])
                ve.tensor_tensor(kout[:, 0], tot, gcs[:, 0, :, 0:SEG], ALU.subtract).then_inc(S("ve_steps"), v.step())
                ve.tensor_tensor(kout[:, 1], gcs[:, 1, :, 0:SEG], gg[:, 1, :, 0:SEG], ALU.subtract).then_inc(S("ve_steps"), v.step())
                ve.wait_ge(S("ve_steps"), v.n)
                ve.sem_inc(S("ctx_arg"), 1)
                for d in range(2):
                    ve.tensor_scalar(ghalf[:, d], gcs[:, d, :, SEG + 63:NT:64], 0.5, None, ALU.mult).then_inc(S("ve_steps"), v.step())
                ve.wait_ge(S("ve_steps"), v.n)
                for c in range(4):
                    hb = lambda d: ghalf[:, d, c].unsqueeze(2).to_broadcast([P, 4, 64])
                    cv = lambda ap: ap.rearrange("p (n t) -> p n t", n=4)
                    ve.tensor_tensor(cv(sq2[:, c]), cv(gcs[:, 0, c, SEG:NT]), hb(0), ALU.subtract).then_inc(S("ve_steps"), v.step())
                    ve.tensor_tensor(sq2[:, 4 + c], gcs[:, 1, c, SEG:NT], gg[:, 1, c, SEG:NT], ALU.subtract).then_inc(S("ve_steps"), v.step())
                    ve.wait_ge(S("ve_steps"), v.n)
                    ve.tensor_tensor(cv(sq2[:, 4 + c]), cv(sq2[:, 4 + c]), hb(1), ALU.subtract).then_inc(S("ve_steps"), v.step())
                ve.wait_ge(S("ve_steps"), v.n)
                ve.wait_ge(S("ctx_exp"), 1)
                ve.sem_inc(S("lat_arg"), 1)
                for d in range(2):
                    ve.tensor_tensor(kout[:, d], kout[:, d], gk[:, :, 0:SEG], ALU.mult).then_inc(S("ve_steps"), v.step())
                ve.wait_ge(S("ve_steps"), v.n)
                ve.sem_inc(S("kout"), 1)
                ve.wait_ge(S("lat_exp"), 1)
                for d in range(2):
                    ve.scalar_tensor_tensor(out=qh[:, d], in0=gq, scalar=HK ** -0.5, in1=qh[:, d],
                                                  op0=ALU.mult, op1=ALU.mult).then_inc(S("ve_steps"), v.step())
                    ve.tensor_tensor(kh[:, d], gk[:, :, SEG:NT], kh[:, d], ALU.mult).then_inc(S("ve_steps"), v.step())
                ve.wait_ge(S("ve_steps"), v.n)
                ve.sem_inc(S("lat_in"), 1)
                ve.wait_ge(S("pm_zero"), 1)
                for n in range(3):
                    for d in range(2):
                        ve.tensor_tensor(gpair[:, d, :, n], gexp[:, d, :, XCHUNK(d, n)], gexp[:, d, :, XCHUNK(d, n + 1)],
                                         ALU.mult).then_inc(S("ve_steps"), v.step())
                ve.wait_ge(S("ve_steps"), v.n)
                eb = lambda d, n: gexp[:, d, :, XCHUNK(d, n)].unsqueeze(2).to_broadcast([P, 4, HV])
                ve.wait_ge(S("gs_mm"), 1)
                for d in range(2):
                    ins = ve.tensor_tensor(gst[:, d, 0], psum[:, 2 * d:2 * d + 2, :].rearrange("p b (c v) -> p (b c) v", c=2),
                                           eb(d, 0), ALU.mult)
                    if d == 0:
                        ins.then_inc(S("ve_steps"), v.step())
                ins.then_inc(S("gst"), 1)
                for d in range(2):
                    for b in range(2):
                        ve.wait_ge(S("sc_mm"), 2 * d + b + 1)
                        ve.copy_predicated(pm[:, d, b], maskv[:, M_GLA + d].unsqueeze(1).to_broadcast([P, 4, P]),
                                           bank[4 + 2 * d + b].rearrange("p (c t) -> p c t", c=4))\
                            .then_inc(S("pm"), 1)
                ve.wait_ge(S("pm"), 4)
                ve.tensor_tensor(pm[:, 0], pm[:, 0], pm[:, 1], ALU.add).then_inc(S("pm"), 1)
                for n in range(3):
                    ve.wait_ge(S("gs_mm"), n + 2)
                    ve.wait_ge(S("gst"), n + 1)
                    b0 = 4 * ((n + 1) % 2)
                    for d in range(2):
                        nxt = gst[:, d, n + 1]
                        ve.tensor_tensor(nxt, psum[:, b0 + 2 * d:b0 + 2 * d + 2, :]
                                               .rearrange("p b (c v) -> p (b c) v", c=2), gst[:, d, n], ALU.add).then_inc(S("ve_steps"), v.step())
                        ve.wait_ge(S("ve_steps"), v.n)
                        ins = ve.tensor_tensor(nxt, nxt, gpair[:, d, :, n].unsqueeze(2).to_broadcast([P, 4, HV]),
                                               ALU.mult)
                        if d == 0:
                            ins.then_inc(S("ve_steps"), v.step())
                    ve.wait_ge(S("ve_steps"), v.n)
                    ins.then_inc(S("gst"), 1)
                for b in range(4):
                    ve.wait_ge(S("go_mm"), b + 1)
                    ve.tensor_copy(go[:, 2 * b:2 * b + 2].rearrange("p c t -> p (c t)"), bank[b])\
                        .then_inc(S("go_done"), 1)
                ve.wait_ge(S("go_done"), 4)
                g2 = go.rearrange("p (c a) t -> p c a t", a=2)
                for i in range(2):
                    ve.wait_ge(S("go_rstd"), i + 1)
                    for a in range(2):
                        o = g2[:, 2 * i:2 * i + 2, a]
                        ve.scalar_tensor_tensor(out=o, in0=o, scalar=col("norm_g", a), in1=grs[:, 2 * i:2 * i + 2],
                                                op0=ALU.mult, op1=ALU.mult).then_inc(S("ve_steps"), v.step())
                    ve.wait_ge(S("ve_steps"), v.n)
                    o = go[:, 4 * i:4 * i + 4]
                    ve.tensor_tensor(o, o, gog[:, 4 * i:4 * i + 4], ALU.mult).then_inc(S("mixed"), 1)
                ve.wait_ge(S("mixed"), CT + 2)
                for k in range(KT):
                    out_lo(4, go[:, k], k, SEG)

            for g in range(SUBS):
                u_lat(g)
                if g + 1 < SUBS:
                    modulation(g + 1)
                if g == 1:
                    even_mixer()
                elif g == 4:
                    odd_mixer()
                else:
                    ffn_gate(g)
                norm(g)

        @block.gpsimd
        def _(pool):
            def remainders(phase, g, sizes, tiles=0, q=0):
                for halves in sizes:
                    for _ in range(halves):
                        hq = half0[phase, g] + q
                        src = half_src(phase, g, q, tiles)
                        pool.wait_ge(S("hi_done"), hq + 1)
                        pool.tensor_tensor(half_shape(split_lo(hq), src), src,
                                           half_shape(split_hi(hq).bitcast(F32), src), ALU.subtract)\
                            .then_inc(S("lo_done"), 1)
                        q += 1
                    pool.wait_ge(S("lo_done"), hq + 1)
                    pool.sem_inc(S("chunk_split"), 1)

            def u_ctx(g):
                pool.wait_ge(S("mods"), g + 1)
                for k in range(KT):
                    pool.wait_ge(S("h_ready"), KT * g + k + 1)
                    pool.tensor_scalar(us[:, k, 0], hs[:, k, 0], modv[:, 24 * (g % 2) + 8 + k, 0:1],
                                       modv[:, 24 * (g % 2) + k, 0:1], ALU.mult, ALU.add).then_inc(S("u_ctx"), 1)
                if g < 4:
                    pool.wait_ge(S("u_ctx"), KT * (g + 1))
                    pool.tensor_scalar(hs[:, :, 0], hs[:, :, 0], ALPHA, None, ALU.mult).then_inc(S("scaled_ctx"), 1)

            def recurrence_resets():
                pool.wait_ge(S("hy_done"), 4)
                pool.wait_ge(S("lora_psum"), 20)
                p = Count()
                pool.wait_ge(S("bonus_coef"), 1)
                pool.wait_ge(S("lora_out"), 16)
                pool.tensor_tensor(bonus, aa[0], aa[1], ALU.add).then_inc(S("pool_steps"), p.step())
                pool.wait_ge(S("pool_steps"), p.n)
                tile_of = lambda ap, c: ap[:, c * NT:(c + 1) * NT]
                for c in range(CT):
                    pool.tensor_scalar(tile_of(bonus, c), tile_of(bonus, c), col("k_a", c), small[:, 24 + c:25 + c],
                                       ALU.mult, ALU.add).then_inc(S("pool_steps"), p.step())
                pool.wait_ge(S("pool_steps"), p.n)
                pool.tensor_tensor(bonus, bonus, zk, ALU.mult).then_inc(S("bonus_k"), 1)
                pool.wait_ge(S("bonus_k"), 1)
                pool.tensor_tensor(bonus, bonus, zr, ALU.mult).then_inc(S("pool_steps"), p.step())
                pool.wait_ge(S("pool_steps"), p.n)
                for c in range(CT):
                    ins = pool.tensor_scalar(tile_of(bonus, c), tile_of(bonus, c), col("r_k", c), None, ALU.mult)
                ins.then_inc(S("bonus_in"), 1)
                pool.memset(arena[:, 6144:10240], 0.0).then_inc(S("nm_zero"), 1)
                pool.memset(arena[:, 12288:13312], 0.0).then_inc(S("nm_zero"), 1)
                pool.wait_ge(S("prepared"), 1)
                for e in range(2):
                    pool.wait_ge(S("nm_zero"), 2 + e)
                    zero = ar[64 - 64 * e:128 - 64 * e, :, :, e].rearrange("p d c a t -> p (d c) (a t)")
                    pool.memset(zero, 0.0).then_inc(S("nm_zero"), 1)
                pool.wait_ge(S("nm_zero"), 4)
                pool.sem_inc(S("zeroed"), 1)
                for gi in range(8):
                    j = gi // 2
                    if gi % 2 == 0:
                        for d in range(2):
                            pool.wait_ge(S("exped"), 2 * j + d + 1)
                            if j:
                                pool.wait_ge(S("os_mm"), 4 * j)
                            ch = chunk_of(d, j)
                            for e in range(2):
                                hp = slice(64 * e, 64 * e + 64)
                                if j:
                                    pool.wait_ge(S("tu_reset"), 4 * j)
                                if j or d or e:
                                    pool.wait_ge(S("readers"), 4 * j + 2 * d + e)
                                pool.tensor_tensor(ar[hp, d, :, e, 1], three(zr)[hp, :, ch * P:(ch + 1) * P],
                                                   decays[d][1][hp], ALU.mult).then_inc(S("readers"), 1)
                            pool.wait_ge(S("readers"), 4 * j + 2 * d + 2)
                            pool.sem_inc(S("slots_r"), 1)
                    if gi:
                        pool.wait_ge(S("sa_mm"), 2 * gi)
                    for d in range(2):
                        pool.tensor_copy(tu[:, d].rearrange("p a h t -> p (a h) t"),
                                         ident[:, :].unsqueeze(1).to_broadcast([P, 8, P])).then_inc(S("tu_reset"), 1)

            pool.wait_ge(S("ld_ident"), 16)
            for g in range(SUBS):
                first_ = "even_in" if g == 1 else "odd_in" if g == 4 else "up_a"
                remainders(first_, g, [2], FA)
                if g < 5:
                    u_ctx(g)
                if g == 1:
                    remainders("even_in", g, [2] * 6, 0, 2)
                    recurrence_resets()
                    remainders("even_out", g, [2, 2])
                elif g == 4:
                    pool.memset(arena[0:32, 40448:41472], 0.0).then_inc(S("gup_zero"), 1)
                    remainders("odd_in", g, [1, 2, 2, 2, 2, 2], 0, 2)
                    pool.wait_ge(S("z1_done"), len(OD_TILES))
                    pool.memset(big[:, 11776:13824], 0.0).then_inc(S("pm_zero"), 1)
                    remainders("odd_out", g, [2, 2])
                else:
                    remainders("up_a", g, [2] * (FA // 2 - 1), FA, 2)
                    remainders("down_a", g, [2] * (FA // 4), FA)
                    remainders("up_b", g, [2] * ((FT - FA) // 2))
                    remainders("down_b", g, [2, 2, 2], FT - FA)


OD_TILES = ([(j // 2, "k", j) for j in range(4)] + [(2, "gd", 0)] + [(3 + j // 2, "q", j) for j in range(4)]
            + [(5 + j // 4, "v", j) for j in range(16)] + [(9 + j // 2, "og", j) for j in range(8)])
OD_HALVES = 13


def kernel(**inputs):
    import concourse.bacc as bacc
    from concourse.bass_utils import run_bass_kernel_spmd as run

    nc = bacc.Bacc("TRN2", target_bir_lowering=False, num_devices=1)
    arrays, A, K = {}, {}, {}
    for name, value in inputs.items():
        arr = np.ascontiguousarray(value)
        arrays["in_" + name] = arr
        A[name] = nc.dram_tensor("in_" + name, arr.shape, mybir.dt.from_np(arr.dtype), kind="ExternalInput").ap()
    for name, arr in constants().items():
        arrays[name] = arr
        K[name] = nc.dram_tensor(name, arr.shape, mybir.dt.from_np(arr.dtype), kind="ExternalInput").ap()
    out = nc.dram_tensor("out", (1, SEG, D), F32, kind="ExternalOutput").ap()
    program(nc, A, K, out)
    r = run(nc, [arrays], core_ids=[0])
    return r.results[0]["out"]
```
